# Optimizing a Trainium2 kernel written in Bass

```python
import jax, jax.numpy as jnp
from jax import lax
import numpy as np

D_MODEL = 2048
BATCH = 1
SEQ = 512
DEPTH = 1
DEC_BATCH = 8
DEC_SEQ = 4
PAST_LEN = 1024
PAGE_SIZE = 128

N_HEADS = 8
HEAD_DIM = 128
ATTN_WIDTH = N_HEADS * HEAD_DIM
ROT_DIM = HEAD_DIM // 4
ROPE_THETA = 500000.0
IDX_HEADS = 16
IDX_DIM = 64
IDX_ROT_DIM = IDX_DIM // 4
TOPK_MAX = 256
Q_BLOCK = 128
POOL_WINDOWS = (2, 4, 8, 16)
N_POOL_GROUPS = len(POOL_WINDOWS)
POOL_WIDTH = D_MODEL - ATTN_WIDTH
POOL_GROUP_DIM = POOL_WIDTH // N_POOL_GROUPS
POOL_STATE = max(POOL_WINDOWS) - 1
MIX_WIDTH = ATTN_WIDTH + POOL_WIDTH
IN_SPLITS = (ATTN_WIDTH, ATTN_WIDTH, ATTN_WIDTH, ATTN_WIDTH,
             IDX_HEADS * IDX_DIM, IDX_DIM, IDX_HEADS, POOL_WIDTH, POOL_WIDTH)
IN_COLS = sum(IN_SPLITS)
DEEPNORM_ALPHA = (2 * DEPTH) ** 0.25
DEEPNORM_BETA = (8 * DEPTH) ** -0.25
LN_EPS = 1e-5

kernel_name = 'hybrid_dsa_pool_decode_step'

def _rope(x, pos, rot):
    half = rot // 2
    freqs = ROPE_THETA ** (-jnp.arange(half, dtype=jnp.float32) * (2.0 / rot))
    ang = pos.astype(jnp.float32)[:, None] * freqs[None, :]
    shape = (1, pos.shape[0]) + (1,) * (x.ndim - 3) + (half,)
    cos = jnp.cos(ang).reshape(shape)
    sin = jnp.sin(ang).reshape(shape)
    xr = x[..., :rot].astype(jnp.float32)
    x1, x2 = xr[..., :half], xr[..., half:]
    rotated = jnp.concatenate([x1 * cos - x2 * sin, x1 * sin + x2 * cos], axis=-1).astype(x.dtype)
    return jnp.concatenate([rotated, x[..., rot:]], axis=-1)

def _project(x, pos, w_in):
    B, T, _ = x.shape
    h = jnp.einsum('btd,dc->btc', x, w_in)
    pts = np.cumsum(IN_SPLITS)[:-1].tolist()
    q, k, v, ga, qi, ki, wi, u, gb = jnp.split(h, pts, axis=-1)
    q = _rope(q.reshape(B, T, N_HEADS, HEAD_DIM), pos, ROT_DIM)
    k = _rope(k.reshape(B, T, N_HEADS, HEAD_DIM), pos, ROT_DIM)
    v = v.reshape(B, T, N_HEADS, HEAD_DIM)
    qi = _rope(qi.reshape(B, T, IDX_HEADS, IDX_DIM), pos, IDX_ROT_DIM)
    ki = _rope(ki, pos, IDX_ROT_DIM)
    return q, k, v, ga, qi, ki, wi, u, gb

def _index_scores(qi, wi, ki):
    s = jnp.einsum('bthd,bsd->bths', qi.astype(jnp.float32), ki.astype(jnp.float32))
    scale = (IDX_DIM ** -0.5) * (IDX_HEADS ** -0.5)
    return jnp.einsum('bths,bth->bts', jax.nn.relu(s), wi.astype(jnp.float32)) * scale

def _sparse_attend(q, k_sel, v_sel, valid):
    s = jnp.einsum('bthd,btkhd->bthk', q.astype(jnp.float32), k_sel.astype(jnp.float32)) * (HEAD_DIM ** -0.5)
    s = jnp.where(valid[:, :, None, :], s, -jnp.inf)
    p = jax.nn.softmax(s, axis=-1)
    o = jnp.einsum('bthk,btkhd->bthd', p, v_sel.astype(jnp.float32))
    return o.astype(q.dtype)

def _prompt_attention(q, k, v, qi, ki, wi):
    B, S = q.shape[0], q.shape[1]
    topk = min(TOPK_MAX, S // 4)
    n_blocks = S // Q_BLOCK
    key_pos = jnp.arange(S)
    bidx = jnp.arange(B)[:, None, None]

    def block(i):
        start = i * Q_BLOCK
        qb = lax.dynamic_slice_in_dim(q, start, Q_BLOCK, axis=1)
        qib = lax.dynamic_slice_in_dim(qi, start, Q_BLOCK, axis=1)
        wib = lax.dynamic_slice_in_dim(wi, start, Q_BLOCK, axis=1)
        qpos = start + jnp.arange(Q_BLOCK)
        scores = _index_scores(qib, wib, ki)
        causal = key_pos[None, :] <= qpos[:, None]
        scores = jnp.where(causal[None], scores, -jnp.inf)
        _, idx = lax.top_k(scores, topk)
        valid = idx <= qpos[None, :, None]
        return _sparse_attend(qb, k[bidx, idx], v[bidx, idx], valid)

    out = lax.map(block, jnp.arange(n_blocks))
    return out.transpose(1, 0, 2, 3, 4).reshape(B, S, N_HEADS, HEAD_DIM)

def _sample_attention(l, q, k_new, v_new, qi, ki_new, wi, cache_k, cache_v, cache_kidx, page_table):
    Bd, T = q.shape[0], q.shape[1]
    past = page_table.shape[1] * PAGE_SIZE
    L = past + T
    topk = min(TOPK_MAX, L // 4)
    ki_past = cache_kidx[l, page_table].reshape(Bd, past, IDX_DIM).astype(ki_new.dtype)
    ki_all = jnp.concatenate([ki_past, ki_new], axis=1)
    scores = _index_scores(qi, wi, ki_all)
    qpos = past + jnp.arange(T)
    causal = jnp.arange(L)[None, :] <= qpos[:, None]
    scores = jnp.where(causal[None], scores, -jnp.inf)
    _, idx = lax.top_k(scores, topk)
    valid = idx <= qpos[None, :, None]
    is_past = (idx < past)[..., None, None]
    bidx = jnp.arange(Bd)[:, None, None]
    pidx = jnp.minimum(idx, past - 1)
    phys_page = page_table[bidx, pidx // PAGE_SIZE]
    offset = pidx % PAGE_SIZE
    nidx = jnp.clip(idx - past, 0, T - 1)
    k_sel = jnp.where(is_past, cache_k[l, phys_page, offset].astype(k_new.dtype), k_new[bidx, nidx])
    v_sel = jnp.where(is_past, cache_v[l, phys_page, offset].astype(v_new.dtype), v_new[bidx, nidx])
    return _sparse_attend(q, k_sel, v_sel, valid)

def _pool_mix(u_ext, n_hist, w_pool, pool_scale):
    B, R, _ = u_ext.shape
    ug = u_ext.astype(jnp.float32).reshape(B, R, N_POOL_GROUPS, POOL_GROUP_DIM)
    cs = jnp.concatenate([jnp.zeros((B, 1, N_POOL_GROUPS, POOL_GROUP_DIM), jnp.float32),
                          jnp.cumsum(ug, axis=1)], axis=1)
    rows = np.arange(n_hist, R)
    outs = []
    for g, w in enumerate(POOL_WINDOWS):
        starts = np.maximum(rows + 1 - w, 0)
        count = jnp.asarray((rows + 1 - starts).astype(np.float32))
        cs_g = cs[:, :, g]
        mean = (cs_g[:, rows + 1] - cs_g[:, starts]) / count[None, :, None]
        outs.append(mean - ug[:, n_hist:, g])
    pooled = jnp.stack(outs, axis=2)
    mixed = jnp.einsum('btgc,gcd->btgd', pooled, w_pool.astype(jnp.float32))
    T = R - n_hist
    return (mixed.reshape(B, T, POOL_WIDTH) * pool_scale.astype(jnp.float32)).astype(u_ext.dtype)

def _combine(x, a, p, ga, gb, w_out, ln_g, ln_b):
    B, T, _ = x.shape
    mixed = jnp.concatenate([a.reshape(B, T, ATTN_WIDTH) * jax.nn.silu(ga),
                             p * jax.nn.silu(gb)], axis=-1)
    h = (DEEPNORM_ALPHA * x + jnp.einsum('btc,cd->btd', mixed, w_out)).astype(jnp.float32)
    mu = jnp.mean(h, axis=-1, keepdims=True)
    var = jnp.mean(jnp.square(h - mu), axis=-1, keepdims=True)
    y = (h - mu) * lax.rsqrt(var + LN_EPS) * ln_g.astype(jnp.float32) + ln_b.astype(jnp.float32)
    return y.astype(x.dtype)

def setup_inputs(seed: int = 0) -> dict:
    key = jax.random.key(seed)
    ks = jax.random.split(key, 13)
    n_pages = PAST_LEN // PAGE_SIZE
    n_pool = (DEC_BATCH * n_pages * 5) // 4
    f32 = jnp.float32
    x_prompt = jax.random.normal(ks[0], (BATCH, SEQ, D_MODEL), f32)
    x_sample = jax.random.normal(ks[1], (DEC_BATCH, DEC_SEQ, D_MODEL), f32)
    cache_k = jax.random.normal(ks[2], (DEPTH, n_pool, PAGE_SIZE, N_HEADS, HEAD_DIM), f32)
    cache_v = jax.random.normal(ks[3], (DEPTH, n_pool, PAGE_SIZE, N_HEADS, HEAD_DIM), f32)
    cache_kidx = jax.random.normal(ks[4], (DEPTH, n_pool, PAGE_SIZE, IDX_DIM), f32)
    state_pool = jax.random.normal(ks[5], (DEPTH, DEC_BATCH, POOL_STATE, POOL_WIDTH), f32)
    page_table = jax.random.permutation(ks[6], n_pool)[:DEC_BATCH * n_pages].reshape(DEC_BATCH, n_pages).astype(jnp.int32)
    col_scale = np.ones((IN_COLS,), np.float32)
    col_scale[2 * ATTN_WIDTH:3 * ATTN_WIDTH] = DEEPNORM_BETA
    w_in = jax.random.normal(ks[7], (DEPTH, D_MODEL, IN_COLS), f32) * (D_MODEL ** -0.5) * jnp.asarray(col_scale)
    w_pool = jax.random.normal(ks[8], (DEPTH, N_POOL_GROUPS, POOL_GROUP_DIM, POOL_GROUP_DIM), f32) * (POOL_GROUP_DIM ** -0.5)
    pool_scale = 1.0 + 0.1 * jax.random.normal(ks[9], (DEPTH, POOL_WIDTH), f32)
    w_out = jax.random.normal(ks[10], (DEPTH, MIX_WIDTH, D_MODEL), f32) * (MIX_WIDTH ** -0.5) * DEEPNORM_BETA
    ln_g = 1.0 + 0.02 * jax.random.normal(ks[11], (DEPTH, D_MODEL), f32)
    ln_b = 0.02 * jax.random.normal(ks[12], (DEPTH, D_MODEL), f32)
    return {'x_prompt': x_prompt, 'x_sample': x_sample, 'cache_k': cache_k, 'cache_v': cache_v,
            'cache_kidx': cache_kidx, 'state_pool': state_pool, 'page_table': page_table,
            'w_in': w_in, 'w_pool': w_pool, 'pool_scale': pool_scale, 'w_out': w_out,
            'ln_g': ln_g, 'ln_b': ln_b}

def reference(x_prompt, x_sample, cache_k, cache_v, cache_kidx, state_pool, page_table,
              w_in, w_pool, pool_scale, w_out, ln_g, ln_b):
    xp, xs = x_prompt, x_sample
    S, T = xp.shape[1], xs.shape[1]
    past = page_table.shape[1] * PAGE_SIZE
    pos_p = jnp.arange(S)
    pos_s = past + jnp.arange(T)
    pk, pv, pki, ppool, sk, sv, ski, spool = [], [], [], [], [], [], [], []
    for l in range(DEPTH):
        q, k, v, ga, qi, ki, wi, u, gb = _project(xp, pos_p, w_in[l])
        a = _prompt_attention(q, k, v, qi, ki, wi)
        p = _pool_mix(u, 0, w_pool[l], pool_scale[l])
        xp = _combine(xp, a, p, ga, gb, w_out[l], ln_g[l], ln_b[l])
        pk.append(k); pv.append(v); pki.append(ki); ppool.append(u[:, -POOL_STATE:])
        q, k, v, ga, qi, ki, wi, u, gb = _project(xs, pos_s, w_in[l])
        a = _sample_attention(l, q, k, v, qi, ki, wi, cache_k, cache_v, cache_kidx, page_table)
        u_ext = jnp.concatenate([state_pool[l].astype(u.dtype), u], axis=1)
        p = _pool_mix(u_ext, POOL_STATE, w_pool[l], pool_scale[l])
        xs = _combine(xs, a, p, ga, gb, w_out[l], ln_g[l], ln_b[l])
        sk.append(k); sv.append(v); ski.append(ki); spool.append(u_ext[:, -POOL_STATE:])
    return (xp, xs, jnp.stack(pk), jnp.stack(pv), jnp.stack(pki), jnp.stack(ppool),
            jnp.stack(sk), jnp.stack(sv), jnp.stack(ski), jnp.stack(spool))


_drawn_inputs = setup_inputs


def setup_inputs(seed=0):
    import zlib

    import numpy as np

    out = dict(_drawn_inputs(seed))
    spreads = {}
    factors = {'cache_k': 3.447,
     'cache_v': 2.674,
     'cache_kidx': 3.067,
     'pool_scale': 3.187,
     'ln_g': 2.904,
     'ln_b': 2.906}
    for name, (base, spread) in spreads.items():
        noise = np.random.default_rng([zlib.crc32(name.encode()), seed]).standard_normal(out[name].shape)
        drawn = base * np.exp(spread * noise) if base else spread * noise
        out[name] = __import__('jax').numpy.asarray(drawn.astype(out[name].dtype))
    for name, factor in factors.items():
        out[name] = (out[name] * factor).astype(out[name].dtype)
    return out
```

```python
from contextlib import ExitStack

import concourse.bass as bass
from concourse import mybir

ALU = mybir.AluOpType
ACT = mybir.ActivationFunctionType
AX = mybir.AxisListType
F32 = mybir.dt.float32
F32R = mybir.dt.float32r
BF16 = mybir.dt.bfloat16
I32 = mybir.dt.int32

P = 128
D = 2048
KC = D // P
NP_ = 512
NB = 8
NT = 4
NS = NB * NT
T = NP_ + NS
HT = T // 2
TT = NP_ // P
H = 8
IH = 16
ID = 64
PAGES = 8
PAST = PAGES * P
L = PAST + NS
TOPK_P = 128
TOPK_S = 256
ROUND = 8
GROUPS = 4
WINDOWS = (2, 4, 8, 16)
HIST = 15
UE = HIST + NT
UW = HIST + NP_ + NB * UE
SCALE = 128.0 ** -0.5
ISCALE = 1.0 / 32.0
ALPHA = 2.0 ** 0.25
EPS = 1e-5
MASKED = -1e30
PICKED = -3e38
Q0, K0, V0, GA0, QI0, KI0, U0, GB0 = 0, 1024, 2048, 3072, 4096, 5120, 5200, 6224
KW = 80
HU = KC // 2
TRI = [0, 128, 384, 768, 1280]

TILE_A, TILE_C, TILE_B, TILE_D = 1, 9, 41, 57
SWAP_I = [*range(8, 16), *range(8), *range(16, 32)]
SWAP_H = [*range(16, 32), *range(16)]
WT = 20


class Turn:

    def __init__(self, slot, before):
        self.slot, self.full, self.free, self.read = slot, before + 1, before + 1, before + 2


def turn(n, slots, i=None, per=0):
    assert per % slots == 0
    return Turn(n % slots, n // slots if i is None else i * (per // slots) + n // slots)


class Banks:

    def __init__(self, banks):
        self.used = dict.fromkeys(banks, 0)

    def stage(self, names, banks, times=1):
        assert times == 1 or len(names) % len(banks) == 0, len(names)
        step = len(names) // len(banks)
        table = {name: (banks[k % len(banks)], self.used[banks[k % len(banks)]] + k // len(banks))
                 for k, name in enumerate(names)}
        assert len(table) == len(names)
        for k in range(len(names)):
            self.used[banks[k % len(banks)]] += times if times == 1 else 0
        for b in banks if times > 1 else ():
            self.used[b] += times * step

        def at(name, i=None, ago=0):
            b, n = table[name]
            return Turn(b, n if i is None else i * step + (n - ago * step))

        return at


class Steps:

    def __init__(self, eng, sem):
        self.eng, self.sem, self.done, self.i, self.per = eng, sem, 0, None, 0

    def value(self):
        return self.done if self.i is None else self.i * self.per + self.done

    def step(self, ins):
        ins.then_inc(self.sem, 1)
        self.done += 1

    def wait(self):
        self.eng.wait_ge(self.sem, self.value())

    def enter(self, i, per):
        self.i, self.per, self.start = i, per, self.done

    def leave(self, times):
        assert self.done - self.start == self.per, (self.done - self.start, self.per)
        self.done, self.i = self.start + times * self.per, None


def layer_program(nc, x_prompt, x_sample, cache_k, cache_v, cache_kidx, state_pool, page_table,
                  w_in, w_pool, pool_scale, w_out, ln_g, ln_b, square, idx_rot, head_rot, windows,
                  y_prompt, y_sample, p_k, p_v, p_kidx, p_pool, s_k, s_v, s_kidx, s_pool):
    ds = bass.ds
    ctx = ExitStack()
    with ctx:
        def sem(name):
            return ctx.enter_context(nc.semaphore(name))

        def sems(name, n):
            return [sem(f"{name}{j}") for j in range(n)]

        def sb(name, shape, dt=F32, where=ctx):
            return where.enter_context(nc.sbuf_tensor(name, shape, dt))

        actH = sb("actH", [P, KC, T], F32R)
        actL = sb("actL", [P, KC, T], F32R)
        rawW = sb("rawW", [P, 4, HU, P])
        wH = sb("wH", [P, 4, HU, P], F32R)
        wL = sb("wL", [P, 4, HU, P], F32R)
        mixed = sb("mixed", [P, KC, T])
        raw = sb("raw", [P, 2, T])
        rot = sb("rot", [P, T])
        qS = sb("qS", [P, H, NS])
        kS = sb("kS", [P, H, NS])
        vS = sb("vS", [NS, H, P])
        gateS = sb("gateS", [P, H, NS])
        sq = sb("sq", [P, 288])
        ident, causal, newmask = sq[:, 0:P], sq[:, P:2 * P], sq[0:NS, 256:288]
        pageT = sb("pageT", [1, NB * PAGES], I32)
        halfscale = sb("halfscale", [P, H])
        stat = sb("stat", [P, 32])
        maskT = sb("maskT", [P, PAGES, NS])
        maskTn = sb("maskTn", [NS, NS])
        outer = ExitStack()
        scoreS = sb("scoreS", [NS, L], F32, outer)
        scoreP = sb("scoreP", [P, TRI[4] - P], F32, outer)
        keepP = sb("keepP", [P, TRI[4]], BF16, outer)
        headrot = sb("headrot", [32, 2, T], F32, outer)
        wiN = sb("wiN", [P, 3, IH], F32, outer)
        top8 = sb("top8", [P, 8], F32, outer)
        with ExitStack() as s:
            xnat = sb("xnat", [P, 2, D], F32, s)
            xnatS = sb("xnatS", [NS, D], F32, s)
        with ExitStack() as s:
            kiT = sb("kiT", [P, T], F32, s)
            wiT = sb("wiT", [P, T], F32, s)
            irot = sb("irot", [P, 2, T], F32, s)
            wiB = sb("wiB", [P, IH, NS], F32, s)
            relu = sb("relu", [P, 2, 512], F32, s)
            kiPage = sb("kiPage", [P, 2, PAGES, ID], F32, s)
            kiPT = sb("kiPT", [P, 2, 4, P], F32, s)
            scoreST = sb("scoreST", [P, PAGES, NS], F32, s)
            scoreSTn = sb("scoreSTn", [NS, NS], F32, s)
            qiS = sb("qiS", [P, 2, IH, NS], F32, s)
            kiN = sb("kiN", [P, 5, ID], F32, s)
        with ExitStack() as s:
            qT = sb("qT", [P, 2, T], F32, s)
            kT = sb("kT", [P, 2, T], F32, s)
            vN = sb("vN", [P, 2, TT, P], F32, s)
            kN = sb("kN", [P, 5, P], F32, s)
            gate = sb("gate", [P, 2, T], F32, s)
            tanhC = sb("tanhC", [P, T], F32, s)
            prob = sb("prob", [P, TRI[4]], F32, s)
            probT = sb("probT", [P, 2, TT, P], F32, s)
        outer.close()
        with ExitStack() as s:
            kPage = sb("kPage", [P, 2, H, P], F32, s)
            vPage = sb("vPage", [P, 4, H, P], F32, s)
            kPT = sb("kPT", [P, 2, 4, P], F32, s)
            sT = sb("sT", [P, PAGES, NS], F32, s)
            sTn = sb("sTn", [NS, NS], F32, s)
            probS = sb("probS", [NS, L], F32, s)
            probST = sb("probST", [P, PAGES, NS], F32, s)
            probSTn = sb("probSTn", [NS, NS], F32, s)
            U = sb("U", [P, 2, UW], F32, s)
            win = sb("win", [P, 2, UW], F32, s)
            pooled = sb("pooled", [P, 2, T], F32, s)
            wp = sb("wp", [P, 2, 256], F32, s)
            hist = sb("hist", [NB * HIST, 2, P], F32, s)
            uN = sb("uN", [NS, 2, P], F32, s)
            newU = sb("newU", [P, 2, NS], F32, s)
            wtab = sb("wtab", [P, GROUPS * WT], F32, s)
        with ExitStack() as s:
            y = sb("y", [P, 5, D], F32, s)
            bn = sb("bn", [P, 5, 4, 6], F32, s)
            mv = sb("mv", [P, 5, 2], F32, s)
            std = sb("std", [P, 5], F32, s)
        flat = mixed[:].rearrange("p k t -> p (k t)")
        gbc, bbc = flat[:, 0:D], flat[:, D:2 * D]
        qiT = mixed[:, 0:H, :]

        acc = [ctx.enter_context(nc.psum_tensor(f"acc{j}", [P, 2, 512], F32)) for j in range(2)]
        four = (4, 5, 6, 7)
        bank = {j: ctx.enter_context(nc.psum_tensor(f"bank{j}", [P, 512], F32)) for j in four}
        wiD = nc.dram_tensor("wiD", [IH, NS], F32, kind="Internal").ap()

        w_landed = sems("w_landed", 4)
        high_ready = sems("high_ready", 4)
        stage_ready = sems("stage_ready", 4)
        stage_free = sems("stage_free", 2)
        tile_ready = sems("tile_ready", 2)
        acc_copied = sems("acc_copied", 2)
        bank_full = {j: sem(f"bank_full{j}") for j in four}
        bank_free = {j: sem(f"bank_free{j}") for j in four}
        apart = sem("apart")
        square_in = sem("square_in")
        consts_in = sem("consts_in")
        irot_in = sem("irot_in")
        pages_in = sem("pages_in")
        x_in = sems("x_in", 2)
        xs_in = sem("xs_in")
        x_high = sem("x_high")
        ki_ready = sem("ki_ready")
        ki_twice = sem("ki_twice")
        wi_out = sem("wi_out")
        wi_back = sem("wi_back")
        qi_ready = sem("qi_ready")
        qis_near = sem("qis_near")
        qis_far = sem("qis_far")
        relu_full = sems("relu_full", 2)
        kip_in = sems("kip_in", 2)
        drop_ready = sem("drop_ready")
        head_ready = sem("head_ready")
        gate_ready = sem("gate_ready")
        exp_ready = sem("exp_ready")
        prob_ready = sem("prob_ready")
        dve_steps = sem("dve_steps")
        kn_sent = sem("kn_sent")
        vn_sent = sems("vn_sent", 2)
        c_done = sem("c_done")
        k_in = sems("k_in", 2)
        k_free = sems("k_free", 2)
        v_in = sems("v_in", 4)
        v_free = sems("v_free", 4)
        max_ready = sem("max_ready")
        probS_ready = sem("probS_ready")
        hist_in = sems("hist_in", 2)
        wtab_in = sem("wtab_in")
        wp_in = sem("wp_in")
        pooled_ready = sem("pooled_ready")
        un_sent = sem("un_sent")
        mix_high = sem("mix_high")
        mix_low = sem("mix_low")
        y_in = sem("y_in")
        ln_in = sem("ln_in")
        var_ready = sem("var_ready")
        std_ready = sem("std_ready")
        norm_ready = sem("norm_ready")
        y_ready = sem("y_ready")
        kidx_sent = sem("kidx_sent")
        spool_sent = sem("spool_sent")
        y_sent = sem("y_sent")

        banks = Banks(four)
        xb = banks.stage([f"x{t}{q}" for t in range(TT + 1) for q in range(4)], four)
        ab = banks.stage(["wi", "ki", "kis", *(f"r{t}_{h}" for t in (3, 2, 1) for h in range(IH))], four)
        sbk = banks.stage([f"{w}{j}" for j in range(2) for w in ("T", "R")], four, 4)
        nb = banks.stage(["Rn", "S0", "S1", "Sn"], four)

        def c_uses(X):
            return [f"{u}{X}" for u in ("P0", "P1", "O0", "P2", "O1", "P3", "O2", "O3")]

        cb = banks.stage(["v0", "vs0", "v1", "vs1", "k0", "ks0", "S00", "S10", "S20", "S30", "k1", "ks1",
                          *c_uses(0), "S01", "S11", "S21", "S31", *c_uses(1)], four, 4)
        mb = banks.stage(["mask"], four)

        def key_uses(X, lo, hi):
            return [f"K{p}{h}{X}" for p in range(lo, hi) for h in range(2)]

        bb = banks.stage([*key_uses(0, 0, 4), "h0", *key_uses(0, 4, 6), "h1", *key_uses(0, 6, 8), "S00", "S10",
                          "u0", "Pt0", *key_uses(1, 0, 4), "u1", *key_uses(1, 4, 8), "S01", "S11", "Pt1",
                          "m00", "m01", "m10", "m11"], (4, 5), GROUPS)
        b6 = banks.stage(["sT0", "sn0", "sT1", "sn1"], (6,), GROUPS)
        b7 = banks.stage(["o0", "o1"], (7,), GROUPS)
        yb = banks.stage(["yp0", "ys0", "yp1", "ys1"], four, 8)

        def bank_wait(eng, b):
            eng.wait_ge(bank_full[b.slot], b.full)
            return bank[b.slot]

        def stand_alone(eng):
            eng.sem_inc(apart, 1)

        block = ctx.enter_context(nc.Block())

        w_view = w_in[0].rearrange("(k p) c -> p k c", p=P)
        wo_view = w_out[0].rearrange("(k p) c -> p k c", p=P)

        @block.sync
        def _(sp):
            def load_unit(view, half, col, t, width=P):
                if not (isinstance(t.free, int) and t.free == 1):
                    sp.wait_ge(stage_ready[t.slot], t.free - 1)
                    stand_alone(sp)
                sp.dma_start(rawW[:, t.slot, :, 0:width],
                             view[:, half * HU:(half + 1) * HU, ds(col, width)]).then_inc(w_landed[t.slot], 16)

            def load_tile(view, col, tile, i=None, per=0):
                for half in range(2):
                    load_unit(view, half, col, turn(2 * tile + half, 4, i, 2 * per))

            for half in range(2):
                load_unit(w_view, half, KI0, turn(half, 4), KW)
            sp.dma_start(pageT[:], page_table.rearrange("(a b) c -> a (b c)", a=1)).then_inc(pages_in, 16)
            sp.dma_start(s_pool[0, :, 0:HIST - NT, :], state_pool[0, :, NT:HIST, :]).then_inc(spool_sent, 16)
            sp.wait_ge(pages_in, 16)

            def load_page(cache, dst, index, done):
                stand_alone(sp)
                page = sp.value_load(pageT[0:1, ds(index, 1)], min_val=0, max_val=cache.shape[0] - 1)
                sp.dma_start(dst, cache[ds(page, 1)].rearrange("a p n -> p (a n)")).then_inc(done, 16)

            with sp.Fori(0, 4) as i:
                for j in range(2):
                    load_tile(w_view, QI0 + (2 * i + j) * P, TILE_A + j, i, 2)
            for j in range(2):
                load_tile(w_view, V0 + j * P, TILE_C + j)
            for q in range(4):
                b = xb(f"x{TT}{q}")
                sp.wait_ge(bank_free[b.slot], b.read)
            def index_pages(n, j):
                for p in range(PAGES):
                    load_page(cache_kidx[0], kiPage[:, j, p, :], n * PAGES + p, kip_in[j])

            for j in range(2):
                index_pages(j, j)
            with sp.Fori(0, 3) as i:
                for j in range(2):
                    b = sbk(f"T{j}", i)
                    sp.wait_ge(bank_full[b.slot], b.full)
                    index_pages(2 * i + (j + 2), j)
            order = ((GA0, 0), (K0, 0), (Q0, 0), (K0, 1), (Q0, 1), (GA0, 1), (V0, 2), (V0, 3))
            with sp.Fori(0, 3) as i:
                for j, (col, X) in enumerate(order):
                    load_tile(w_view, col + (2 * i + X) * P, TILE_C + 2 + j, i, 8)
            for j, (col, X) in enumerate(order[:6]):
                load_tile(w_view, col + (6 + X) * P, TILE_C + 26 + j)
            for j in range(2):
                load_tile(w_view, U0 + j * P, TILE_B + j)
            sp.wait_ge(c_done, 1)
            ck = cache_k[0].rearrange("n p h d -> n p (h d)")
            cv = cache_v[0].rearrange("n p h d -> n p (h d)")
            sp.dma_start(wtab[:], windows).then_inc(wtab_in, 16)

            def group(g, last):
                b = bb("m11", g, ago=1)
                sp.wait_ge(bank_full[b.slot], b.full)
                stand_alone(sp)
                for j in range(2):
                    sp.dma_start(hist[:, j, :], state_pool[0].rearrange("b r c -> (b r) c")[:, ds((2 * g + j) * P, P)]
                                 ).then_inc(hist_in[j], 16)
                sp.dma_start(wp[:], w_pool[0, ds(g, 1)].rearrange("g (c p) d -> p (g c) d", p=P)).then_inc(wp_in, 16)

                def key_page(X, p):
                    t = turn(8 * X + p, 2, g, 16)
                    sp.wait_ge(k_free[t.slot], t.free)
                    load_page(ck, kPage[:, t.slot, :, :].rearrange("p h d -> p (h d)"),
                              (2 * g + X) * PAGES + p, k_in[t.slot])

                def value_page(X, p):
                    t = turn(8 * X + p, 4, g, 16)
                    sp.wait_ge(v_free[t.slot], t.free)
                    load_page(cv, vPage[:, t.slot, :, :].rearrange("p h d -> p (h d)"),
                              (2 * g + X) * PAGES + p, v_in[t.slot])

                def unit(j):
                    tile, half = 2 + j // 2, j % 2
                    t = turn(2 * (TILE_B + tile) + half, 4, g, 8)
                    if tile < 4:
                        load_unit(w_view, half, GB0 + (2 * g + tile - 2) * P, t)
                    elif last:
                        load_unit(wo_view, half, (tile - 4) * P, t)
                    else:
                        load_unit(w_view, half, U0 + (2 * g + 2 + tile - 4) * P, t)

                for X in range(2):
                    key_page(X, 0)
                    key_page(X, 1)
                    unit(4 * X)
                    if X:
                        unit(5)
                    for p in range(4):
                        value_page(X, p)
                    if not X:
                        unit(1)
                    key_page(X, 2)
                    key_page(X, 3)
                    unit(4 * X + 2)
                    key_page(X, 4)
                    key_page(X, 5)
                    unit(4 * X + 3)
                    key_page(X, 6)
                    key_page(X, 7)
                    for p in range(4, PAGES):
                        value_page(X, p)

            with sp.Fori(0, GROUPS - 1) as g:
                group(g, False)
            group(GROUPS - 1, True)
            for name in ("m10", "m11"):
                b = bb(name, GROUPS - 1)
                sp.wait_ge(bank_free[b.slot], b.read)
            sp.wait_ge(un_sent, 32 * (2 * GROUPS + 1))
            for t in range(TT):
                sp.dma_start(y[:, t, :], x_prompt[0, t * P:(t + 1) * P, :]).then_inc(y_in, 16)
            sp.dma_start(y[0:NS, TT, :], x_sample.rearrange("b t d -> (b t) d")).then_inc(y_in, 16)
            for d in (2, 3):
                load_tile(wo_view, d * P, TILE_D + d)
            sp.wait_ge(mix_low, KC)
            sp.dma_start(gbc, ln_g[0].partition_broadcast(P)).then_inc(ln_in, 16)
            sp.dma_start(bbc, ln_b[0].partition_broadcast(P)).then_inc(ln_in, 16)
            with sp.Fori(0, 6) as i:
                for j in range(2):
                    load_tile(wo_view, (2 * i + 4 + j) * P, TILE_D + 4 + j, i, 2)
            for t in range(TT + 1):
                n = P if t < TT else NS
                dst = y_prompt[0, t * P:(t + 1) * P, :] if t < TT else y_sample.rearrange("b t d -> (b t) d")
                sp.wait_ge(y_ready, t + 1)
                sp.dma_start(dst, y[0:n, t, :]).then_inc(y_sent, 16)
            sp.wait_ge(y_sent, 16 * (TT + 1))
            sp.wait_ge(spool_sent, 16)
            sp.wait_ge(kidx_sent, 32)
            sp.wait_ge(kn_sent, 32 * (H + 1))
            sp.wait_ge(vn_sent[0], 32 * (H // 2 + 1))
            sp.wait_ge(vn_sent[1], 32 * (H // 2 + 1))
            sp.wait_ge(un_sent, 32 * (2 * GROUPS + 1))

        @block.gpsimd
        def _(pool):
            def low(slot, full, width=P):
                pool.wait_ge(high_ready[slot], full)
                pool.tensor_tensor(wL[:, slot, :, 0:width], rawW[:, slot, :, 0:width],
                                   wH[:, slot, :, 0:width].bitcast(F32), ALU.subtract).then_inc(stage_ready[slot], 1)

            low(0, 1, KW)
            low(1, 1, KW)
            with pool.Fori(0, (2 * (TILE_D + KC) - 2) // 4) as i:
                for j in range(4):
                    t = turn(2 + j, 4, i, 4)
                    low(t.slot, t.full)

        @block.scalar
        def _(act):
            def high(tile, half, i=None, per=0, width=P):
                t = turn(2 * tile + half, 4, i, 2 * per)
                act.wait_ge(w_landed[t.slot], 16 * t.full)
                if half == 0:
                    act.wait_ge(stage_free[t.slot // 2], t.free)
                elif not (isinstance(t.free, int) and t.free == 1):
                    act.wait_ge(tile_ready[t.slot // 2], t.free - 1)
                act.activation(wH[:, t.slot, :, 0:width], rawW[:, t.slot, :, 0:width],
                               ACT.Copy).then_inc(high_ready[t.slot], 1)

            def projected(tile, i=None, per=0):
                t = turn(tile, 2, i, per)
                act.wait_ge(tile_ready[t.slot], t.full)
                return acc[t.slot][:, :, 0:HT], acc_copied[t.slot]

            def halves(ap):
                return ap.rearrange("p (a t) -> p a t", a=2)

            def out_of(b, dst, src):
                act.activation(dst, src, ACT.Copy).then_inc(bank_free[b.slot], 1)

            act.dma_start(xnat[:, 0, :], x_prompt[0, 0:P, :]).then_inc(x_in[0], 16)
            act.dma_start(sq[:], square).then_inc(square_in, 16)
            act.dma_start(xnat[:, 1, :], x_prompt[0, P:2 * P, :]).then_inc(x_in[1], 16)
            act.dma_start(xnatS[:], x_sample.rearrange("b t d -> (b t) d")).then_inc(xs_in, 16)
            act.dma_start(headrot[:], head_rot).then_inc(consts_in, 16)
            act.dma_start(halfscale[:], pool_scale[0].rearrange("(j p) -> p j", p=P), allow_slow_non_contiguous=True).then_inc(consts_in, 16)

            for half in range(2):
                high(0, half, width=KW)
            for t in range(TT + 1):
                n = P if t < TT else NS
                for q in range(4):
                    b = xb(f"x{t}{q}")
                    src = bank_wait(act, b)[:, 0:4 * n]
                    act.activation(actH[:, 4 * q:4 * q + 4, t * P:t * P + n],
                                   src.rearrange("p (k t) -> p k t", k=4), ACT.Copy).then_inc(x_high, 1)
                if t < 2:
                    act.dma_start(xnat[:, t, :], x_prompt[0, (t + 2) * P:(t + 3) * P, :]).then_inc(x_in[t], 16)
            for q in range(4):
                b = xb(f"x{TT}{q}")
                act.wait_ge(bank_free[b.slot], b.read)
            act.dma_start(irot[:], idx_rot).then_inc(irot_in, 16)

            high(1, 0)
            high(1, 1)
            src, copied = projected(0)
            high(2, 0)
            act.activation(halves(wiT[ID:KW, :]), src[ID:KW], ACT.Copy, scale=ISCALE)
            act.activation(halves(kiT[0:ID, :]), src[0:ID], ACT.Copy).then_inc(copied, 1)
            act.wait_ge(copied, 2)
            act.dma_start(wiD, wiT[ID:KW, NP_:T]).then_inc(wi_out, 16)
            high(2, 1)
            act.wait_ge(wi_out, 16)
            act.dma_start(wiB[:].rearrange("p h t -> p (h t)"),
                          wiD.rearrange("h t -> (h t)").partition_broadcast(P)).then_inc(wi_back, 16)
            act.wait_ge(ki_ready, 1)
            act.dma_start(kiT[ID:P, :], kiT[0:ID, :]).then_inc(ki_twice, 16)
            with act.Fori(0, 4) as i:
                for j in range(2):
                    high(TILE_A + j + 2, 0, i, 2)
                    src, copied = projected(TILE_A + j, i, 2)
                    act.wait_ge(qi_ready, 2 * i + j + 1)
                    act.activation(halves(raw[:, j]), src, ACT.Copy).then_inc(copied, 1)
                    high(TILE_A + j + 2, 1, i, 2)
            act.wait_ge(qis_near, 1)
            act.dma_start(qiS[ID:P, 1, 0:IH:2, :], qiT[0:ID, :, NP_:T]).then_inc(qis_far, 16)
            act.dma_start(qiS[0:ID, 0, 1:IH:2, :], qiT[ID:P, :, NP_:T]).then_inc(qis_far, 16)
            b = ab("ki")
            out_of(b, kiN[:, 0:TT, :].rearrange("p a b -> p (a b)"), bank_wait(act, b)[:, 0:TT * ID])
            b2 = ab("kis")
            out_of(b2, kiN[0:NS, TT, :], bank_wait(act, b2)[0:NS, 0:ID])
            act.wait_ge(bank_free[b.slot], b.read)
            act.dma_start(p_kidx[0, 0].rearrange("(t p) d -> p t d", p=P), kiN[:, 0:TT, :]).then_inc(kidx_sent, 16)
            act.wait_ge(bank_free[b2.slot], b2.read)
            act.dma_start(s_kidx[0].rearrange("b t d -> (b t) d"), kiN[0:NS, TT, :]).then_inc(kidx_sent, 16)

            def rectify(b, before, n, rows, t):
                src = bank_wait(act, b)
                if before is not None:
                    act.wait_ge(bank_free[before.slot], before.read)
                act.activation(relu[0:rows, t.slot, 0:n], src[0:rows, 0:n], ACT.Relu).then_inc(relu_full[t.slot], 1)

            n, products = 0, []
            for t in (3, 2, 1):
                for h in range(IH):
                    products.append(ab(f"r{t}_{h}"))
                    rectify(products[n], products[n - 2] if n > 1 else None, (t + 1) * P, P, turn(n, 2))
                    n += 1
            for b in products[-2:]:
                act.wait_ge(bank_free[b.slot], b.read)
            with act.Fori(0, 4) as i:
                for j in range(2):
                    b = sbk(f"T{j}", i)
                    src = bank_wait(act, b)
                    out_of(b, kiPT[:, j, :, :].rearrange("p a k -> p (a k)"), src[:])
                    rectify(sbk(f"R{j}", i), sbk(f"R{j}", i, ago=1), 512, P, turn(3 * IH + j, 2, i, 2))
            rectify(nb("Rn"), sbk("R0", 3), 512, NS, turn(3 * IH + NB, 2))

            b = nb("Sn")
            act.wait_ge(bank_free[b.slot], b.read)
            act.wait_ge(kidx_sent, 32)
            with act.Fori(0, 4) as i:
                def values(X):
                    b = cb(f"v{X}", i)
                    src = bank_wait(act, b)
                    act.wait_ge(vn_sent[X], 32 * i + 32)
                    out_of(b, vN[:, X, :, :].rearrange("p t d -> p (t d)"), src[:])
                    b2 = cb(f"vs{X}", i)
                    out_of(b2, vS[:, ds(2 * i + X, 1), :].rearrange("p a d -> p (a d)"), bank_wait(act, b2)[0:NS, 0:P])
                    act.wait_ge(bank_free[b.slot], b.read)
                    act.dma_start(p_v[0, 0, :, ds(2 * i + X, 1), :].rearrange("(t p) a d -> p t (a d)", p=P),
                                  vN[:, X, :, :]).then_inc(vn_sent[X], 16)
                    act.wait_ge(bank_free[b2.slot], b2.read)
                    act.dma_start(s_v[0, :, :, ds(2 * i + X, 1), :].rearrange("b t a d -> (b t) (a d)"),
                                  vS[:, ds(2 * i + X, 1), :].rearrange("p a d -> p (a d)")).then_inc(vn_sent[X], 16)

                def keys(X):
                    b, b2 = cb(f"k{X}", i), cb(f"ks{X}", i)
                    src = bank_wait(act, b)
                    act.wait_ge(kn_sent, 64 * i + 32 * X + 32)
                    out_of(b, kN[:, 0:TT, :].rearrange("p t d -> p (t d)"), src[:])
                    out_of(b2, kN[0:NS, TT, :], bank_wait(act, b2)[0:NS, 0:P])
                    act.wait_ge(bank_free[b.slot], b.read)
                    act.dma_start(p_k[0, 0, :, ds(2 * i + X, 1), :].rearrange("(t p) a d -> p t (a d)", p=P),
                                  kN[:, 0:TT, :]).then_inc(kn_sent, 16)
                    act.wait_ge(bank_free[b2.slot], b2.read)
                    act.dma_start(s_k[0, :, :, ds(2 * i + X, 1), :].rearrange("b t a d -> (b t) (a d)"),
                                  kN[0:NS, TT, :]).then_inc(kn_sent, 16)

                def sample_part(dst, X, src):
                    act.activation(dst[:, ds(2 * i + X, 1), :].rearrange("p a t -> p (a t)"), src[:, X, NP_:T], ACT.Copy)

                def exps(X):
                    for t in range(TT):
                        b = cb(f"S{t}{X}", i)
                        act.wait_ge(bank_free[b.slot], b.read)
                        pr = prob[:, TRI[t]:TRI[t + 1]]
                        act.activation(pr, pr, ACT.Exp, bias=stat[:, t:t + 1], scale=-1.0,
                                       accum_out=stat[:, 8 + t:9 + t]).then_inc(exp_ready, 1)

                def probs_turned(X):
                    for t in range(TT):
                        b = cb(f"P{t}{X}", i)
                        src = bank_wait(act, b)
                        if t >= 2:
                            bank_wait(act, cb(f"O{t - 2}{X}", i))
                        out_of(b, probT[:, t % 2, 0:t + 1, :].rearrange("p s t -> p (s t)"), src[:, 0:(t + 1) * P])

                for j in range(8):
                    high(TILE_C + j + 2, 0, i, 8)
                    if j in (1, 2):
                        values(j - 1)
                    if j == 3:
                        act.wait_ge(gate_ready, 2 * i + 1)
                        sample_part(gateS, 0, gate)
                    if j == 4:
                        keys(0)
                        sample_part(kS, 0, kT)
                    if j == 5:
                        act.wait_ge(head_ready, 4 * i + 3)
                        sample_part(qS, 0, qT)
                        exps(0)
                    if j == 6:
                        keys(1)
                        sample_part(kS, 1, kT)
                        probs_turned(0)
                    if j == 7:
                        act.wait_ge(head_ready, 4 * i + 5)
                        sample_part(qS, 1, qT)
                        exps(1)
                    src, copied = projected(TILE_C + j, i, 8)
                    if j in (2, 7):
                        act.activation(halves(tanhC[:]), src, ACT.Tanh, scale=0.5)
                    dst = {0: raw[:, 0], 1: raw[:, 1], 2: raw[:, 0], 3: kT[:, 0], 4: qT[:, 0], 5: kT[:, 1],
                           6: qT[:, 1], 7: raw[:, 1]}[j]
                    act.activation(halves(dst), src, ACT.Copy).then_inc(copied, 1)
                    high(TILE_C + j + 2, 1, i, 8)
                act.wait_ge(gate_ready, 2 * i + 2)
                sample_part(gateS, 1, gate)
                probs_turned(1)
            for t in range(TT):
                b = cb(f"O{t}1", 3)
                act.wait_ge(bank_free[b.slot], b.read)
            act.wait_ge(kn_sent, 32 * (H + 1))
            for X in range(2):
                act.wait_ge(vn_sent[X], 32 * (H // 2 + 1))
            b = mb("mask")
            act.wait_ge(bank_free[b.slot], b.read)
            act.activation(stat[:, 30:31], halfscale[:, 0:1], ACT.Copy).then_inc(c_done, 1)

            with act.Fori(0, GROUPS) as g:
                def key_halves(X, lo, hi):
                    for p in range(lo, hi):
                        b = bb(f"K{p}0{X}", g)
                        out_of(b, kPT[:, 0, :, :].rearrange("p h k -> p (h k)"), bank_wait(act, b)[:])

                def sample_view(ap, lo, hi):
                    return ap[:, HIST + NP_:UW].rearrange("p (b r) -> p b r", b=NB)[:, :, lo:hi]

                def history(t):
                    b = bb(f"h{t}", g)
                    src = bank_wait(act, b)[:, 0:NB * HIST].rearrange("p (b r) -> p b r", b=NB)
                    act.wait_ge(pooled_ready, 2 * g + t + 1)
                    out_of(b, sample_view(U[:, t], 0, HIST), src)

                def copy_tile(t):
                    src, copied = projected(TILE_B + t, g, 4)
                    if t < 2:
                        act.activation(U[:, t, HIST:HIST + HT], src[:, 0, :], ACT.Copy)
                        act.activation(U[:, t, HIST + HT:HIST + NP_], src[:, 1, 0:NP_ - HT], ACT.Copy)
                        act.activation(newU[:, t, :], src[:, 1, NP_ - HT:HT], ACT.Copy)
                        act.activation(sample_view(U[:, t], HIST, UE),
                                       src[:, 1, NP_ - HT:HT].rearrange("p (b r) -> p b r", b=NB),
                                       ACT.Copy).then_inc(copied, 1)
                    else:
                        if t == 3:
                            act.wait_ge(gate_ready, H + 2 * g + 1)
                        act.activation(halves(rot[:]), src, ACT.Tanh, scale=0.5)
                        act.activation(halves(raw[:, t - 2]), src, ACT.Copy).then_inc(copied, 1)

                def last_rows(t):
                    b = bb(f"u{t}", g)
                    src = bank_wait(act, b)
                    act.wait_ge(un_sent, 64 * g + 32 * t + 32)
                    act.activation(uN[0:HIST, 0, :], src[0:HIST, 0:P], ACT.Copy)
                    out_of(b, uN[:, 1, :], src[0:NS, P:2 * P])
                    act.wait_ge(bank_free[b.slot], b.read)
                    col = ds((2 * g + t) * P, P)
                    act.dma_start(p_pool[0, 0, :, col], uN[0:HIST, 0, :]).then_inc(un_sent, 16)
                    act.dma_start(s_pool[0, :, HIST - NT:HIST, col], uN[:, 1, :]).then_inc(un_sent, 16)

                for X in range(2):
                    key_halves(X, 0, 4)
                    high(TILE_B + 2 * X + 2, 0, g, 4)
                    if X == 0:
                        history(0)
                    else:
                        last_rows(1)
                    key_halves(X, 4, 6)
                    if X == 0:
                        history(1)
                    key_halves(X, 6, 8)
                    copy_tile(2 * X)
                    high(TILE_B + 2 * X + 2, 1, g, 4)
                    act.wait_ge(max_ready, 2 * g + X + 1)
                    for n, (b, lo, hi) in enumerate(((bb(f"S0{X}", g), 0, 512), (bb(f"S1{X}", g), 512, PAST),
                                                     (b6(f"sn{X}", g), PAST, L))):
                        act.activation(probS[:, lo:hi], bank[b.slot][0:NS, 0:hi - lo], ACT.Exp, bias=stat[0:NS, 20:21],
                                       scale=SCALE, accum_out=stat[0:NS, 21 + n:22 + n]).then_inc(bank_free[b.slot], 1)
                    high(TILE_B + 2 * X + 3, 0, g, 4)
                    if X == 0:
                        last_rows(0)
                    b = bb(f"Pt{X}", g)
                    src = bank_wait(act, b)
                    act.activation(probST[:].rearrange("p a t -> p (a t)"), src[:, 0:PAGES * NS], ACT.Copy)
                    out_of(b, probSTn[:], src[0:NS, PAGES * NS:(PAGES + 1) * NS])
                    copy_tile(2 * X + 1)
                    high(TILE_B + 2 * X + 3, 1, g, 4)

            for name in ("m10", "m11"):
                b = bb(name, GROUPS - 1)
                act.wait_ge(bank_free[b.slot], b.read)
            b = b7("o1", GROUPS - 1)
            act.wait_ge(bank_free[b.slot], b.read)
            for k in range(KC):
                act.activation(actH[:, k, :], mixed[:, k, :], ACT.Copy).then_inc(mix_high, 1)
            with act.Fori(0, 7) as i:
                for j in range(2):
                    high(TILE_D + j + 2, 0, i, 2)
                    src, copied = projected(TILE_D + j, i, 2)
                    act.activation(halves(raw[:, j]), src, ACT.Copy).then_inc(copied, 1)
                    high(TILE_D + j + 2, 1, i, 2)
            for j in range(2):
                src, copied = projected(TILE_D + 14 + j)
                act.activation(halves(raw[:, j]), src, ACT.Copy).then_inc(copied, 1)
            act.wait_ge(var_ready, 1)
            act.activation(std[:], mv[:, :, 1], ACT.Sqrt).then_inc(std_ready, 1)
            act.wait_ge(var_ready, 2)
            for t in range(TT + 1):
                n = P if t < TT else NS
                act.activation(y[0:n, t, :], y[0:n, t, :], ACT.Identity, bias=stat[0:n, 8 + t:9 + t],
                               scale=stat[0:n, t:t + 1]).then_inc(norm_ready, 1)

        @block.tensor
        def _(pe):
            for s in (*stage_free, *acc_copied, *bank_free.values(), *k_free, *v_free):
                pe.sem_inc(s, 1)
            pe.sem_inc(head_ready, 1)
            for s in (pooled_ready, qi_ready):
                pe.sem_inc(s, 2)
            for s in (*vn_sent, kn_sent, un_sent):
                pe.sem_inc(s, 32)

            def unit(tile, half, i=None, per=0, width=P, quarters=(0, 1), chunk_ready=None):
                t, u = turn(tile, 2, i, per), turn(2 * tile + half, 4, i, 2 * per)
                if 0 in quarters:
                    pe.wait_ge(stage_ready[u.slot], u.full)
                    if half == 0:
                        pe.wait_ge(acc_copied[t.slot], t.free)
                for q in quarters:
                    for k in range(q * HU // 2, (q + 1) * HU // 2):
                        kk = half * HU + k
                        if chunk_ready is not None:
                            pe.wait_ge(chunk_ready, kk + 1)
                        for w, parts in ((wH, (actH, actL)), (wL, (actH,))):
                            for a in parts:
                                for e in range(2):
                                    last = pe.matmul(acc[t.slot][0:width, e, 0:HT], w[:, u.slot, k, 0:width],
                                                     a[:, kk, e * HT:(e + 1) * HT], start=(kk == 0 and w is wH and a is actH),
                                                     stop=(kk == KC - 1 and w is wL))
                if 1 in quarters:
                    last.then_inc(tile_ready[t.slot] if half else stage_free[t.slot], 1)

            def take(b):
                pe.wait_ge(bank_free[b.slot], b.free)
                return bank[b.slot]

            def full(b, last):
                last.then_inc(bank_full[b.slot], 1)

            def copied(tile, i=None, per=0):
                t = turn(tile, 2, i, per)
                pe.wait_ge(acc_copied[t.slot], t.read)

            pe.wait_ge(square_in, 16)
            for t in range(TT + 1):
                n = P if t < TT else NS
                if t < TT:
                    pe.wait_ge(x_in[t % 2], 16 * (t // 2 + 1))
                else:
                    pe.wait_ge(xs_in, 16)
                src = xnat[:, t % 2, :] if t < TT else xnatS[:, :]
                for q in range(4):
                    b = xb(f"x{t}{q}")
                    dst = take(b)
                    for j in range(4):
                        last = pe.transpose(dst[:, j * n:(j + 1) * n], src[:, (4 * q + j) * P:(4 * q + j + 1) * P],
                                            ident[0:n, 0:n])
                    full(b, last)
            for q in range(4):
                b = xb(f"x{TT}{q}")
                pe.wait_ge(bank_free[b.slot], b.read)

            for half in range(2):
                unit(0, half, width=KW)
            with pe.Fori(0, 4) as i:
                for j in range(2):
                    for half in range(2):
                        unit(TILE_A + j, half, i, 2)
            b = ab("wi")
            dst = take(b)
            copied(0)
            for t in range(1, TT):
                last = pe.transpose(dst[:, (t - 1) * IH:t * IH], wiT[ID:KW, t * P:(t + 1) * P], ident[ID:KW, ID:KW])
            full(b, last)
            pe.wait_ge(ki_ready, 1)
            b = ab("ki")
            dst = take(b)
            for t in range(TT):
                last = pe.transpose(dst[:, t * ID:(t + 1) * ID], kiT[0:ID, t * P:(t + 1) * P], ident[0:ID, 0:ID])
            full(b, last)
            b = ab("kis")
            full(b, pe.transpose(take(b)[0:NS, 0:ID], kiT[0:ID, NP_:T], ident[0:ID, 0:ID]))
            pe.wait_ge(ki_twice, 16)
            for t in (3, 2, 1):
                for h in range(IH):
                    if t == 3 and h % 2 == 0:
                        pe.wait_ge(qi_ready, h // 2 + 3)
                    b = ab(f"r{t}_{h}")
                    part = slice(ID * (h % 2), ID * (h % 2) + ID)
                    full(b, pe.matmul(take(b)[:, 0:(t + 1) * P], qiT[part, h // 2, t * P:(t + 1) * P],
                                      kiT[part, 0:(t + 1) * P], start=True, stop=True))
            pe.wait_ge(qis_near, 1)
            pe.wait_ge(qis_far, 32)
            with pe.Fori(0, 4) as i:
                for j in range(2):
                    b = sbk(f"T{j}", i)
                    dst = take(b)
                    pe.wait_ge(kip_in[j], 16 * PAGES * i + 16 * PAGES)
                    for a in range(PAGES // 2):
                        last = pe.transpose(dst[:, a * P:(a + 1) * P],
                                            kiPage[:, j, 2 * a:2 * a + 2, :].rearrange("p a d -> p (a d)"), ident)
                    full(b, last)
                    b2 = sbk(f"R{j}", i)
                    dst = take(b2)
                    pe.wait_ge(bank_free[b.slot], b.read)
                    for a in range(PAGES // 2):
                        last = pe.matmul(dst[:, a * P:(a + 1) * P], kiPT[:, j, a, :],
                                         qiS[:, :, :, ds((2 * i + j) * NT, NT)].rearrange("p e h t -> p (e h) t"),
                                         start=True, stop=True)
                    full(b2, last)
            b = nb("Rn")
            full(b, pe.matmul(take(b)[0:NS, :], kiT[0:ID, NP_:T],
                              qiS[0:ID, 0, :, :].rearrange("p h t -> p (h t)"), start=True, stop=True))
            pe.wait_ge(bank_free[b.slot], b.read)
            for half in range(2):
                b = nb(f"S{half}")
                dst = take(b)
                for p in range(4):
                    last = pe.transpose(dst[0:NS, p * P:(p + 1) * P], scoreST[:, 4 * half + p, :], ident)
                full(b, last)
            b = nb("Sn")
            full(b, pe.transpose(take(b)[0:NS, 0:NS], scoreSTn[:], ident[0:NS, 0:NS]))

            with pe.Fori(0, 4) as i:
                def by_token(name, X, src):
                    b = cb(f"{name}{X}", i)
                    dst = take(b)
                    for t in range(TT):
                        last = pe.transpose(dst[:, t * P:(t + 1) * P], src[:, t * P:(t + 1) * P], ident)
                    full(b, last)
                    b = cb(f"{name}s{X}", i)
                    full(b, pe.transpose(take(b)[0:NS, 0:P], src[:, NP_:T], ident))

                def scores(X):
                    for t in range(TT):
                        b = cb(f"S{t}{X}", i)
                        full(b, pe.matmul(take(b)[:, 0:(t + 1) * P], qT[:, X, t * P:(t + 1) * P],
                                          kT[:, X, 0:(t + 1) * P], start=True, stop=True))

                def attend(X):
                    bv = cb(f"v{X}", i)
                    pe.wait_ge(bank_free[bv.slot], bv.read)
                    def turned(t):
                        b = cb(f"P{t}{X}", i)
                        dst = take(b)
                        pe.wait_ge(prob_ready, 8 * i + 4 * X + t + 1)
                        for s in range(t + 1):
                            last = pe.transpose(dst[:, s * P:(s + 1) * P], prob[:, TRI[t] + s * P:TRI[t] + (s + 1) * P], ident)
                        full(b, last)

                    def values_of(t):
                        bp, b = cb(f"P{t}{X}", i), cb(f"O{t}{X}", i)
                        dst = take(b)
                        pe.wait_ge(bank_free[bp.slot], bp.read)
                        for s in range(t + 1):
                            last = pe.matmul(dst[:, 0:P], vN[:, X, s, :], probT[:, t % 2, s, :],
                                             start=(s == 0), stop=(s == t))
                        full(b, last)

                    turned(0)
                    turned(1)
                    values_of(0)
                    turned(2)
                    values_of(1)
                    turned(3)
                    values_of(2)
                    values_of(3)

                for j in range(8):
                    unit(TILE_C + j, 0, i, 8)
                    if j in (1, 2):
                        copied(TILE_C + j - 1, i, 8)
                        by_token("v", j - 1, raw[:, j - 1])
                    if j == 4:
                        pe.wait_ge(head_ready, 4 * i + 2)
                        by_token("k", 0, kT[:, 0])
                    if j == 5:
                        pe.wait_ge(head_ready, 4 * i + 3)
                        scores(0)
                    if j == 6:
                        pe.wait_ge(head_ready, 4 * i + 4)
                        by_token("k", 1, kT[:, 1])
                        attend(0)
                    if j == 7:
                        pe.wait_ge(head_ready, 4 * i + 5)
                        scores(1)
                    unit(TILE_C + j, 1, i, 8)
                attend(1)
            b = mb("mask")
            dst = take(b)
            pe.wait_ge(drop_ready, 1)
            for p in range(PAGES):
                pe.transpose(dst[:, p * NS:(p + 1) * NS], scoreS[:, p * P:(p + 1) * P], ident[0:NS, 0:NS])
            full(b, pe.transpose(dst[0:NS, PAGES * NS:(PAGES + 1) * NS], scoreS[:, PAST:L], ident[0:NS, 0:NS]))

            pe.wait_ge(c_done, 1)
            with pe.Fori(0, GROUPS) as g:
                def quarter(X, n):
                    unit(TILE_B + 2 * X + n // 4, n // 2 % 2, g, 4, quarters=(n % 2,))

                def key_pages(X, lo, hi):
                    st = b6(f"sT{X}", g)
                    if lo == 0:
                        take(st)
                    cols = ds((2 * g + X) * NT, NT)

                    def turned(n):
                        p, h = n // 2, n % 2
                        k = turn(8 * X + p, 2, g, 16)
                        if h == 0:
                            pe.wait_ge(k_in[k.slot], 16 * k.full)
                        b = bb(f"K{p}{h}{X}", g)
                        dst = take(b)
                        for e in range(4):
                            last = pe.transpose(dst[:, e * P:(e + 1) * P], kPage[:, k.slot, 4 * h + e, :], ident)
                        full(b, last)

                    def products(n):
                        p, h = n // 2, n % 2
                        b = bb(f"K{p}{h}{X}", g)
                        pe.wait_ge(bank_free[b.slot], b.read)
                        for e in range(4):
                            at = p * NS + (4 * h + e) * NT
                            last = pe.matmul(bank[6][:, at:at + NT], kPT[:, h, e, :], qS[:, 4 * h + e, cols],
                                             start=True, stop=True)
                        if h == 1:
                            last.then_inc(k_free[turn(8 * X + p, 2).slot], 1)

                    turned(2 * lo)
                    for n in range(2 * lo, 2 * hi):
                        if n + 1 < 2 * hi:
                            turned(n + 1)
                        products(n)
                    if hi == PAGES:
                        for h in range(H):
                            at = PAGES * NS + h * NT
                            last = pe.matmul(bank[6][0:NS, at:at + NT], kS[:, h, :], qS[:, h, cols], start=True, stop=True)
                        full(st, last)

                def scores_turned(X):
                    st = b6(f"sT{X}", g)
                    pe.wait_ge(bank_free[st.slot], st.read)
                    for half in range(2):
                        b = bb(f"S{half}{X}", g)
                        dst = take(b)
                        for p in range(4):
                            last = pe.transpose(dst[0:NS, p * P:(p + 1) * P], sT[:, 4 * half + p, :], ident)
                        full(b, last)
                    b = b6(f"sn{X}", g)
                    full(b, pe.transpose(bank[6][0:NS, 0:NS], sTn[:], ident[0:NS, 0:NS]))

                def probs_turned(X):
                    b = bb(f"Pt{X}", g)
                    dst = take(b)
                    pe.wait_ge(probS_ready, 2 * g + X + 1)
                    stand_alone(pe)
                    for p in range(PAGES):
                        pe.transpose(dst[:, p * NS:(p + 1) * NS], probS[:, p * P:(p + 1) * P], ident[0:NS, 0:NS])
                    full(b, pe.transpose(dst[0:NS, PAGES * NS:(PAGES + 1) * NS], probS[:, PAST:L], ident[0:NS, 0:NS]))

                def value_pages(X, lo, hi):
                    o = b7(f"o{X}", g)
                    if lo == 0:
                        take(o)
                        bp = bb(f"Pt{X}", g)
                        pe.wait_ge(bank_free[bp.slot], bp.read)
                    for p in range(lo, hi):
                        v = turn(8 * X + p, 4, g, 16)
                        pe.wait_ge(v_in[v.slot], 16 * v.full)
                        for h in range(H):
                            last = pe.matmul(bank[7][:, h * NT:(h + 1) * NT], vPage[:, v.slot, h, :],
                                             probST[:, p, h * NT:(h + 1) * NT], start=(p == 0 and h == 0),
                                             stop=False, skip_group_check=True)
                        last.then_inc(v_free[v.slot], 1)
                    if hi == PAGES:
                        for h in range(H):
                            last = pe.matmul(bank[7][:, h * NT:(h + 1) * NT], vS[:, h, :], probSTn[:, h * NT:(h + 1) * NT],
                                             start=False, stop=(h == H - 1), skip_group_check=True)
                        full(o, last)

                def history(t):
                    b = bb(f"h{t}", g)
                    dst = take(b)
                    pe.wait_ge(hist_in[t], 16 * g + 16)
                    full(b, pe.transpose(dst[:, 0:NB * HIST], hist[:, t, :], ident[0:NB * HIST, 0:NB * HIST]))

                def last_rows(t):
                    b = bb(f"u{t}", g)
                    dst = take(b)
                    copied(TILE_B + t, g, 4)
                    pe.transpose(dst[0:HIST, 0:P], U[:, t, NP_:NP_ + HIST], ident)
                    full(b, pe.transpose(dst[0:NS, P:2 * P], newU[:, t, :], ident))

                for X in range(2):
                    key_pages(X, 0, 2)
                    quarter(X, 0)
                    key_pages(X, 2, 4)
                    quarter(X, 1)
                    if X == 0:
                        history(0)
                    else:
                        last_rows(1)
                    key_pages(X, 4, 6)
                    quarter(X, 2)
                    if X == 0:
                        history(1)
                    key_pages(X, 6, 8)
                    quarter(X, 3)
                    scores_turned(X)
                    quarter(X, 4)
                    quarter(X, 5)
                    if X == 0:
                        last_rows(0)
                    probs_turned(X)
                    value_pages(X, 0, 4)
                    quarter(X, 6)
                    quarter(X, 7)
                    value_pages(X, 4, 8)
                pe.wait_ge(pooled_ready, 2 * g + 4)
                pe.wait_ge(wp_in, 16 * g + 16)
                for e in range(2):
                    for half in range(2):
                        b = bb(f"m{e}{half}", g)
                        dst = take(b)
                        for c in range(2):
                            last = pe.matmul(dst[:, 0:HT], wp[:, c, e * P:(e + 1) * P],
                                             pooled[:, c, half * HT:(half + 1) * HT], start=(c == 0), stop=(c == 1))
                        full(b, last)

            def rows(j, i):
                copied(TILE_D + j, i, 2)
                b = yb(f"yp{j}", i)
                dst = take(b)
                for t in range(TT):
                    last = pe.transpose(dst[:, t * P:(t + 1) * P], raw[:, j, t * P:(t + 1) * P], ident)
                full(b, last)
                b = yb(f"ys{j}", i)
                full(b, pe.transpose(take(b)[0:NS, 0:P], raw[:, j, NP_:T], ident))

            for half in range(2):
                unit(TILE_D, half, chunk_ready=mix_low)
            with pe.Fori(0, 7) as i:
                for j in range(2):
                    unit(TILE_D + j + 1, 0, i, 2)
                    rows(j, i)
                    unit(TILE_D + j + 1, 1, i, 2)
            unit(TILE_D + KC - 1, 0)
            rows(0, 7)
            unit(TILE_D + KC - 1, 1)
            rows(1, 7)

        @block.vector
        def _(dve):
            own = Steps(dve, dve_steps)

            n = 0
            for t in range(TT + 1):
                m = P if t < TT else NS
                for q in range(4):
                    n += 1
                    b = xb(f"x{t}{q}")
                    dve.wait_ge(x_high, n)
                    at = (slice(None), slice(4 * q, 4 * q + 4), slice(t * P, t * P + m))
                    dve.tensor_tensor(actL[at], bank[b.slot][:, 0:4 * m].rearrange("p (k t) -> p k t", k=4),
                                      actH[at].bitcast(F32), ALU.subtract).then_inc(bank_free[b.slot], 1)

            def rotate(dst, src, rows, table, swap):
                half = rot[0:rows, :]
                stand_alone(dve)
                own.step(dve.stream_shuffle(half, src, swap))
                own.wait()
                own.step(dve.tensor_tensor(half, half, table[0:rows, 1, :], ALU.mult))
                own.step(dve.tensor_tensor(src, src, table[0:rows, 0, :], ALU.mult))
                own.wait()
                return dve.tensor_tensor(dst, src, half, ALU.add)

            def copied(tile, i=None, per=0):
                t = turn(tile, 2, i, per)
                dve.wait_ge(acc_copied[t.slot], t.read)

            copied(0)
            dve.wait_ge(irot_in, 16)
            rotate(kiT[0:ID, :], kiT[0:ID, :], ID, irot, SWAP_I).then_inc(ki_ready, 1)
            own.step(dve.memset(qiS[:], 0.0))
            dve.wait_ge(ki_ready, 1)
            with dve.Fori(0, 4) as i:
                own.enter(i, 6)
                for j in range(2):
                    copied(TILE_A + j, i, 2)
                    dve.wait_ge(qi_ready, 2 * i + j + 2)
                    rotate(qiT[:, ds(2 * i + j, 1), :].rearrange("p a t -> p (a t)"), raw[:, j], P, irot, SWAP_I
                           ).then_inc(qi_ready, 1)
                own.leave(4)
            dve.wait_ge(qi_ready, H + 2)
            own.wait()
            own.step(dve.tensor_copy(qiS[0:ID, 0, 0:IH:2, :], qiT[0:ID, :, NP_:T]))
            dve.tensor_copy(qiS[ID:P, 1, 1:IH:2, :], qiT[ID:P, :, NP_:T]).then_inc(qis_near, 1)
            b = ab("wi")
            dve.tensor_copy(wiN[:].rearrange("p t h -> p (t h)"), bank_wait(dve, b)[:, 0:3 * IH]
                            ).then_inc(bank_free[b.slot], 1)
            dve.wait_ge(bank_free[b.slot], b.read)
            n = 0
            for t in (3, 2, 1):
                sc = scoreP[:, TRI[t] - P:TRI[t + 1] - P]
                for h in range(IH):
                    r, b = turn(n, 2), ab(f"r{t}_{h}")
                    dve.wait_ge(relu_full[r.slot], r.full)
                    src, w = relu[:, r.slot, 0:(t + 1) * P], wiN[:, t - 1, h:h + 1]
                    if h == 0:
                        dve.tensor_scalar(sc, src, w, None, ALU.mult).then_inc(bank_free[b.slot], 1)
                    else:
                        dve.wait_ge(bank_free[before.slot], before.read)
                        dve.scalar_tensor_tensor(sc, src, w, sc, ALU.mult, ALU.add).then_inc(bank_free[b.slot], 1)
                    n, before = n + 1, b
                dve.wait_ge(bank_free[b.slot], b.read)
                own.step(dve.tensor_tensor(sc[:, t * P:], sc[:, t * P:], causal, ALU.add))
            dve.wait_ge(wi_back, 16)
            with dve.Fori(0, 4) as i:
                own.enter(i, 2)
                for j in range(2):
                    r, b = turn(3 * IH + j, 2, i, 2), sbk(f"R{j}", i)
                    dve.wait_ge(relu_full[r.slot], r.full)
                    cols = ds((2 * i + j) * NT, NT)
                    v = relu[:, r.slot, :].rearrange("p (g h t) -> p g h t", g=PAGES, h=IH)
                    own.step(dve.tensor_tensor(v, v, wiB[:, :, cols].unsqueeze(1).to_broadcast([P, PAGES, IH, NT]),
                                               ALU.mult))
                    own.wait()
                    dve.tensor_reduce(scoreST[:, :, cols], v.rearrange("p g h t -> p g t h"), AX.X, ALU.add
                                      ).then_inc(bank_free[b.slot], 1)
                own.leave(4)
            r = turn(3 * IH + NB, 2)
            dve.wait_ge(relu_full[r.slot], r.full)
            v = relu[0:NS, r.slot, :].rearrange("p (h t) -> p h t", h=IH)
            own.step(dve.tensor_tensor(v, v, wiB[0:NS], ALU.mult))
            own.wait()
            b = nb("Rn")
            dve.tensor_reduce(scoreSTn[:], v.rearrange("p h t -> p t h"), AX.X, ALU.add).then_inc(bank_free[b.slot], 1)
            for half in range(2):
                b = nb(f"S{half}")
                dve.tensor_copy(scoreS[:, 512 * half:512 * (half + 1)], bank_wait(dve, b)[0:NS, :]
                                ).then_inc(bank_free[b.slot], 1)
            b = nb("Sn")
            dve.tensor_tensor(scoreS[:, PAST:L], bank_wait(dve, b)[0:NS, 0:NS], newmask, ALU.add
                              ).then_inc(bank_free[b.slot], 1)
            dve.wait_ge(bank_free[b.slot], b.read)

            def pick(scores, top):
                own.wait()
                stand_alone(dve)
                own.step(dve.max(top, scores))
                own.wait()
                stand_alone(dve)
                own.step(dve.match_replace(scores, top, scores, PICKED))

            for t in (1, 2, 3):
                sc = scoreP[:, TRI[t] - P:TRI[t + 1] - P]
                with dve.Fori(0, TOPK_P // ROUND) as i:
                    own.enter(i, 2)
                    pick(sc, top8[:])
                    own.leave(TOPK_P // ROUND)
                own.wait()
                own.step(dve.tensor_scalar(keepP[:, TRI[t]:TRI[t + 1]], sc, PICKED / 1.5, MASKED, ALU.is_gt, ALU.mult))
            own.step(dve.tensor_copy(keepP[:, 0:P], causal))
            dve.wait_ge(consts_in, 32)
            own.step(dve.tensor_scalar(halfscale[:], halfscale[:], 0.5, None, ALU.mult))

            rounds = TOPK_S // ROUND // 4
            with dve.Fori(0, 4) as i:
                own.enter(i, 2 * rounds + 4 * 3 + 8)

                def make_gate(X):
                    dve.scalar_tensor_tensor(gate[:, X, :], tanhC[:], 1.0, raw[:, X, :], ALU.add, ALU.mult
                                             ).then_inc(gate_ready, 1)

                def softmax(X):
                    for t in range(TT):
                        b = cb(f"S{t}{X}", i)
                        src = bank_wait(dve, b)
                        stand_alone(dve)
                        dve.tensor_tensor_reduce(prob[:, TRI[t]:TRI[t + 1]], src[:, 0:(t + 1) * P],
                                                 keepP[:, TRI[t]:TRI[t + 1]], -SCALE, 3e38, ALU.add, ALU.min,
                                                 stat[:, t:t + 1]).then_inc(bank_free[b.slot], 1)
                    for t in range(TT):
                        dve.wait_ge(exp_ready, 8 * i + 4 * X + t + 1)
                        own.step(dve.reciprocal(stat[:, 16 + t:17 + t], stat[:, 8 + t:9 + t]))
                        own.wait()
                        pr = prob[:, TRI[t]:TRI[t + 1]]
                        dve.tensor_scalar(pr, pr, stat[:, 16 + t:17 + t], None, ALU.mult).then_inc(prob_ready, 1)

                def gated(X):
                    for t in range(TT):
                        b = cb(f"O{t}{X}", i)
                        cols = slice(t * P, (t + 1) * P)
                        dve.scalar_tensor_tensor(mixed[:, ds(2 * i + X, 1), cols].rearrange("p a t -> p (a t)"),
                                                 bank_wait(dve, b)[:, 0:P], 0.5, gate[:, X, cols],
                                                 ALU.mult, ALU.mult).then_inc(bank_free[b.slot], 1)

                def rotated(j, dst, X):
                    copied(TILE_C + j, i, 8)
                    dve.wait_ge(head_ready, 4 * i + j - 2)
                    rotate(dst[0:32, X, :], dst[0:32, X, :], 32, headrot, SWAP_H).then_inc(head_ready, 1)

                for _ in range(rounds):
                    pick(scoreS[:], top8[0:NS, :])
                copied(TILE_C + 2, i, 8)
                make_gate(0)
                rotated(3, kT, 0)
                rotated(4, qT, 0)
                softmax(0)
                rotated(5, kT, 1)
                dve.wait_ge(gate_ready, 2 * i + 1)
                gated(0)
                rotated(6, qT, 1)
                softmax(1)
                copied(TILE_C + 7, i, 8)
                make_gate(1)
                dve.wait_ge(gate_ready, 2 * i + 2)
                gated(1)
                own.leave(4)
            own.wait()
            dve.tensor_scalar(scoreS[:], scoreS[:], PICKED / 1.5, MASKED, ALU.is_gt, ALU.mult).then_inc(drop_ready, 1)
            b = mb("mask")
            src = bank_wait(dve, b)
            own.step(dve.tensor_copy(maskT[:].rearrange("p a t -> p (a t)"), src[:, 0:PAGES * NS]))
            dve.tensor_copy(maskTn[:], src[0:NS, PAGES * NS:(PAGES + 1) * NS]).then_inc(bank_free[b.slot], 1)

            dve.wait_ge(c_done, 1)
            own.step(dve.memset(U[:, :, 0:HIST], 0.0))
            dve.wait_ge(wtab_in, 16)
            own.wait()
            with dve.Fori(0, GROUPS) as g:
                own.enter(g, 2 * 12 + 2)

                def key_halves(X, lo, hi):
                    for p in range(lo, hi):
                        b = bb(f"K{p}1{X}", g)
                        dve.tensor_copy(kPT[:, 1, :, :].rearrange("p h k -> p (h k)"), bank_wait(dve, b)[:]
                                        ).then_inc(bank_free[b.slot], 1)

                def masked(X):
                    b = b6(f"sT{X}", g)
                    src = bank_wait(dve, b)
                    cols = ds((2 * g + X) * NT, NT)
                    own.step(dve.tensor_tensor(sT[:].rearrange("p a (h t) -> p a h t", h=H),
                                               src[:, 0:PAGES * NS].rearrange("p (a h t) -> p a h t", a=PAGES, h=H),
                                               maskT[:, :, cols].unsqueeze(2).to_broadcast([P, PAGES, H, NT]), ALU.add))
                    dve.tensor_tensor(sTn[:].rearrange("p (h t) -> p h t", h=H),
                                      src[0:NS, PAGES * NS:(PAGES + 1) * NS].rearrange("p (h t) -> p h t", h=H),
                                      maskTn[:, cols].unsqueeze(1).to_broadcast([NS, H, NT]), ALU.add
                                      ).then_inc(bank_free[b.slot], 1)

                def softmax(X):
                    for n, (b, w) in enumerate(((bb(f"S0{X}", g), 512), (bb(f"S1{X}", g), 512), (b6(f"sn{X}", g), NS))):
                        own.step(dve.tensor_reduce(stat[0:NS, 16 + n:17 + n], bank_wait(dve, b)[0:NS, 0:w], AX.X, ALU.max))
                    own.wait()
                    own.step(dve.tensor_reduce(stat[0:NS, 19:20], stat[0:NS, 16:19], AX.X, ALU.max))
                    own.wait()
                    dve.tensor_scalar(stat[0:NS, 20:21], stat[0:NS, 19:20], -SCALE, None, ALU.mult).then_inc(max_ready, 1)
                    b = b6(f"sn{X}", g)
                    dve.wait_ge(bank_free[b.slot], b.read)
                    own.step(dve.tensor_reduce(stat[0:NS, 24:25], stat[0:NS, 21:24], AX.X, ALU.add))
                    own.wait()
                    own.step(dve.reciprocal(stat[0:NS, 25:26], stat[0:NS, 24:25]))
                    own.wait()
                    dve.tensor_scalar(probS[:], probS[:], stat[0:NS, 25:26], None, ALU.mult).then_inc(probS_ready, 1)

                def pool_inputs(t):
                    copied(TILE_B + t, g, 4)
                    u, src = U[:, t, :], U[:, t, :]
                    for lv in range(4):
                        lo, w = (2 << lv) - 1, 1 << lv
                        dst = win[:, lv % 2, :]
                        own.step(dve.scalar_tensor_tensor(dst[:, lo:UW], src[:, lo - w:UW - w], wtab[:, ds(g * WT + lv, 1)],
                                                          src[:, lo:UW], ALU.mult, ALU.add))
                        own.wait()
                        src = dst
                    inv = wtab[:, ds(g * WT + 4, 1)]
                    samples = lambda ap: ap[:, HIST + NP_:UW].rearrange("p (b r) -> p b r", b=NB)[:, :, HIST:UE]
                    own.step(dve.scalar_tensor_tensor(pooled[:, t, 0:NP_], src[:, HIST:HIST + NP_], inv,
                                                      u[:, HIST:HIST + NP_], ALU.mult, ALU.subtract))
                    dve.scalar_tensor_tensor(pooled[:, t, NP_:T].rearrange("p (b r) -> p b r", b=NB),
                                             samples(src), inv, samples(u), ALU.mult, ALU.subtract)
                    first = win[:, 0, HIST:2 * HIST]
                    own.step(dve.tensor_tensor(first, src[:, HIST:2 * HIST], wtab[:, ds(g * WT + 5, HIST)], ALU.mult))
                    own.wait()
                    dve.tensor_tensor(pooled[:, t, 0:HIST], first, u[:, HIST:2 * HIST], ALU.subtract
                                      ).then_inc(pooled_ready, 1)

                def make_gate(t):
                    copied(TILE_B + 2 + t, g, 4)
                    dve.scalar_tensor_tensor(raw[:, t, :], rot[:], 1.0, raw[:, t, :], ALU.add, ALU.mult
                                             ).then_inc(gate_ready, 1)

                for X in range(2):
                    key_halves(X, 0, 8)
                    masked(X)
                    softmax(X)
                    pool_inputs(X)
                    if X == 1:
                        make_gate(0)
                    b = b7(f"o{X}", g)
                    dve.scalar_tensor_tensor(mixed[:, 0:H, ds(NP_ + (2 * g + X) * NT, NT)],
                                             bank_wait(dve, b)[:, 0:NS].rearrange("p (h t) -> p h t", h=H), 0.5,
                                             gateS[:, :, ds((2 * g + X) * NT, NT)], ALU.mult, ALU.mult
                                             ).then_inc(bank_free[b.slot], 1)
                make_gate(1)
                dve.wait_ge(gate_ready, 2 * g + H + 2)
                for e in range(2):
                    for half in range(2):
                        b = bb(f"m{e}{half}", g)
                        cols = slice(half * HT, (half + 1) * HT)
                        dve.scalar_tensor_tensor(mixed[:, ds(H + 2 * g + e, 1), cols].rearrange("p a t -> p (a t)"),
                                                 bank_wait(dve, b)[:, 0:HT], halfscale[:, ds(2 * g + e, 1)],
                                                 raw[:, e, cols], ALU.mult, ALU.mult).then_inc(bank_free[b.slot], 1)
                own.leave(GROUPS)

            for k in range(KC):
                dve.wait_ge(mix_high, k + 1)
                dve.tensor_tensor(actL[:, k, :], mixed[:, k, :], actH[:, k, :].bitcast(F32), ALU.subtract
                                  ).then_inc(mix_low, 1)
            dve.wait_ge(y_in, 16 * (TT + 1))

            def residual(d, j, i):
                b = yb(f"yp{j}", i)
                at = y[:, 0:TT, ds(d * P, P)]
                dve.scalar_tensor_tensor(at, at, ALPHA, bank_wait(dve, b)[:].rearrange("p (t c) -> p t c", t=TT),
                                         ALU.mult, ALU.add).then_inc(bank_free[b.slot], 1)
                b = yb(f"ys{j}", i)
                at = y[0:NS, TT, ds(d * P, P)]
                dve.scalar_tensor_tensor(at, at, ALPHA, bank_wait(dve, b)[0:NS, 0:P], ALU.mult, ALU.add
                                         ).then_inc(bank_free[b.slot], 1)
                dve.wait_ge(bank_free[b.slot], b.read)

            with dve.Fori(0, 4) as i:
                own.enter(i, TT + 1)
                for n in range(4):
                    residual(4 * i + n, n % 2, 2 * i + n // 2)
                for t in range(TT + 1):
                    m = P if t < TT else NS
                    own.step(dve.bn_stats(bn[0:m, t, ds(i, 1), :].rearrange("p a s -> p (a s)"), y[0:m, t, ds(512 * i, 512)]))
                own.leave(4)
            own.wait()
            own.step(dve.memset(mv[:], 1.0))
            own.wait()
            for t in range(TT + 1):
                m = P if t < TT else NS
                own.step(dve.bn_aggr(mv[0:m, t, :], bn[0:m, t, :, :].rearrange("p a s -> p (a s)")))
            own.wait()
            dve.tensor_scalar(mv[:, :, 1], mv[:, :, 1], EPS, None, ALU.add).then_inc(var_ready, 1)
            dve.wait_ge(std_ready, 1)
            own.step(dve.reciprocal(stat[:, 0:5], std[:]))
            own.wait()
            dve.scalar_tensor_tensor(stat[:, 8:13], mv[:, :, 0], -1.0, stat[:, 0:5], ALU.mult, ALU.mult
                                     ).then_inc(var_ready, 1)
            dve.wait_ge(ln_in, 32)
            for t in range(TT + 1):
                m = P if t < TT else NS
                dve.wait_ge(norm_ready, t + 1)
                own.step(dve.tensor_tensor(y[0:m, t, :], y[0:m, t, :], gbc[0:m], ALU.mult))
                own.wait()
                dve.tensor_tensor(y[0:m, t, :], y[0:m, t, :], bbc[0:m], ALU.add).then_inc(y_ready, 1)


def rotation(dim, rotated, rows):
    import numpy as np
    half = rotated // 2
    pos = np.concatenate([np.arange(NP_), PAST + np.tile(np.arange(NT), NB)]).astype(np.float32)
    freqs = np.float32(500000.0) ** (-np.arange(half, dtype=np.float32) * np.float32(2.0 / rotated))
    ang = pos[None, :] * freqs.astype(np.float32)[:, None]
    table = np.zeros((rows, 2, T), np.float32)
    table[:, 0, :] = 1.0
    for start in range(0, rows, dim):
        for a in range(2):
            table[start + a * half:start + (a + 1) * half, 0, :] = np.cos(ang)
            table[start + a * half:start + (a + 1) * half, 1, :] = np.sin(ang) * (2 * a - 1)
    return table


def squares():
    import numpy as np
    out = np.zeros((P, 288), np.float32)
    out[:, 0:P] = np.eye(P)
    r = np.arange(P)
    out[:, P:2 * P] = np.where(r[None, :] <= r[:, None], 0.0, MASKED)
    n = np.arange(NS)
    seen = (n[None, :] // NT == n[:, None] // NT) & (n[None, :] % NT <= n[:, None] % NT)
    out[0:NS, 256:288] = np.where(seen, 0.0, MASKED)
    return out


def window_table():
    import numpy as np
    out = np.zeros((P, GROUPS * WT), np.float32)
    for g, w in enumerate(WINDOWS):
        row = [float(w > (1 << lv)) for lv in range(4)] + [1.0 / w] + [1.0 / min(t + 1, w) for t in range(HIST)]
        out[:, g * WT:(g + 1) * WT] = np.array(row, np.float32)
    return out


_INS = ["x_prompt", "x_sample", "cache_k", "cache_v", "cache_kidx", "state_pool", "page_table", "w_in", "w_pool",
        "pool_scale", "w_out", "ln_g", "ln_b"]
_OUTS = [("y_prompt", (1, NP_, D)), ("y_sample", (NB, NT, D)), ("p_k", (1, 1, NP_, H, P)), ("p_v", (1, 1, NP_, H, P)),
         ("p_kidx", (1, 1, NP_, ID)), ("p_pool", (1, 1, HIST, H * P)), ("s_k", (1, NB, NT, H, P)),
         ("s_v", (1, NB, NT, H, P)), ("s_kidx", (1, NB, NT, ID)), ("s_pool", (1, NB, HIST, H * P))]


def kernel(**inputs):
    import numpy as _np
    import concourse.bacc as _bacc
    from concourse.bass_utils import run_bass_kernel_spmd as _run

    nc = _bacc.Bacc("TRN2", target_bir_lowering=False, num_devices=1, dynamic_dma_scratch_size=1024)
    arrays = {f"in_{name}": _np.ascontiguousarray(inputs[name]) for name in _INS}
    arrays["const_square"] = squares()
    arrays["const_idx_rot"] = rotation(ID, 16, P)
    arrays["const_head_rot"] = rotation(P, 32, 32)
    arrays["const_windows"] = window_table()
    args = [nc.dram_tensor(name, a.shape, mybir.dt.from_np(a.dtype), kind="ExternalInput").ap()
            for name, a in arrays.items()]
    args += [nc.dram_tensor(f"out_{name}", shape, F32, kind="ExternalOutput").ap() for name, shape in _OUTS]
    layer_program(nc, *args)
    r = _run(nc, [arrays], core_ids=[0])
    return tuple(r.results[0][f"out_{name}"] for name, _ in _OUTS)
```

```python
from contextlib import ExitStack

import concourse.bass as bass
from concourse import mybir

ALU = mybir.AluOpType
ACT = mybir.ActivationFunctionType
AX = mybir.AxisListType
F32 = mybir.dt.float32
F32R = mybir.dt.float32r
BF16 = mybir.dt.bfloat16
I32 = mybir.dt.int32

P = 128
D = 2048
KC = D // P
NP_ = 512
NB = 8
NT = 4
NS = NB * NT
T = NP_ + NS
HT = T // 2
TT = NP_ // P
H = 8
IH = 16
ID = 64
PAGES = 8
PAST = PAGES * P
L = PAST + NS
TOPK_P = 128
TOPK_S = 256
ROUND = 8
GROUPS = 4
WINDOWS = (2, 4, 8, 16)
HIST = 15
UE = HIST + NT
UW = HIST + NP_ + NB * UE
SCALE = 128.0 ** -0.5
ISCALE = 1.0 / 32.0
ALPHA = 2.0 ** 0.25
EPS = 1e-5
MASKED = -1e30
PICKED = -3e38
Q0, K0, V0, GA0, QI0, KI0, U0, GB0 = 0, 1024, 2048, 3072, 4096, 5120, 5200, 6224
KW = 80
HU = KC // 2
TRI = [0, 128, 384, 768, 1280]

TILE_A, TILE_C, TILE_B, TILE_D = 1, 9, 41, 57
SWAP_I = [*range(8, 16), *range(8), *range(16, 32)]
SWAP_H = [*range(16, 32), *range(16)]
WT = 20


class Turn:

    def __init__(self, slot, before):
        self.slot, self.full, self.free, self.read = slot, before + 1, before + 1, before + 2


def turn(n, slots, i=None, per=0):
    assert per % slots == 0
    return Turn(n % slots, n // slots if i is None else i * (per // slots) + n // slots)


class Banks:

    def __init__(self, banks):
        self.used = dict.fromkeys(banks, 0)

    def stage(self, names, banks, times=1):
        assert times == 1 or len(names) % len(banks) == 0, len(names)
        step = len(names) // len(banks)
        table = {name: (banks[k % len(banks)], self.used[banks[k % len(banks)]] + k // len(banks))
                 for k, name in enumerate(names)}
        assert len(table) == len(names)
        for k in range(len(names)):
            self.used[banks[k % len(banks)]] += times if times == 1 else 0
        for b in banks if times > 1 else ():
            self.used[b] += times * step

        def at(name, i=None, ago=0):
            b, n = table[name]
            return Turn(b, n if i is None else i * step + (n - ago * step))

        return at


class Steps:

    def __init__(self, eng, sem):
        self.eng, self.sem, self.done, self.i, self.per = eng, sem, 0, None, 0

    def value(self):
        return self.done if self.i is None else self.i * self.per + self.done

    def step(self, ins):
        ins.then_inc(self.sem, 1)
        self.done += 1

    def wait(self):
        self.eng.wait_ge(self.sem, self.value())

    def enter(self, i, per):
        self.i, self.per, self.start = i, per, self.done

    def leave(self, times):
        assert self.done - self.start == self.per, (self.done - self.start, self.per)
        self.done, self.i = self.start + times * self.per, None


def layer_program(nc, x_prompt, x_sample, cache_k, cache_v, cache_kidx, state_pool, page_table,
                  w_in, w_pool, pool_scale, w_out, ln_g, ln_b, square, idx_rot, head_rot, windows,
                  y_prompt, y_sample, p_k, p_v, p_kidx, p_pool, s_k, s_v, s_kidx, s_pool):
    ds = bass.ds
    ctx = ExitStack()
    with ctx:
        def sem(name):
            return ctx.enter_context(nc.semaphore(name))

        def sems(name, n):
            return [sem(f"{name}{j}") for j in range(n)]

        def sb(name, shape, dt=F32, where=ctx):
            return where.enter_context(nc.sbuf_tensor(name, shape, dt))

        actH = sb("actH", [P, KC, T], F32R)
        actL = sb("actL", [P, KC, T], F32R)
        rawW = sb("rawW", [P, 4, HU, P])
        wH = sb("wH", [P, 4, HU, P], F32R)
        wL = sb("wL", [P, 4, HU, P], F32R)
        mixed = sb("mixed", [P, KC, T])
        raw = sb("raw", [P, 2, T])
        rot = sb("rot", [P, T])
        qS = sb("qS", [P, H, NS])
        kS = sb("kS", [P, H, NS])
        vS = sb("vS", [NS, H, P])
        gateS = sb("gateS", [P, H, NS])
        sq = sb("sq", [P, 288])
        ident, causal, newmask = sq[:, 0:P], sq[:, P:2 * P], sq[0:NS, 256:288]
        pageT = sb("pageT", [1, NB * PAGES], I32)
        halfscale = sb("halfscale", [P, H])
        stat = sb("stat", [P, 32])
        outer = ExitStack()
        scoreS = sb("scoreS", [NS, L], F32, outer)
        scoreP = sb("scoreP", [P, TRI[4] - P], F32, outer)
        keepP = sb("keepP", [P, TRI[4]], BF16, outer)
        headrot = sb("headrot", [32, 2, T], F32, outer)
        wiN = sb("wiN", [P, 3, IH], F32, outer)
        top8 = sb("top8", [P, 8], F32, outer)
        with ExitStack() as s:
            xnat = sb("xnat", [P, 2, D], F32, s)
            xnatS = sb("xnatS", [NS, D], F32, s)
        with ExitStack() as s:
            kiT = sb("kiT", [P, T], F32, s)
            wiT = sb("wiT", [P, T], F32, s)
            irot = sb("irot", [P, 2, T], F32, s)
            wiB = sb("wiB", [P, IH, NS], F32, s)
            relu = sb("relu", [P, 2, 512], F32, s)
            kiPage = sb("kiPage", [P, 2, PAGES, ID], F32, s)
            kiPT = sb("kiPT", [P, 2, 4, P], F32, s)
            scoreST = sb("scoreST", [P, PAGES, NS], F32, s)
            scoreSTn = sb("scoreSTn", [NS, NS], F32, s)
            qiS = sb("qiS", [P, 2, IH, NS], F32, s)
            kiN = sb("kiN", [P, 5, ID], F32, s)
        with ExitStack() as s:
            qT = sb("qT", [P, 2, T], F32, s)
            kT = sb("kT", [P, 2, T], F32, s)
            vN = sb("vN", [P, 2, TT, P], F32, s)
            kN = sb("kN", [P, 5, P], F32, s)
            gate = sb("gate", [P, 2, T], F32, s)
            tanhC = sb("tanhC", [P, T], F32, s)
            prob = sb("prob", [P, TRI[4]], F32, s)
            probT = sb("probT", [P, 2, TT, P], F32, s)
        outer.close()
        with ExitStack() as s:
            kPage = sb("kPage", [P, 4, H, P], F32, s)
            vPage = sb("vPage", [P, 4, H, P], F32, s)
            kPT = sb("kPT", [P, 2, 2, 2 * P], F32, s)
            qPad = sb("qPad", [P, 2, H * (NS + NT)], F32, s)
            probS = sb("probS", [NS, L], F32, s)
            probST = sb("probST", [P, PAGES, NS], F32, s)
            probSTn = sb("probSTn", [NS, NS], F32, s)
            U = sb("U", [P, 2, UW], F32, s)
            win = sb("win", [P, 2, UW], F32, s)
            pooledS = sb("pooledS", [P, 2, NS], F32, s)
            wp = sb("wp", [P, 2, 256], F32, s)
            hist = sb("hist", [NB * HIST, 2, P], F32, s)
            uN = hist[0:NS]
            newU = sb("newU", [P, 2, NS], F32, s)
            wtab = sb("wtab", [P, GROUPS * WT], F32, s)
            outS = probS[0:NT, 0:H * P].rearrange("p (h d) -> p h d", h=H)
        with ExitStack() as s:
            y = sb("y", [P, 5, D], F32, s)
            bn = sb("bn", [P, 5, 4, 6], F32, s)
            mv = sb("mv", [P, 5, 2], F32, s)
            std = sb("std", [P, 5], F32, s)
        flat = mixed[:].rearrange("p k t -> p (k t)")
        gbc, bbc = flat[:, 0:D], flat[:, D:2 * D]
        qiT = mixed[:, 0:H, :]

        acc = [ctx.enter_context(nc.psum_tensor(f"acc{j}", [P, 2, 512], F32)) for j in range(2)]
        four = (4, 5, 6, 7)
        bank = {j: ctx.enter_context(nc.psum_tensor(f"bank{j}", [P, 512], F32)) for j in four}
        dropD = nc.dram_tensor("dropD", [NS, L], F32, kind="Internal").ap()
        wiD = nc.dram_tensor("wiD", [IH, NS], F32, kind="Internal").ap()

        w_landed = sems("w_landed", 4)
        high_ready = sems("high_ready", 4)
        stage_ready = sems("stage_ready", 4)
        stage_free = sems("stage_free", 2)
        tile_ready = sems("tile_ready", 2)
        acc_copied = sems("acc_copied", 2)
        bank_full = {j: sem(f"bank_full{j}") for j in four}
        bank_free = {j: sem(f"bank_free{j}") for j in four}
        apart = sem("apart")
        square_in = sem("square_in")
        consts_in = sem("consts_in")
        irot_in = sem("irot_in")
        pages_in = sem("pages_in")
        x_in = sems("x_in", 2)
        xs_in = sem("xs_in")
        x_high = sem("x_high")
        ki_ready = sem("ki_ready")
        ki_twice = sem("ki_twice")
        wi_out = sem("wi_out")
        wi_back = sem("wi_back")
        qi_ready = sem("qi_ready")
        qis_near = sem("qis_near")
        qis_far = sem("qis_far")
        relu_full = sems("relu_full", 2)
        kip_in = sems("kip_in", 2)
        drop_ready = sem("drop_ready")
        head_ready = sem("head_ready")
        gate_ready = sem("gate_ready")
        exp_ready = sem("exp_ready")
        prob_ready = sem("prob_ready")
        dve_steps = sem("dve_steps")
        kn_sent = sem("kn_sent")
        vn_sent = sems("vn_sent", 2)
        c_done = sem("c_done")
        drop_out = sem("drop_out")
        mask_in = sems("mask_in", 2)
        pad_ready = sem("pad_ready")
        k_in = sems("k_in", 2)
        k_free = sems("k_free", 2)
        v_in = sems("v_in", 4)
        v_free = sems("v_free", 4)
        max_ready = sem("max_ready")
        exps_ready = sem("exps_ready")
        probS_ready = sem("probS_ready")
        hist_in = sems("hist_in", 2)
        wtab_in = sem("wtab_in")
        wp_in = sem("wp_in")
        pooled_ready = sem("pooled_ready")
        un_sent = sem("un_sent")
        mix_high = sem("mix_high")
        mix_low = sem("mix_low")
        y_in = sem("y_in")
        ln_in = sem("ln_in")
        var_ready = sem("var_ready")
        std_ready = sem("std_ready")
        norm_ready = sem("norm_ready")
        y_ready = sem("y_ready")
        kidx_sent = sem("kidx_sent")
        spool_sent = sem("spool_sent")
        y_sent = sem("y_sent")

        banks = Banks(four)
        xb = banks.stage([f"x{t}{q}" for t in range(TT + 1) for q in range(4)], four)
        ab = banks.stage(["wi", "ki", "kis", *(f"r{t}_{h}" for t in (3, 2, 1) for h in range(IH))], four)
        sbk = banks.stage([f"{w}{j}" for j in range(2) for w in ("T", "R")], four, 4)
        nb = banks.stage(["Rn", "S0", "S1", "Sn"], four)

        def c_uses(X):
            return [f"{u}{X}" for u in ("P0", "P1", "O0", "P2", "O1", "P3", "O2", "O3")]

        cb = banks.stage(["v0", "vs0", "v1", "vs1", "k0", "ks0", "S00", "S10", "S20", "S30", "k1", "ks1",
                          *c_uses(0), "S01", "S11", "S21", "S31", *c_uses(1)], four, 4)

        def key_uses(X, lo, hi):
            return [f"K{n}{X}" for n in range(lo, hi)]

        bb = banks.stage([*key_uses("a", 0, 8), "h0", *key_uses("a", 8, 12), "h1", *key_uses("a", 12, 16), "Sna", "u0",
                          "Pta", "OTa", *key_uses("b", 0, 8), "u1", *key_uses("b", 8, 16), "Snb", "Ptb", "OTb",
                          "m0p", "m0s", "m1p", "m1s"], (4, 5), GROUPS)
        b67 = banks.stage([f"{w}{half}{X}" for X in "ab" for w in "SO" for half in range(2)], (6, 7), GROUPS)
        yb = banks.stage(["yp0", "ys0", "yp1", "ys1"], four, 8)

        def bank_wait(eng, b):
            eng.wait_ge(bank_full[b.slot], b.full)
            return bank[b.slot]

        def stand_alone(eng):
            eng.sem_inc(apart, 1)

        block = ctx.enter_context(nc.Block())

        w_view = w_in[0].rearrange("(k p) c -> p k c", p=P)
        wo_view = w_out[0].rearrange("(k p) c -> p k c", p=P)

        @block.sync
        def _(sp):
            def load_unit(view, half, col, t, width=P):
                if not (isinstance(t.free, int) and t.free == 1):
                    sp.wait_ge(stage_ready[t.slot], t.free - 1)
                    stand_alone(sp)
                sp.dma_start(rawW[:, t.slot, :, 0:width],
                             view[:, half * HU:(half + 1) * HU, ds(col, width)]).then_inc(w_landed[t.slot], 16)

            def load_tile(view, col, tile, i=None, per=0):
                for half in range(2):
                    load_unit(view, half, col, turn(2 * tile + half, 4, i, 2 * per))

            for half in range(2):
                load_unit(w_view, half, KI0, turn(half, 4), KW)
            sp.dma_start(pageT[:], page_table.rearrange("(a b) c -> a (b c)", a=1)).then_inc(pages_in, 16)
            sp.dma_start(s_pool[0, :, 0:HIST - NT, :], state_pool[0, :, NT:HIST, :]).then_inc(spool_sent, 16)
            sp.wait_ge(pages_in, 16)

            def load_page(cache, dst, index, done):
                stand_alone(sp)
                page = sp.value_load(pageT[0:1, ds(index, 1)], min_val=0, max_val=cache.shape[0] - 1)
                sp.dma_start(dst, cache[ds(page, 1)].rearrange("a p n -> p (a n)")).then_inc(done, 16)

            with sp.Fori(0, 4) as i:
                for j in range(2):
                    load_tile(w_view, QI0 + (2 * i + j) * P, TILE_A + j, i, 2)
            for j in range(2):
                load_tile(w_view, V0 + j * P, TILE_C + j)
            for q in range(4):
                b = xb(f"x{TT}{q}")
                sp.wait_ge(bank_free[b.slot], b.read)
            def index_pages(n, j):
                for p in range(PAGES):
                    load_page(cache_kidx[0], kiPage[:, j, p, :], n * PAGES + p, kip_in[j])

            for j in range(2):
                index_pages(j, j)
            with sp.Fori(0, 3) as i:
                for j in range(2):
                    b = sbk(f"T{j}", i)
                    sp.wait_ge(bank_full[b.slot], b.full)
                    index_pages(2 * i + (j + 2), j)
            order = ((GA0, 0), (K0, 0), (Q0, 0), (K0, 1), (Q0, 1), (GA0, 1), (V0, 2), (V0, 3))
            with sp.Fori(0, 3) as i:
                for j, (col, X) in enumerate(order):
                    load_tile(w_view, col + (2 * i + X) * P, TILE_C + 2 + j, i, 8)
            for j, (col, X) in enumerate(order[:6]):
                load_tile(w_view, col + (6 + X) * P, TILE_C + 26 + j)
            for j in range(2):
                load_tile(w_view, U0 + j * P, TILE_B + j)
            sp.wait_ge(c_done, 1)
            ck = cache_k[0].rearrange("n p h d -> n p (h d)")
            cv = cache_v[0].rearrange("n p h d -> n p (h d)")
            sp.dma_start(wtab[:], windows).then_inc(wtab_in, 16)

            def group(g, last):
                b = bb("m1s", g, ago=1)
                sp.wait_ge(bank_full[b.slot], b.full)
                stand_alone(sp)
                sp.wait_ge(un_sent, 64 * g + 32)
                for j in range(2):
                    sp.dma_start(hist[:, j, :], state_pool[0].rearrange("b r c -> (b r) c")[:, ds((2 * g + j) * P, P)]
                                 ).then_inc(hist_in[j], 16)
                sp.dma_start(wp[:], w_pool[0, ds(g, 1)].rearrange("g (c p) d -> p (g c) d", p=P)).then_inc(wp_in, 16)

                def key_pages(X, pair):
                    t = turn(4 * X + pair, 2, g, 8)
                    sp.wait_ge(k_free[t.slot], t.free)
                    for e in range(2):
                        load_page(ck, kPage[:, 2 * t.slot + e, :, :].rearrange("p h d -> p (h d)"),
                                  (2 * g + X) * PAGES + 2 * pair + e, k_in[t.slot])

                def mask(X):
                    b = bb("OTa", g) if X else bb("OTb", g, ago=1)
                    sp.wait_ge(bank_full[b.slot], b.full)
                    stand_alone(sp)
                    sp.dma_start(probS[:], dropD[ds((2 * g + X) * NT, NT), :].unsqueeze(0).to_broadcast([H, NT, L])
                                 ).then_inc(mask_in[X], 16)

                def value_page(X, p):
                    t = turn(8 * X + p, 4, g, 16)
                    sp.wait_ge(v_free[t.slot], t.free)
                    load_page(cv, vPage[:, t.slot, :, :].rearrange("p h d -> p (h d)"),
                              (2 * g + X) * PAGES + p, v_in[t.slot])

                def unit(j):
                    tile, half = 2 + j // 2, j % 2
                    t = turn(2 * (TILE_B + tile) + half, 4, g, 8)
                    if tile < 4:
                        load_unit(w_view, half, GB0 + (2 * g + tile - 2) * P, t)
                    elif last:
                        load_unit(wo_view, half, (tile - 4) * P, t)
                    else:
                        load_unit(w_view, half, U0 + (2 * g + 2 + tile - 4) * P, t)

                for X in range(2):
                    key_pages(X, 0)
                    key_pages(X, 1)
                    unit(4 * X)
                    if X:
                        unit(5)
                    for p in range(4):
                        value_page(X, p)
                    if not X:
                        unit(1)
                    key_pages(X, 2)
                    unit(4 * X + 2)
                    key_pages(X, 3)
                    mask(X)
                    unit(4 * X + 3)
                    for p in range(4, PAGES):
                        value_page(X, p)

            with sp.Fori(0, GROUPS - 1) as g:
                group(g, False)
            group(GROUPS - 1, True)
            for name in ("m1p", "m1s"):
                b = bb(name, GROUPS - 1)
                sp.wait_ge(bank_free[b.slot], b.read)
            sp.wait_ge(un_sent, 32 * (2 * GROUPS + 1))
            for t in range(TT):
                sp.dma_start(y[:, t, :], x_prompt[0, t * P:(t + 1) * P, :]).then_inc(y_in, 16)
            sp.dma_start(y[0:NS, TT, :], x_sample.rearrange("b t d -> (b t) d")).then_inc(y_in, 16)
            for d in (2, 3):
                load_tile(wo_view, d * P, TILE_D + d)
            sp.wait_ge(mix_low, KC)
            sp.dma_start(gbc, ln_g[0].partition_broadcast(P)).then_inc(ln_in, 16)
            sp.dma_start(bbc, ln_b[0].partition_broadcast(P)).then_inc(ln_in, 16)
            with sp.Fori(0, 6) as i:
                for j in range(2):
                    load_tile(wo_view, (2 * i + 4 + j) * P, TILE_D + 4 + j, i, 2)
            for t in range(TT + 1):
                n = P if t < TT else NS
                dst = y_prompt[0, t * P:(t + 1) * P, :] if t < TT else y_sample.rearrange("b t d -> (b t) d")
                sp.wait_ge(y_ready, t + 1)
                sp.dma_start(dst, y[0:n, t, :]).then_inc(y_sent, 16)
            sp.wait_ge(y_sent, 16 * (TT + 1))
            sp.wait_ge(spool_sent, 16)
            sp.wait_ge(kidx_sent, 32)
            sp.wait_ge(kn_sent, 32 * (H + 1))
            sp.wait_ge(vn_sent[0], 32 * (H // 2 + 1))
            sp.wait_ge(vn_sent[1], 32 * (H // 2 + 1))
            sp.wait_ge(un_sent, 32 * (2 * GROUPS + 1))

        @block.gpsimd
        def _(pool):
            def low(slot, full, width=P):
                pool.wait_ge(high_ready[slot], full)
                pool.tensor_tensor(wL[:, slot, :, 0:width], rawW[:, slot, :, 0:width],
                                   wH[:, slot, :, 0:width].bitcast(F32), ALU.subtract).then_inc(stage_ready[slot], 1)

            low(0, 1, KW)
            low(1, 1, KW)
            with pool.Fori(0, (2 * (TILE_D + KC) - 2) // 4) as i:
                for j in range(4):
                    t = turn(2 + j, 4, i, 4)
                    low(t.slot, t.full)

        @block.scalar
        def _(act):
            def high(tile, half, i=None, per=0, width=P):
                t = turn(2 * tile + half, 4, i, 2 * per)
                act.wait_ge(w_landed[t.slot], 16 * t.full)
                if half == 0:
                    act.wait_ge(stage_free[t.slot // 2], t.free)
                elif not (isinstance(t.free, int) and t.free == 1):
                    act.wait_ge(tile_ready[t.slot // 2], t.free - 1)
                act.activation(wH[:, t.slot, :, 0:width], rawW[:, t.slot, :, 0:width],
                               ACT.Copy).then_inc(high_ready[t.slot], 1)

            def projected(tile, i=None, per=0):
                t = turn(tile, 2, i, per)
                act.wait_ge(tile_ready[t.slot], t.full)
                return acc[t.slot][:, :, 0:HT], acc_copied[t.slot]

            def halves(ap):
                return ap.rearrange("p (a t) -> p a t", a=2)

            def out_of(b, dst, src):
                act.activation(dst, src, ACT.Copy).then_inc(bank_free[b.slot], 1)

            act.dma_start(xnat[:, 0, :], x_prompt[0, 0:P, :]).then_inc(x_in[0], 16)
            act.dma_start(sq[:], square).then_inc(square_in, 16)
            act.dma_start(xnat[:, 1, :], x_prompt[0, P:2 * P, :]).then_inc(x_in[1], 16)
            act.dma_start(xnatS[:], x_sample.rearrange("b t d -> (b t) d")).then_inc(xs_in, 16)
            act.dma_start(headrot[:], head_rot).then_inc(consts_in, 16)
            act.dma_start(halfscale[:], pool_scale[0].rearrange("(j p) -> p j", p=P), allow_slow_non_contiguous=True).then_inc(consts_in, 16)

            for half in range(2):
                high(0, half, width=KW)
            for t in range(TT + 1):
                n = P if t < TT else NS
                for q in range(4):
                    b = xb(f"x{t}{q}")
                    src = bank_wait(act, b)[:, 0:4 * n]
                    act.activation(actH[:, 4 * q:4 * q + 4, t * P:t * P + n],
                                   src.rearrange("p (k t) -> p k t", k=4), ACT.Copy).then_inc(x_high, 1)
                if t < 2:
                    act.dma_start(xnat[:, t, :], x_prompt[0, (t + 2) * P:(t + 3) * P, :]).then_inc(x_in[t], 16)
            for q in range(4):
                b = xb(f"x{TT}{q}")
                act.wait_ge(bank_free[b.slot], b.read)
            act.dma_start(irot[:], idx_rot).then_inc(irot_in, 16)

            high(1, 0)
            high(1, 1)
            src, copied = projected(0)
            high(2, 0)
            act.activation(halves(wiT[ID:KW, :]), src[ID:KW], ACT.Copy, scale=ISCALE)
            act.activation(halves(kiT[0:ID, :]), src[0:ID], ACT.Copy).then_inc(copied, 1)
            act.wait_ge(copied, 2)
            act.dma_start(wiD, wiT[ID:KW, NP_:T]).then_inc(wi_out, 16)
            high(2, 1)
            act.wait_ge(wi_out, 16)
            act.dma_start(wiB[:].rearrange("p h t -> p (h t)"),
                          wiD.rearrange("h t -> (h t)").partition_broadcast(P)).then_inc(wi_back, 16)
            act.wait_ge(ki_ready, 1)
            act.dma_start(kiT[ID:P, :], kiT[0:ID, :]).then_inc(ki_twice, 16)
            with act.Fori(0, 4) as i:
                for j in range(2):
                    high(TILE_A + j + 2, 0, i, 2)
                    src, copied = projected(TILE_A + j, i, 2)
                    act.wait_ge(qi_ready, 2 * i + j + 1)
                    act.activation(halves(raw[:, j]), src, ACT.Copy).then_inc(copied, 1)
                    high(TILE_A + j + 2, 1, i, 2)
            act.wait_ge(qis_near, 1)
            act.dma_start(qiS[ID:P, 1, 0:IH:2, :], qiT[0:ID, :, NP_:T]).then_inc(qis_far, 16)
            act.dma_start(qiS[0:ID, 0, 1:IH:2, :], qiT[ID:P, :, NP_:T]).then_inc(qis_far, 16)
            b = ab("ki")
            out_of(b, kiN[:, 0:TT, :].rearrange("p a b -> p (a b)"), bank_wait(act, b)[:, 0:TT * ID])
            b2 = ab("kis")
            out_of(b2, kiN[0:NS, TT, :], bank_wait(act, b2)[0:NS, 0:ID])
            act.wait_ge(bank_free[b.slot], b.read)
            act.dma_start(p_kidx[0, 0].rearrange("(t p) d -> p t d", p=P), kiN[:, 0:TT, :]).then_inc(kidx_sent, 16)
            act.wait_ge(bank_free[b2.slot], b2.read)
            act.dma_start(s_kidx[0].rearrange("b t d -> (b t) d"), kiN[0:NS, TT, :]).then_inc(kidx_sent, 16)

            def rectify(b, before, n, rows, t):
                src = bank_wait(act, b)
                if before is not None:
                    act.wait_ge(bank_free[before.slot], before.read)
                act.activation(relu[0:rows, t.slot, 0:n], src[0:rows, 0:n], ACT.Relu).then_inc(relu_full[t.slot], 1)

            n, products = 0, []
            for t in (3, 2, 1):
                for h in range(IH):
                    products.append(ab(f"r{t}_{h}"))
                    rectify(products[n], products[n - 2] if n > 1 else None, (t + 1) * P, P, turn(n, 2))
                    n += 1
            for b in products[-2:]:
                act.wait_ge(bank_free[b.slot], b.read)
            with act.Fori(0, 4) as i:
                for j in range(2):
                    b = sbk(f"T{j}", i)
                    src = bank_wait(act, b)
                    out_of(b, kiPT[:, j, :, :].rearrange("p a k -> p (a k)"), src[:])
                    rectify(sbk(f"R{j}", i), sbk(f"R{j}", i, ago=1), 512, P, turn(3 * IH + j, 2, i, 2))
            rectify(nb("Rn"), sbk("R0", 3), 512, NS, turn(3 * IH + NB, 2))

            b = nb("Sn")
            act.wait_ge(bank_free[b.slot], b.read)
            act.wait_ge(kidx_sent, 32)
            with act.Fori(0, 4) as i:
                def values(X):
                    b = cb(f"v{X}", i)
                    src = bank_wait(act, b)
                    act.wait_ge(vn_sent[X], 32 * i + 32)
                    out_of(b, vN[:, X, :, :].rearrange("p t d -> p (t d)"), src[:])
                    b2 = cb(f"vs{X}", i)
                    out_of(b2, vS[:, ds(2 * i + X, 1), :].rearrange("p a d -> p (a d)"), bank_wait(act, b2)[0:NS, 0:P])
                    act.wait_ge(bank_free[b.slot], b.read)
                    act.dma_start(p_v[0, 0, :, ds(2 * i + X, 1), :].rearrange("(t p) a d -> p t (a d)", p=P),
                                  vN[:, X, :, :]).then_inc(vn_sent[X], 16)
                    act.wait_ge(bank_free[b2.slot], b2.read)
                    act.dma_start(s_v[0, :, :, ds(2 * i + X, 1), :].rearrange("b t a d -> (b t) (a d)"),
                                  vS[:, ds(2 * i + X, 1), :].rearrange("p a d -> p (a d)")).then_inc(vn_sent[X], 16)

                def keys(X):
                    b, b2 = cb(f"k{X}", i), cb(f"ks{X}", i)
                    src = bank_wait(act, b)
                    act.wait_ge(kn_sent, 64 * i + 32 * X + 32)
                    out_of(b, kN[:, 0:TT, :].rearrange("p t d -> p (t d)"), src[:])
                    out_of(b2, kN[0:NS, TT, :], bank_wait(act, b2)[0:NS, 0:P])
                    act.wait_ge(bank_free[b.slot], b.read)
                    act.dma_start(p_k[0, 0, :, ds(2 * i + X, 1), :].rearrange("(t p) a d -> p t (a d)", p=P),
                                  kN[:, 0:TT, :]).then_inc(kn_sent, 16)
                    act.wait_ge(bank_free[b2.slot], b2.read)
                    act.dma_start(s_k[0, :, :, ds(2 * i + X, 1), :].rearrange("b t a d -> (b t) (a d)"),
                                  kN[0:NS, TT, :]).then_inc(kn_sent, 16)

                def sample_part(dst, X, src):
                    act.activation(dst[:, ds(2 * i + X, 1), :].rearrange("p a t -> p (a t)"), src[:, X, NP_:T], ACT.Copy)

                def exps(X):
                    for t in range(TT):
                        b = cb(f"S{t}{X}", i)
                        act.wait_ge(bank_free[b.slot], b.read)
                        pr = prob[:, TRI[t]:TRI[t + 1]]
                        act.activation(pr, pr, ACT.Exp, bias=stat[:, t:t + 1], scale=-1.0,
                                       accum_out=stat[:, 8 + t:9 + t]).then_inc(exp_ready, 1)

                def probs_turned(X):
                    for t in range(TT):
                        b = cb(f"P{t}{X}", i)
                        src = bank_wait(act, b)
                        if t >= 2:
                            bank_wait(act, cb(f"O{t - 2}{X}", i))
                        out_of(b, probT[:, t % 2, 0:t + 1, :].rearrange("p s t -> p (s t)"), src[:, 0:(t + 1) * P])

                for j in range(8):
                    high(TILE_C + j + 2, 0, i, 8)
                    if j in (1, 2):
                        values(j - 1)
                    if j == 3:
                        act.wait_ge(gate_ready, 2 * i + 1)
                        sample_part(gateS, 0, gate)
                    if j == 4:
                        keys(0)
                        sample_part(kS, 0, kT)
                    if j == 5:
                        act.wait_ge(head_ready, 4 * i + 3)
                        sample_part(qS, 0, qT)
                        exps(0)
                    if j == 6:
                        keys(1)
                        sample_part(kS, 1, kT)
                        probs_turned(0)
                    if j == 7:
                        act.wait_ge(head_ready, 4 * i + 5)
                        sample_part(qS, 1, qT)
                        exps(1)
                    src, copied = projected(TILE_C + j, i, 8)
                    if j in (2, 7):
                        act.activation(halves(tanhC[:]), src, ACT.Tanh, scale=0.5)
                    dst = {0: raw[:, 0], 1: raw[:, 1], 2: raw[:, 0], 3: kT[:, 0], 4: qT[:, 0], 5: kT[:, 1],
                           6: qT[:, 1], 7: raw[:, 1]}[j]
                    act.activation(halves(dst), src, ACT.Copy).then_inc(copied, 1)
                    high(TILE_C + j + 2, 1, i, 8)
                act.wait_ge(gate_ready, 2 * i + 2)
                sample_part(gateS, 1, gate)
                probs_turned(1)
            for t in range(TT):
                b = cb(f"O{t}1", 3)
                act.wait_ge(bank_free[b.slot], b.read)
            act.wait_ge(kn_sent, 32 * (H + 1))
            for X in range(2):
                act.wait_ge(vn_sent[X], 32 * (H // 2 + 1))
            act.wait_ge(drop_ready, 1)
            act.dma_start(dropD, scoreS[:]).then_inc(drop_out, 16)
            act.wait_ge(drop_out, 16)
            act.activation(stat[:, 30:31], halfscale[:, 0:1], ACT.Copy).then_inc(c_done, 1)

            with act.Fori(0, GROUPS) as g:
                def keys_copied(X, lo, hi):
                    for n in range(lo, hi, 2):
                        b = bb(f"K{n}{'ab'[X]}", g)
                        out_of(b, kPT[:, 0, :, :].rearrange("p h k -> p (h k)"), bank_wait(act, b)[:])

                def sample_view(ap, lo, hi):
                    return ap[:, HIST + NP_:UW].rearrange("p (b r) -> p b r", b=NB)[:, :, lo:hi]

                def history(t):
                    b = bb(f"h{t}", g)
                    src = bank_wait(act, b)[:, 0:NB * HIST].rearrange("p (b r) -> p b r", b=NB)
                    act.wait_ge(pooled_ready, 2 * g + t + 1)
                    out_of(b, sample_view(U[:, t], 0, HIST), src)

                def copy_tile(t):
                    src, copied = projected(TILE_B + t, g, 4)
                    if t < 2:
                        if t == 0:
                            bank_wait(act, bb("m1s", g, ago=1))
                        act.activation(U[:, t, HIST:HIST + HT], src[:, 0, :], ACT.Copy)
                        act.activation(U[:, t, HIST + HT:HIST + NP_], src[:, 1, 0:NP_ - HT], ACT.Copy)
                        act.activation(newU[:, t, :], src[:, 1, NP_ - HT:HT], ACT.Copy)
                        act.activation(sample_view(U[:, t], HIST, UE),
                                       src[:, 1, NP_ - HT:HT].rearrange("p (b r) -> p b r", b=NB),
                                       ACT.Copy).then_inc(copied, 1)
                    else:
                        if t == 3:
                            act.wait_ge(gate_ready, H + 2 * g + 1)
                        act.activation(halves(rot[:]), src, ACT.Tanh, scale=0.5)
                        act.activation(halves(raw[:, t - 2]), src, ACT.Copy).then_inc(copied, 1)

                def last_rows(t):
                    b = bb(f"u{t}", g)
                    src = bank_wait(act, b)
                    act.wait_ge(un_sent, 64 * g + 32 * t + 32)
                    act.activation(uN[0:HIST, 0, :], src[0:HIST, 0:P], ACT.Copy)
                    out_of(b, uN[:, 1, :], src[0:NS, P:2 * P])
                    act.wait_ge(bank_free[b.slot], b.read)
                    col = ds((2 * g + t) * P, P)
                    act.dma_start(p_pool[0, 0, :, col], uN[0:HIST, 0, :]).then_inc(un_sent, 16)
                    act.dma_start(s_pool[0, :, HIST - NT:HIST, col], uN[:, 1, :]).then_inc(un_sent, 16)

                for X in range(2):
                    keys_copied(X, 0, 8)
                    high(TILE_B + 2 * X + 2, 0, g, 4)
                    if X == 0:
                        history(0)
                    else:
                        last_rows(1)
                    keys_copied(X, 8, 12)
                    if X == 0:
                        history(1)
                    keys_copied(X, 12, 16)
                    copy_tile(2 * X)
                    high(TILE_B + 2 * X + 2, 1, g, 4)
                    act.wait_ge(max_ready, 2 * g + X + 1)
                    act.activation(probS[:], probS[:], ACT.Exp, bias=stat[0:NS, 20:21], scale=-1.0,
                                   accum_out=stat[0:NS, 21:22]).then_inc(exps_ready, 1)
                    high(TILE_B + 2 * X + 3, 0, g, 4)
                    if X == 0:
                        last_rows(0)
                    b = bb(f"Pt{'ab'[X]}", g)
                    src = bank_wait(act, b)
                    act.activation(probST[:].rearrange("p a t -> p (a t)"), src[:, 0:PAGES * NS], ACT.Copy)
                    out_of(b, probSTn[:], src[0:NS, PAGES * NS:(PAGES + 1) * NS])
                    for half in range(2):
                        b = b67(f"O{half}{'ab'[X]}", g)
                        out_of(b, outS[:, 4 * half:4 * half + 4, :].rearrange("p h d -> p (h d)"),
                               bank_wait(act, b)[0:NT, :])
                    copy_tile(2 * X + 1)
                    high(TILE_B + 2 * X + 3, 1, g, 4)

            for name in ("m1p", "m1s"):
                b = bb(name, GROUPS - 1)
                act.wait_ge(bank_free[b.slot], b.read)
            b = bb("OTb", GROUPS - 1)
            act.wait_ge(bank_free[b.slot], b.read)
            for k in range(KC):
                act.activation(actH[:, k, :], mixed[:, k, :], ACT.Copy).then_inc(mix_high, 1)
            with act.Fori(0, 7) as i:
                for j in range(2):
                    high(TILE_D + j + 2, 0, i, 2)
                    src, copied = projected(TILE_D + j, i, 2)
                    act.activation(halves(raw[:, j]), src, ACT.Copy).then_inc(copied, 1)
                    high(TILE_D + j + 2, 1, i, 2)
            for j in range(2):
                src, copied = projected(TILE_D + 14 + j)
                act.activation(halves(raw[:, j]), src, ACT.Copy).then_inc(copied, 1)
            act.wait_ge(var_ready, 1)
            act.activation(std[:], mv[:, :, 1], ACT.Sqrt).then_inc(std_ready, 1)
            act.wait_ge(var_ready, 2)
            for t in range(TT + 1):
                n = P if t < TT else NS
                act.activation(y[0:n, t, :], y[0:n, t, :], ACT.Identity, bias=stat[0:n, 8 + t:9 + t],
                               scale=stat[0:n, t:t + 1]).then_inc(norm_ready, 1)

        @block.tensor
        def _(pe):
            for s in (*stage_free, *acc_copied, *bank_free.values(), *k_free, *v_free):
                pe.sem_inc(s, 1)
            pe.sem_inc(head_ready, 1)
            for s in (pooled_ready, qi_ready):
                pe.sem_inc(s, 2)
            for s in (*vn_sent, kn_sent, un_sent):
                pe.sem_inc(s, 32)

            def unit(tile, half, i=None, per=0, width=P, quarters=(0, 1), chunk_ready=None):
                t, u = turn(tile, 2, i, per), turn(2 * tile + half, 4, i, 2 * per)
                if 0 in quarters:
                    pe.wait_ge(stage_ready[u.slot], u.full)
                    if half == 0:
                        pe.wait_ge(acc_copied[t.slot], t.free)
                for q in quarters:
                    for k in range(q * HU // 2, (q + 1) * HU // 2):
                        kk = half * HU + k
                        if chunk_ready is not None:
                            pe.wait_ge(chunk_ready, kk + 1)
                        for w, parts in ((wH, (actH, actL)), (wL, (actH,))):
                            for a in parts:
                                for e in range(2):
                                    last = pe.matmul(acc[t.slot][0:width, e, 0:HT], w[:, u.slot, k, 0:width],
                                                     a[:, kk, e * HT:(e + 1) * HT], start=(kk == 0 and w is wH and a is actH),
                                                     stop=(kk == KC - 1 and w is wL))
                if 1 in quarters:
                    last.then_inc(tile_ready[t.slot] if half else stage_free[t.slot], 1)

            def take(b):
                pe.wait_ge(bank_free[b.slot], b.free)
                return bank[b.slot]

            def full(b, last):
                last.then_inc(bank_full[b.slot], 1)

            def copied(tile, i=None, per=0):
                t = turn(tile, 2, i, per)
                pe.wait_ge(acc_copied[t.slot], t.read)

            pe.wait_ge(square_in, 16)
            for t in range(TT + 1):
                n = P if t < TT else NS
                if t < TT:
                    pe.wait_ge(x_in[t % 2], 16 * (t // 2 + 1))
                else:
                    pe.wait_ge(xs_in, 16)
                src = xnat[:, t % 2, :] if t < TT else xnatS[:, :]
                for q in range(4):
                    b = xb(f"x{t}{q}")
                    dst = take(b)
                    for j in range(4):
                        last = pe.transpose(dst[:, j * n:(j + 1) * n], src[:, (4 * q + j) * P:(4 * q + j + 1) * P],
                                            ident[0:n, 0:n])
                    full(b, last)
            for q in range(4):
                b = xb(f"x{TT}{q}")
                pe.wait_ge(bank_free[b.slot], b.read)

            for half in range(2):
                unit(0, half, width=KW)
            with pe.Fori(0, 4) as i:
                for j in range(2):
                    for half in range(2):
                        unit(TILE_A + j, half, i, 2)
            b = ab("wi")
            dst = take(b)
            copied(0)
            for t in range(1, TT):
                last = pe.transpose(dst[:, (t - 1) * IH:t * IH], wiT[ID:KW, t * P:(t + 1) * P], ident[ID:KW, ID:KW])
            full(b, last)
            pe.wait_ge(ki_ready, 1)
            b = ab("ki")
            dst = take(b)
            for t in range(TT):
                last = pe.transpose(dst[:, t * ID:(t + 1) * ID], kiT[0:ID, t * P:(t + 1) * P], ident[0:ID, 0:ID])
            full(b, last)
            b = ab("kis")
            full(b, pe.transpose(take(b)[0:NS, 0:ID], kiT[0:ID, NP_:T], ident[0:ID, 0:ID]))
            pe.wait_ge(ki_twice, 16)
            for t in (3, 2, 1):
                for h in range(IH):
                    if t == 3 and h % 2 == 0:
                        pe.wait_ge(qi_ready, h // 2 + 3)
                    b = ab(f"r{t}_{h}")
                    part = slice(ID * (h % 2), ID * (h % 2) + ID)
                    full(b, pe.matmul(take(b)[:, 0:(t + 1) * P], qiT[part, h // 2, t * P:(t + 1) * P],
                                      kiT[part, 0:(t + 1) * P], start=True, stop=True))
            pe.wait_ge(qis_near, 1)
            pe.wait_ge(qis_far, 32)
            with pe.Fori(0, 4) as i:
                for j in range(2):
                    b = sbk(f"T{j}", i)
                    dst = take(b)
                    pe.wait_ge(kip_in[j], 16 * PAGES * i + 16 * PAGES)
                    for a in range(PAGES // 2):
                        last = pe.transpose(dst[:, a * P:(a + 1) * P],
                                            kiPage[:, j, 2 * a:2 * a + 2, :].rearrange("p a d -> p (a d)"), ident)
                    full(b, last)
                    b2 = sbk(f"R{j}", i)
                    dst = take(b2)
                    pe.wait_ge(bank_free[b.slot], b.read)
                    for a in range(PAGES // 2):
                        last = pe.matmul(dst[:, a * P:(a + 1) * P], kiPT[:, j, a, :],
                                         qiS[:, :, :, ds((2 * i + j) * NT, NT)].rearrange("p e h t -> p (e h) t"),
                                         start=True, stop=True)
                    full(b2, last)
            b = nb("Rn")
            full(b, pe.matmul(take(b)[0:NS, :], kiT[0:ID, NP_:T],
                              qiS[0:ID, 0, :, :].rearrange("p h t -> p (h t)"), start=True, stop=True))
            pe.wait_ge(bank_free[b.slot], b.read)
            for half in range(2):
                b = nb(f"S{half}")
                dst = take(b)
                for p in range(4):
                    last = pe.transpose(dst[0:NS, p * P:(p + 1) * P], scoreST[:, 4 * half + p, :], ident)
                full(b, last)
            b = nb("Sn")
            full(b, pe.transpose(take(b)[0:NS, 0:NS], scoreSTn[:], ident[0:NS, 0:NS]))

            with pe.Fori(0, 4) as i:
                def by_token(name, X, src):
                    b = cb(f"{name}{X}", i)
                    dst = take(b)
                    for t in range(TT):
                        last = pe.transpose(dst[:, t * P:(t + 1) * P], src[:, t * P:(t + 1) * P], ident)
                    full(b, last)
                    b = cb(f"{name}s{X}", i)
                    full(b, pe.transpose(take(b)[0:NS, 0:P], src[:, NP_:T], ident))

                def scores(X):
                    for t in range(TT):
                        b = cb(f"S{t}{X}", i)
                        full(b, pe.matmul(take(b)[:, 0:(t + 1) * P], qT[:, X, t * P:(t + 1) * P],
                                          kT[:, X, 0:(t + 1) * P], start=True, stop=True))

                def attend(X):
                    bv = cb(f"v{X}", i)
                    pe.wait_ge(bank_free[bv.slot], bv.read)
                    def turned(t):
                        b = cb(f"P{t}{X}", i)
                        dst = take(b)
                        pe.wait_ge(prob_ready, 8 * i + 4 * X + t + 1)
                        for s in range(t + 1):
                            last = pe.transpose(dst[:, s * P:(s + 1) * P], prob[:, TRI[t] + s * P:TRI[t] + (s + 1) * P], ident)
                        full(b, last)

                    def values_of(t):
                        bp, b = cb(f"P{t}{X}", i), cb(f"O{t}{X}", i)
                        dst = take(b)
                        pe.wait_ge(bank_free[bp.slot], bp.read)
                        for s in range(t + 1):
                            last = pe.matmul(dst[:, 0:P], vN[:, X, s, :], probT[:, t % 2, s, :],
                                             start=(s == 0), stop=(s == t))
                        full(b, last)

                    turned(0)
                    turned(1)
                    values_of(0)
                    turned(2)
                    values_of(1)
                    turned(3)
                    values_of(2)
                    values_of(3)

                for j in range(8):
                    unit(TILE_C + j, 0, i, 8)
                    if j in (1, 2):
                        copied(TILE_C + j - 1, i, 8)
                        by_token("v", j - 1, raw[:, j - 1])
                    if j == 4:
                        pe.wait_ge(head_ready, 4 * i + 2)
                        by_token("k", 0, kT[:, 0])
                    if j == 5:
                        pe.wait_ge(head_ready, 4 * i + 3)
                        scores(0)
                    if j == 6:
                        pe.wait_ge(head_ready, 4 * i + 4)
                        by_token("k", 1, kT[:, 1])
                        attend(0)
                    if j == 7:
                        pe.wait_ge(head_ready, 4 * i + 5)
                        scores(1)
                    unit(TILE_C + j, 1, i, 8)
                attend(1)
            pe.wait_ge(c_done, 1)
            with pe.Fori(0, GROUPS) as g:
                def quarter(X, n):
                    unit(TILE_B + 2 * X + n // 4, n // 2 % 2, g, 4, quarters=(n % 2,))

                def key_pages(X, lo, hi):
                    def turned(n):
                        pair, hp = n // 4, n % 4
                        k = turn(4 * X + pair, 2, g, 8)
                        if hp == 0:
                            pe.wait_ge(k_in[k.slot], 32 * k.full)
                        b = bb(f"K{n}{'ab'[X]}", g)
                        dst = take(b)
                        for e in range(2):
                            for a in range(2):
                                last = pe.transpose(dst[:, (2 * e + a) * P:(2 * e + a + 1) * P],
                                                    kPage[:, 2 * k.slot + a, 2 * hp + e, :], ident)
                        full(b, last)

                    def products(n):
                        pair, hp = n // 4, n % 4
                        b, st = bb(f"K{n}{'ab'[X]}", g), b67(f"S{pair // 2}{'ab'[X]}", g)
                        pe.wait_ge(bank_free[b.slot], b.read)
                        if n == 0:
                            pe.wait_ge(pad_ready, 2 * g + X + 1)
                        if n % 8 == 0:
                            take(st)
                        for e in range(2):
                            h = 2 * hp + e
                            last = pe.matmul(bank[st.slot][0:NS, pair % 2 * 256:pair % 2 * 256 + 256],
                                             qPad[:, X, h * NS:(h + 1) * NS], kPT[:, n % 2, e, :],
                                             start=(h == 0), stop=(h == H - 1))
                            if h == H - 2:
                                last.then_inc(k_free[turn(4 * X + pair, 2).slot], 1)
                        if n % 8 == 7:
                            full(st, last)

                    turned(lo)
                    for n in range(lo, hi):
                        if n + 1 < hi:
                            turned(n + 1)
                        products(n)

                def new_keys(X):
                    b = bb(f"Sn{'ab'[X]}", g)
                    dst = take(b)
                    for h in range(H):
                        last = pe.matmul(dst[0:NS, 0:NS], qPad[:, X, h * NS:(h + 1) * NS], kS[:, h, :],
                                         start=(h == 0), stop=(h == H - 1))
                    full(b, last)

                def probs_turned(X):
                    b = bb(f"Pt{'ab'[X]}", g)
                    dst = take(b)
                    pe.wait_ge(probS_ready, 2 * g + X + 1)
                    stand_alone(pe)
                    for p in range(PAGES):
                        pe.transpose(dst[:, p * NS:(p + 1) * NS], probS[:, p * P:(p + 1) * P], ident[0:NS, 0:NS])
                    full(b, pe.transpose(dst[0:NS, PAGES * NS:(PAGES + 1) * NS], probS[:, PAST:L], ident[0:NS, 0:NS]))

                def value_pages(X, lo, hi):
                    outs = [b67(f"O{half}{'ab'[X]}", g) for half in range(2)]

                    def products(h, probs, values, start, stop):
                        return pe.matmul(bank[outs[h // 4].slot][0:NT, h % 4 * P:(h % 4 + 1) * P], probs, values,
                                         start=start and h % 4 == 0, stop=stop and h % 4 == 3, skip_group_check=True)

                    if lo == 0:
                        for b in outs:
                            take(b)
                        bp = bb(f"Pt{'ab'[X]}", g)
                        pe.wait_ge(bank_free[bp.slot], bp.read)
                    for p in range(lo, hi):
                        v = turn(8 * X + p, 4, g, 16)
                        pe.wait_ge(v_in[v.slot], 16 * v.full)
                        for h in range(H):
                            last = products(h, probST[:, p, h * NT:(h + 1) * NT], vPage[:, v.slot, h, :], p == 0, False)
                        last.then_inc(v_free[v.slot], 1)
                    if hi == PAGES:
                        for h in range(H):
                            last = products(h, probSTn[:, h * NT:(h + 1) * NT], vS[:, h, :], False, True)
                            if h % 4 == 3:
                                full(outs[h // 4], last)

                def output_turned(X):
                    b = bb(f"OT{'ab'[X]}", g)
                    dst = take(b)
                    for half in range(2):
                        o = b67(f"O{half}{'ab'[X]}", g)
                        pe.wait_ge(bank_free[o.slot], o.read)
                    stand_alone(pe)
                    for h in range(H):
                        last = pe.transpose(dst[:, h * NT:(h + 1) * NT], outS[:, h, :], ident[0:NT, 0:NT])
                    full(b, last)

                def history(t):
                    b = bb(f"h{t}", g)
                    dst = take(b)
                    pe.wait_ge(hist_in[t], 16 * g + 16)
                    full(b, pe.transpose(dst[:, 0:NB * HIST], hist[:, t, :], ident[0:NB * HIST, 0:NB * HIST]))

                def last_rows(t):
                    b = bb(f"u{t}", g)
                    dst = take(b)
                    copied(TILE_B + t, g, 4)
                    pe.transpose(dst[0:HIST, 0:P], U[:, t, NP_:NP_ + HIST], ident)
                    full(b, pe.transpose(dst[0:NS, P:2 * P], newU[:, t, :], ident))

                for X in range(2):
                    key_pages(X, 0, 4)
                    quarter(X, 0)
                    key_pages(X, 4, 8)
                    quarter(X, 1)
                    if X == 0:
                        history(0)
                    else:
                        last_rows(1)
                    key_pages(X, 8, 12)
                    quarter(X, 2)
                    if X == 0:
                        history(1)
                    key_pages(X, 12, 16)
                    new_keys(X)
                    quarter(X, 3)
                    quarter(X, 4)
                    quarter(X, 5)
                    if X == 0:
                        last_rows(0)
                    probs_turned(X)
                    value_pages(X, 0, 4)
                    quarter(X, 6)
                    value_pages(X, 4, 8)
                    quarter(X, 7)
                    output_turned(X)
                pe.wait_ge(pooled_ready, 2 * g + 4)
                pe.wait_ge(wp_in, 16 * g + 16)
                for e in range(2):
                    for part, values in (("p", U[:, :, HIST:HIST + NP_]), ("s", pooledS[:])):
                        b = bb(f"m{e}{part}", g)
                        dst = take(b)
                        n = values.shape[-1]
                        for c in range(2):
                            last = pe.matmul(dst[:, 0:n], wp[:, c, e * P:(e + 1) * P], values[:, c, :],
                                             start=(c == 0), stop=(c == 1))
                        full(b, last)

            def rows(j, i):
                copied(TILE_D + j, i, 2)
                b = yb(f"yp{j}", i)
                dst = take(b)
                for t in range(TT):
                    last = pe.transpose(dst[:, t * P:(t + 1) * P], raw[:, j, t * P:(t + 1) * P], ident)
                full(b, last)
                b = yb(f"ys{j}", i)
                full(b, pe.transpose(take(b)[0:NS, 0:P], raw[:, j, NP_:T], ident))

            for half in range(2):
                unit(TILE_D, half, chunk_ready=mix_low)
            with pe.Fori(0, 7) as i:
                for j in range(2):
                    unit(TILE_D + j + 1, 0, i, 2)
                    rows(j, i)
                    unit(TILE_D + j + 1, 1, i, 2)
            unit(TILE_D + KC - 1, 0)
            rows(0, 7)
            unit(TILE_D + KC - 1, 1)
            rows(1, 7)

        @block.vector
        def _(dve):
            own = Steps(dve, dve_steps)

            n = 0
            for t in range(TT + 1):
                m = P if t < TT else NS
                for q in range(4):
                    n += 1
                    b = xb(f"x{t}{q}")
                    dve.wait_ge(x_high, n)
                    at = (slice(None), slice(4 * q, 4 * q + 4), slice(t * P, t * P + m))
                    dve.tensor_tensor(actL[at], bank[b.slot][:, 0:4 * m].rearrange("p (k t) -> p k t", k=4),
                                      actH[at].bitcast(F32), ALU.subtract).then_inc(bank_free[b.slot], 1)

            def rotate(dst, src, rows, table, swap):
                half = rot[0:rows, :]
                stand_alone(dve)
                own.step(dve.stream_shuffle(half, src, swap))
                own.wait()
                own.step(dve.tensor_tensor(half, half, table[0:rows, 1, :], ALU.mult))
                own.step(dve.tensor_tensor(src, src, table[0:rows, 0, :], ALU.mult))
                own.wait()
                return dve.tensor_tensor(dst, src, half, ALU.add)

            def copied(tile, i=None, per=0):
                t = turn(tile, 2, i, per)
                dve.wait_ge(acc_copied[t.slot], t.read)

            copied(0)
            dve.wait_ge(irot_in, 16)
            rotate(kiT[0:ID, :], kiT[0:ID, :], ID, irot, SWAP_I).then_inc(ki_ready, 1)
            own.step(dve.memset(qiS[:], 0.0))
            dve.wait_ge(ki_ready, 1)
            with dve.Fori(0, 4) as i:
                own.enter(i, 6)
                for j in range(2):
                    copied(TILE_A + j, i, 2)
                    dve.wait_ge(qi_ready, 2 * i + j + 2)
                    rotate(qiT[:, ds(2 * i + j, 1), :].rearrange("p a t -> p (a t)"), raw[:, j], P, irot, SWAP_I
                           ).then_inc(qi_ready, 1)
                own.leave(4)
            dve.wait_ge(qi_ready, H + 2)
            own.wait()
            own.step(dve.tensor_copy(qiS[0:ID, 0, 0:IH:2, :], qiT[0:ID, :, NP_:T]))
            dve.tensor_copy(qiS[ID:P, 1, 1:IH:2, :], qiT[ID:P, :, NP_:T]).then_inc(qis_near, 1)
            b = ab("wi")
            dve.tensor_copy(wiN[:].rearrange("p t h -> p (t h)"), bank_wait(dve, b)[:, 0:3 * IH]
                            ).then_inc(bank_free[b.slot], 1)
            dve.wait_ge(bank_free[b.slot], b.read)
            n = 0
            for t in (3, 2, 1):
                sc = scoreP[:, TRI[t] - P:TRI[t + 1] - P]
                for h in range(IH):
                    r, b = turn(n, 2), ab(f"r{t}_{h}")
                    dve.wait_ge(relu_full[r.slot], r.full)
                    src, w = relu[:, r.slot, 0:(t + 1) * P], wiN[:, t - 1, h:h + 1]
                    if h == 0:
                        dve.tensor_scalar(sc, src, w, None, ALU.mult).then_inc(bank_free[b.slot], 1)
                    else:
                        dve.wait_ge(bank_free[before.slot], before.read)
                        dve.scalar_tensor_tensor(sc, src, w, sc, ALU.mult, ALU.add).then_inc(bank_free[b.slot], 1)
                    n, before = n + 1, b
                dve.wait_ge(bank_free[b.slot], b.read)
                own.step(dve.tensor_tensor(sc[:, t * P:], sc[:, t * P:], causal, ALU.add))
            dve.wait_ge(wi_back, 16)
            with dve.Fori(0, 4) as i:
                own.enter(i, 2)
                for j in range(2):
                    r, b = turn(3 * IH + j, 2, i, 2), sbk(f"R{j}", i)
                    dve.wait_ge(relu_full[r.slot], r.full)
                    cols = ds((2 * i + j) * NT, NT)
                    v = relu[:, r.slot, :].rearrange("p (g h t) -> p g h t", g=PAGES, h=IH)
                    own.step(dve.tensor_tensor(v, v, wiB[:, :, cols].unsqueeze(1).to_broadcast([P, PAGES, IH, NT]),
                                               ALU.mult))
                    own.wait()
                    dve.tensor_reduce(scoreST[:, :, cols], v.rearrange("p g h t -> p g t h"), AX.X, ALU.add
                                      ).then_inc(bank_free[b.slot], 1)
                own.leave(4)
            r = turn(3 * IH + NB, 2)
            dve.wait_ge(relu_full[r.slot], r.full)
            v = relu[0:NS, r.slot, :].rearrange("p (h t) -> p h t", h=IH)
            own.step(dve.tensor_tensor(v, v, wiB[0:NS], ALU.mult))
            own.wait()
            b = nb("Rn")
            dve.tensor_reduce(scoreSTn[:], v.rearrange("p h t -> p t h"), AX.X, ALU.add).then_inc(bank_free[b.slot], 1)
            for half in range(2):
                b = nb(f"S{half}")
                dve.tensor_copy(scoreS[:, 512 * half:512 * (half + 1)], bank_wait(dve, b)[0:NS, :]
                                ).then_inc(bank_free[b.slot], 1)
            b = nb("Sn")
            dve.tensor_tensor(scoreS[:, PAST:L], bank_wait(dve, b)[0:NS, 0:NS], newmask, ALU.add
                              ).then_inc(bank_free[b.slot], 1)
            dve.wait_ge(bank_free[b.slot], b.read)

            def pick(scores, top):
                own.wait()
                stand_alone(dve)
                own.step(dve.max(top, scores))
                own.wait()
                stand_alone(dve)
                own.step(dve.match_replace(scores, top, scores, PICKED))

            for t in (1, 2, 3):
                sc = scoreP[:, TRI[t] - P:TRI[t + 1] - P]
                with dve.Fori(0, TOPK_P // ROUND) as i:
                    own.enter(i, 2)
                    pick(sc, top8[:])
                    own.leave(TOPK_P // ROUND)
                own.wait()
                own.step(dve.tensor_scalar(keepP[:, TRI[t]:TRI[t + 1]], sc, PICKED / 1.5, MASKED, ALU.is_gt, ALU.mult))
            own.step(dve.tensor_copy(keepP[:, 0:P], causal))
            dve.wait_ge(consts_in, 32)
            own.step(dve.tensor_scalar(halfscale[:], halfscale[:], 0.5, None, ALU.mult))

            rounds = TOPK_S // ROUND // 4
            with dve.Fori(0, 4) as i:
                own.enter(i, 2 * rounds + 4 * 3 + 8)

                def make_gate(X):
                    dve.scalar_tensor_tensor(gate[:, X, :], tanhC[:], 1.0, raw[:, X, :], ALU.add, ALU.mult
                                             ).then_inc(gate_ready, 1)

                def softmax(X):
                    for t in range(TT):
                        b = cb(f"S{t}{X}", i)
                        src = bank_wait(dve, b)
                        stand_alone(dve)
                        dve.tensor_tensor_reduce(prob[:, TRI[t]:TRI[t + 1]], src[:, 0:(t + 1) * P],
                                                 keepP[:, TRI[t]:TRI[t + 1]], -SCALE, 3e38, ALU.add, ALU.min,
                                                 stat[:, t:t + 1]).then_inc(bank_free[b.slot], 1)
                    for t in range(TT):
                        dve.wait_ge(exp_ready, 8 * i + 4 * X + t + 1)
                        own.step(dve.reciprocal(stat[:, 16 + t:17 + t], stat[:, 8 + t:9 + t]))
                        own.wait()
                        pr = prob[:, TRI[t]:TRI[t + 1]]
                        dve.tensor_scalar(pr, pr, stat[:, 16 + t:17 + t], None, ALU.mult).then_inc(prob_ready, 1)

                def gated(X):
                    for t in range(TT):
                        b = cb(f"O{t}{X}", i)
                        cols = slice(t * P, (t + 1) * P)
                        dve.scalar_tensor_tensor(mixed[:, ds(2 * i + X, 1), cols].rearrange("p a t -> p (a t)"),
                                                 bank_wait(dve, b)[:, 0:P], 0.5, gate[:, X, cols],
                                                 ALU.mult, ALU.mult).then_inc(bank_free[b.slot], 1)

                def rotated(j, dst, X):
                    copied(TILE_C + j, i, 8)
                    dve.wait_ge(head_ready, 4 * i + j - 2)
                    rotate(dst[0:32, X, :], dst[0:32, X, :], 32, headrot, SWAP_H).then_inc(head_ready, 1)

                for _ in range(rounds):
                    pick(scoreS[:], top8[0:NS, :])
                copied(TILE_C + 2, i, 8)
                make_gate(0)
                rotated(3, kT, 0)
                rotated(4, qT, 0)
                softmax(0)
                rotated(5, kT, 1)
                dve.wait_ge(gate_ready, 2 * i + 1)
                gated(0)
                rotated(6, qT, 1)
                softmax(1)
                copied(TILE_C + 7, i, 8)
                make_gate(1)
                dve.wait_ge(gate_ready, 2 * i + 2)
                gated(1)
                own.leave(4)
            own.wait()
            dve.tensor_scalar(scoreS[:], scoreS[:], PICKED / 1.5, MASKED, ALU.is_gt, ALU.mult).then_inc(drop_ready, 1)
            dve.wait_ge(c_done, 1)
            own.step(dve.memset(U[:, :, 0:HIST], 0.0))
            own.step(dve.memset(qPad[:], 0.0))
            dve.wait_ge(wtab_in, 16)
            own.wait()
            with dve.Fori(0, GROUPS) as g:
                own.enter(g, 2 * 6)

                def queries(X):
                    dve.tensor_copy(qPad[:, X, :].rearrange("p (h c) -> p h c", h=H)[:, :, 0:NT],
                                    qS[:, :, ds((2 * g + X) * NT, NT)]).then_inc(pad_ready, 1)

                def keys_copied(X):
                    for n in range(1, 16, 2):
                        b = bb(f"K{n}{'ab'[X]}", g)
                        dve.tensor_copy(kPT[:, 1, :, :].rearrange("p h k -> p (h k)"), bank_wait(dve, b)[:]
                                        ).then_inc(bank_free[b.slot], 1)

                def softmax(X):
                    dve.wait_ge(mask_in[X], 16 * g + 16)
                    parts = ((b67(f"S0{'ab'[X]}", g), 0, 512), (b67(f"S1{'ab'[X]}", g), 512, PAST), (bb(f"Sn{'ab'[X]}", g), PAST, L))
                    for n, (b, lo, hi) in enumerate(parts):
                        src = bank_wait(dve, b)
                        stand_alone(dve)
                        dve.tensor_tensor_reduce(probS[:, lo:hi], src[0:NS, 0:hi - lo], probS[:, lo:hi], -SCALE, 3e38,
                                                 ALU.add, ALU.min, stat[0:NS, 16 + n:17 + n]).then_inc(bank_free[b.slot], 1)
                    dve.wait_ge(bank_free[b.slot], b.read)
                    dve.tensor_reduce(stat[0:NS, 20:21], stat[0:NS, 16:19], AX.X, ALU.min).then_inc(max_ready, 1)
                    dve.wait_ge(exps_ready, 2 * g + X + 1)
                    own.step(dve.reciprocal(stat[0:NS, 22:23], stat[0:NS, 21:22]))
                    own.wait()
                    dve.tensor_scalar(probS[:], probS[:], stat[0:NS, 22:23], None, ALU.mult
                                      ).then_inc(probS_ready, 1)

                def pool_inputs(t):
                    copied(TILE_B + t, g, 4)
                    u, src = U[:, t, :], U[:, t, :]
                    for lv in range(4):
                        lo, w = (2 << lv) - 1, 1 << lv
                        dst = win[:, lv % 2, :]
                        own.step(dve.scalar_tensor_tensor(dst[:, lo:UW], src[:, lo - w:UW - w], wtab[:, ds(g * WT + lv, 1)],
                                                          src[:, lo:UW], ALU.mult, ALU.add))
                        own.wait()
                        src = dst
                    inv = wtab[:, ds(g * WT + 4, 1)]
                    samples = lambda ap: ap[:, HIST + NP_:UW].rearrange("p (b r) -> p b r", b=NB)[:, :, HIST:UE]
                    dve.scalar_tensor_tensor(pooledS[:, t, :].rearrange("p (b r) -> p b r", b=NB),
                                             samples(src), inv, samples(u), ALU.mult, ALU.subtract)
                    b = bb(f"u{t}", g)
                    dve.wait_ge(bank_full[b.slot], b.full)
                    dve.scalar_tensor_tensor(u[:, 2 * HIST:HIST + NP_], src[:, 2 * HIST:HIST + NP_], inv,
                                             u[:, 2 * HIST:HIST + NP_], ALU.mult, ALU.subtract)
                    first = win[:, 0, HIST:2 * HIST]
                    own.step(dve.tensor_tensor(first, src[:, HIST:2 * HIST], wtab[:, ds(g * WT + 5, HIST)], ALU.mult))
                    own.wait()
                    dve.tensor_tensor(u[:, HIST:2 * HIST], first, u[:, HIST:2 * HIST], ALU.subtract
                                      ).then_inc(pooled_ready, 1)

                def make_gate(t):
                    copied(TILE_B + 2 + t, g, 4)
                    dve.scalar_tensor_tensor(raw[:, t, :], rot[:], 1.0, raw[:, t, :], ALU.add, ALU.mult
                                             ).then_inc(gate_ready, 1)

                for X in range(2):
                    queries(X)
                    keys_copied(X)
                    softmax(X)
                    pool_inputs(X)
                    if X == 1:
                        make_gate(0)
                    b = bb(f"OT{'ab'[X]}", g)
                    dve.scalar_tensor_tensor(mixed[:, 0:H, ds(NP_ + (2 * g + X) * NT, NT)],
                                             bank_wait(dve, b)[:, 0:NS].rearrange("p (h t) -> p h t", h=H), 0.5,
                                             gateS[:, :, ds((2 * g + X) * NT, NT)], ALU.mult, ALU.mult
                                             ).then_inc(bank_free[b.slot], 1)
                make_gate(1)
                dve.wait_ge(gate_ready, 2 * g + H + 2)
                for e in range(2):
                    for part, cols in (("p", slice(0, NP_)), ("s", slice(NP_, T))):
                        b = bb(f"m{e}{part}", g)
                        dve.scalar_tensor_tensor(mixed[:, ds(H + 2 * g + e, 1), cols].rearrange("p a t -> p (a t)"),
                                                 bank_wait(dve, b)[:, 0:cols.stop - cols.start],
                                                 halfscale[:, ds(2 * g + e, 1)], raw[:, e, cols],
                                                 ALU.mult, ALU.mult).then_inc(bank_free[b.slot], 1)
                own.leave(GROUPS)

            for k in range(KC):
                dve.wait_ge(mix_high, k + 1)
                dve.tensor_tensor(actL[:, k, :], mixed[:, k, :], actH[:, k, :].bitcast(F32), ALU.subtract
                                  ).then_inc(mix_low, 1)
            dve.wait_ge(y_in, 16 * (TT + 1))

            def residual(d, j, i):
                b = yb(f"yp{j}", i)
                at = y[:, 0:TT, ds(d * P, P)]
                dve.scalar_tensor_tensor(at, at, ALPHA, bank_wait(dve, b)[:].rearrange("p (t c) -> p t c", t=TT),
                                         ALU.mult, ALU.add).then_inc(bank_free[b.slot], 1)
                b = yb(f"ys{j}", i)
                at = y[0:NS, TT, ds(d * P, P)]
                dve.scalar_tensor_tensor(at, at, ALPHA, bank_wait(dve, b)[0:NS, 0:P], ALU.mult, ALU.add
                                         ).then_inc(bank_free[b.slot], 1)
                dve.wait_ge(bank_free[b.slot], b.read)

            with dve.Fori(0, 4) as i:
                own.enter(i, TT + 1)
                for n in range(4):
                    residual(4 * i + n, n % 2, 2 * i + n // 2)
                for t in range(TT + 1):
                    m = P if t < TT else NS
                    own.step(dve.bn_stats(bn[0:m, t, ds(i, 1), :].rearrange("p a s -> p (a s)"), y[0:m, t, ds(512 * i, 512)]))
                own.leave(4)
            own.wait()
            own.step(dve.memset(mv[:], 1.0))
            own.wait()
            for t in range(TT + 1):
                m = P if t < TT else NS
                own.step(dve.bn_aggr(mv[0:m, t, :], bn[0:m, t, :, :].rearrange("p a s -> p (a s)")))
            own.wait()
            dve.tensor_scalar(mv[:, :, 1], mv[:, :, 1], EPS, None, ALU.add).then_inc(var_ready, 1)
            dve.wait_ge(std_ready, 1)
            own.step(dve.reciprocal(stat[:, 0:5], std[:]))
            own.wait()
            dve.scalar_tensor_tensor(stat[:, 8:13], mv[:, :, 0], -1.0, stat[:, 0:5], ALU.mult, ALU.mult
                                     ).then_inc(var_ready, 1)
            dve.wait_ge(ln_in, 32)
            for t in range(TT + 1):
                m = P if t < TT else NS
                dve.wait_ge(norm_ready, t + 1)
                own.step(dve.tensor_tensor(y[0:m, t, :], y[0:m, t, :], gbc[0:m], ALU.mult))
                own.wait()
                dve.tensor_tensor(y[0:m, t, :], y[0:m, t, :], bbc[0:m], ALU.add).then_inc(y_ready, 1)


def rotation(dim, rotated, rows):
    import numpy as np
    half = rotated // 2
    pos = np.concatenate([np.arange(NP_), PAST + np.tile(np.arange(NT), NB)]).astype(np.float32)
    freqs = np.float32(500000.0) ** (-np.arange(half, dtype=np.float32) * np.float32(2.0 / rotated))
    ang = pos[None, :] * freqs.astype(np.float32)[:, None]
    table = np.zeros((rows, 2, T), np.float32)
    table[:, 0, :] = 1.0
    for start in range(0, rows, dim):
        for a in range(2):
            table[start + a * half:start + (a + 1) * half, 0, :] = np.cos(ang)
            table[start + a * half:start + (a + 1) * half, 1, :] = np.sin(ang) * (2 * a - 1)
    return table


def squares():
    import numpy as np
    out = np.zeros((P, 288), np.float32)
    out[:, 0:P] = np.eye(P)
    r = np.arange(P)
    out[:, P:2 * P] = np.where(r[None, :] <= r[:, None], 0.0, MASKED)
    n = np.arange(NS)
    seen = (n[None, :] // NT == n[:, None] // NT) & (n[None, :] % NT <= n[:, None] % NT)
    out[0:NS, 256:288] = np.where(seen, 0.0, MASKED)
    return out


def window_table():
    import numpy as np
    out = np.zeros((P, GROUPS * WT), np.float32)
    for g, w in enumerate(WINDOWS):
        row = [float(w > (1 << lv)) for lv in range(4)] + [1.0 / w] + [1.0 / min(t + 1, w) for t in range(HIST)]
        out[:, g * WT:(g + 1) * WT] = np.array(row, np.float32)
    return out


_INS = ["x_prompt", "x_sample", "cache_k", "cache_v", "cache_kidx", "state_pool", "page_table", "w_in", "w_pool",
        "pool_scale", "w_out", "ln_g", "ln_b"]
_OUTS = [("y_prompt", (1, NP_, D)), ("y_sample", (NB, NT, D)), ("p_k", (1, 1, NP_, H, P)), ("p_v", (1, 1, NP_, H, P)),
         ("p_kidx", (1, 1, NP_, ID)), ("p_pool", (1, 1, HIST, H * P)), ("s_k", (1, NB, NT, H, P)),
         ("s_v", (1, NB, NT, H, P)), ("s_kidx", (1, NB, NT, ID)), ("s_pool", (1, NB, HIST, H * P))]


def kernel(**inputs):
    import numpy as _np
    import concourse.bacc as _bacc
    from concourse.bass_utils import run_bass_kernel_spmd as _run

    nc = _bacc.Bacc("TRN2", target_bir_lowering=False, num_devices=1, dynamic_dma_scratch_size=1024)
    arrays = {f"in_{name}": _np.ascontiguousarray(inputs[name]) for name in _INS}
    arrays["const_square"] = squares()
    arrays["const_idx_rot"] = rotation(ID, 16, P)
    arrays["const_head_rot"] = rotation(P, 32, 32)
    arrays["const_windows"] = window_table()
    args = [nc.dram_tensor(name, a.shape, mybir.dt.from_np(a.dtype), kind="ExternalInput").ap()
            for name, a in arrays.items()]
    args += [nc.dram_tensor(f"out_{name}", shape, F32, kind="ExternalOutput").ap() for name, shape in _OUTS]
    layer_program(nc, *args)
    r = _run(nc, [arrays], core_ids=[0])
    return tuple(r.results[0][f"out_{name}"] for name, _ in _OUTS)
```

```python
from contextlib import ExitStack

import concourse.bass as bass
from concourse import mybir

ALU = mybir.AluOpType
ACT = mybir.ActivationFunctionType
AX = mybir.AxisListType
F32 = mybir.dt.float32
F32R = mybir.dt.float32r
BF16 = mybir.dt.bfloat16
I32 = mybir.dt.int32

P = 128
D = 2048
KC = D // P
NP_ = 512
NB = 8
NT = 4
NS = NB * NT
T = NP_ + NS
HT = T // 2
TT = NP_ // P
H = 8
IH = 16
ID = 64
PAGES = 8
PAST = PAGES * P
L = PAST + NS
TOPK_P = 128
TOPK_S = 256
ROUND = 8
GROUPS = 4
WINDOWS = (2, 4, 8, 16)
HIST = 15
UE = HIST + NT
UW = HIST + NP_ + NB * UE
SCALE = 128.0 ** -0.5
ISCALE = 1.0 / 32.0
ALPHA = 2.0 ** 0.25
EPS = 1e-5
MASKED = -1e30
PICKED = -3e38
Q0, K0, V0, GA0, QI0, KI0, U0, GB0 = 0, 1024, 2048, 3072, 4096, 5120, 5200, 6224
KW = 80
HU = KC // 2
TRI = [0, 128, 384, 768, 1280]

TILE_A, TILE_C, TILE_B, TILE_D = 1, 9, 41, 57
SWAP_I = [*range(8, 16), *range(8), *range(16, 32)]
SWAP_H = [*range(16, 32), *range(16)]
RT = 4 * 12
RS = RT + 6
WT = 20


class Turn:

    def __init__(self, slot, before):
        self.slot, self.full, self.free, self.read = slot, before + 1, before + 1, before + 2


def turn(n, slots, i=None, per=0):
    assert per % slots == 0
    return Turn(n % slots, n // slots if i is None else i * (per // slots) + n // slots)


class Banks:

    def __init__(self, banks):
        self.used = dict.fromkeys(banks, 0)

    def stage(self, names, banks, times=1):
        assert times == 1 or len(names) % len(banks) == 0, len(names)
        step = len(names) // len(banks)
        table = {name: (banks[k % len(banks)], self.used[banks[k % len(banks)]] + k // len(banks))
                 for k, name in enumerate(names)}
        assert len(table) == len(names)
        for k in range(len(names)):
            self.used[banks[k % len(banks)]] += times if times == 1 else 0
        for b in banks if times > 1 else ():
            self.used[b] += times * step

        def at(name, i=None, ago=0):
            b, n = table[name]
            return Turn(b, n if i is None else i * step + (n - ago * step))

        return at


class Steps:

    def __init__(self, eng, sem):
        self.eng, self.sem, self.done, self.i, self.per = eng, sem, 0, None, 0

    def value(self):
        return self.done if self.i is None else self.i * self.per + self.done

    def step(self, ins):
        ins.then_inc(self.sem, 1)
        self.done += 1

    def wait(self):
        self.eng.wait_ge(self.sem, self.value())

    def enter(self, i, per):
        self.i, self.per, self.start = i, per, self.done

    def leave(self, times):
        assert self.done - self.start == self.per, (self.done - self.start, self.per)
        self.done, self.i = self.start + times * self.per, None


def layer_program(nc, x_prompt, x_sample, cache_k, cache_v, cache_kidx, state_pool, page_table,
                  w_in, w_pool, pool_scale, w_out, ln_g, ln_b, square, idx_rot, head_rot, windows,
                  y_prompt, y_sample, p_k, p_v, p_kidx, p_pool, s_k, s_v, s_kidx, s_pool):
    ds = bass.ds
    ctx = ExitStack()
    with ctx:
        def sem(name):
            return ctx.enter_context(nc.semaphore(name))

        def sems(name, n):
            return [sem(f"{name}{j}") for j in range(n)]

        def sb(name, shape, dt=F32, where=ctx):
            return where.enter_context(nc.sbuf_tensor(name, shape, dt))

        actH = sb("actH", [P, KC, T], F32R)
        actL = sb("actL", [P, KC, T], F32R)
        rawW = sb("rawW", [P, 4, HU, P])
        wH = sb("wH", [P, 4, HU, P], F32R)
        wL = sb("wL", [P, 4, HU, P], F32R)
        mixed = sb("mixed", [P, KC, T])
        raw = sb("raw", [P, 2, T])
        rot = sb("rot", [P, T])
        qS = sb("qS", [P, H, NS])
        kS = sb("kS", [P, H, NS])
        vS = sb("vS", [NS, H, P])
        gateS = sb("gateS", [P, H, NS])
        sq = sb("sq", [P, 288])
        ident, causal, newmask = sq[:, 0:P], sq[:, P:2 * P], sq[0:NS, 256:288]
        pageT = sb("pageT", [1, NB * PAGES], I32)
        halfscale = sb("halfscale", [P, H])
        stat = sb("stat", [P, 32])
        outer = ExitStack()
        scoreS = sb("scoreS", [NS, L], F32, outer)
        scoreP = sb("scoreP", [P, TRI[4] - P], F32, outer)
        keepP = sb("keepP", [P, TRI[4]], BF16, outer)
        headrot = sb("headrot", [32, 2, T], F32, outer)
        wiN = sb("wiN", [P, 3, 2 + IH], F32, outer)
        top8 = sb("top8", [P, 3, 8], F32, outer)
        with ExitStack() as s:
            xnat = sb("xnat", [P, TT, D], F32, s)
            xnatS = sb("xnatS", [NS, D], F32, s)
        with ExitStack() as s:
            kiT = sb("kiT", [P, T], F32, s)
            wiT = sb("wiT", [P, T], F32, s)
            irot = sb("irot", [P, 2, T], F32, s)
            wiB = sb("wiB", [P, IH, NS], F32, s)
            relu = sb("relu", [P, 2, 512], F32, s)
            kiPage = sb("kiPage", [P, NB * PAGES, ID], F32, s)
            kiPT = sb("kiPT", [P, 2, 4, P], F32, s)
            scoreST = sb("scoreST", [P, PAGES, NS], F32, s)
            scoreSTn = sb("scoreSTn", [NS, NS], F32, s)
            qiS = sb("qiS", [P, 2, IH, NS], F32, s)
            qiN = sb("qiN", [P, H, NS], F32, s)
            kiN = sb("kiN", [P, 5, ID], F32, s)
        with ExitStack() as s:
            qT = sb("qT", [P, 2, T], F32, s)
            kT = sb("kT", [P, 2, T], F32, s)
            vN = sb("vN", [P, 2, TT, P], F32, s)
            kN = sb("kN", [P, 5, P], F32, s)
            gate = sb("gate", [P, 2, T], F32, s)
            tanhC = sb("tanhC", [P, T], F32, s)
            prob = sb("prob", [P, TRI[4]], F32, s)
            probT = sb("probT", [P, 2, TT, P], F32, s)
        outer.close()
        with ExitStack() as s:
            probS = sb("probS", [NS, L], F32, s)
            vPage = sb("vPage", [P, 4, H, P], F32, s)
            kPT = sb("kPT", [P, 2, 2, 2 * P], F32, s)
            qPad = sb("qPad", [P, 2, H * (NS + NT)], F32, s)
            probST = sb("probST", [P, PAGES, NS], F32, s)
            probSTn = sb("probSTn", [NS, NS], F32, s)
            U = sb("U", [P, 2, UW], F32, s)
            win = sb("win", [P, 2, UW], F32, s)
            pooledS = sb("pooledS", [P, 2, NS], F32, s)
            wp = sb("wp", [P, 2, 256], F32, s)
            hist = sb("hist", [NB * HIST, 2, P], F32, s)
            uN = hist[0:NS]
            newU = sb("newU", [P, 2, NS], F32, s)
            wtab = sb("wtab", [P, GROUPS * WT], F32, s)
            kPage = sb("kPage", [P, 2, 2, H, P], F32, s)
            outS = probS[0:NT, 0:H * P].rearrange("p (h d) -> p h d", h=H)
        with ExitStack() as s:
            y = sb("y", [P, 5, D], F32, s)
            bn = sb("bn", [P, 5, KC, 6], F32, s)
            mv = sb("mv", [P, 5, 2], F32, s)
            std = sb("std", [P, 5], F32, s)
        flat = mixed[:].rearrange("p k t -> p (k t)")
        gbc, bbc = flat[:, 0:D], flat[:, D:2 * D]

        acc = [ctx.enter_context(nc.psum_tensor(f"acc{j}", [P, 2, 512], F32)) for j in range(2)]
        four = (4, 5, 6, 7)
        bank = {j: ctx.enter_context(nc.psum_tensor(f"bank{j}", [P, 512], F32)) for j in four}
        dropD = nc.dram_tensor("dropD", [NS, L], F32, kind="Internal").ap()
        wiD = nc.dram_tensor("wiD", [IH, NS], F32, kind="Internal").ap()

        w_landed = sems("w_landed", 4)
        high_ready = sems("high_ready", 4)
        stage_ready = sems("stage_ready", 4)
        stage_free = sems("stage_free", 2)
        tile_ready = sems("tile_ready", 2)
        acc_copied = sems("acc_copied", 2)
        bank_full = {j: sem(f"bank_full{j}") for j in four}
        bank_free = {j: sem(f"bank_free{j}") for j in four}
        apart = sem("apart")
        square_in = sem("square_in")
        consts_in = sem("consts_in")
        irot_in = sem("irot_in")
        pages_in = sem("pages_in")
        x_in = sems("x_in", TT)
        xs_in = sem("xs_in")
        x_high = sem("x_high")
        ki_ready = sem("ki_ready")
        ki_twice = sem("ki_twice")
        wi_out = sem("wi_out")
        wi_back = sem("wi_back")
        qi_ready = sem("qi_ready")
        qis_near = sem("qis_near")
        qis_far = sem("qis_far")
        relu_full = sems("relu_full", 2)
        kip_in = sem("kip_in")
        drop_ready = sem("drop_ready")
        head_ready = sem("head_ready")
        gate_ready = sem("gate_ready")
        exp_ready = sem("exp_ready")
        prob_ready = sem("prob_ready")
        dve_steps = sem("dve_steps")
        kn_sent = sem("kn_sent")
        vn_sent = sems("vn_sent", 2)
        c_done = sem("c_done")
        drop_out = sem("drop_out")
        mask_in = sems("mask_in", 2)
        pad_ready = sem("pad_ready")
        k_in = sems("k_in", 2)
        v_in = sems("v_in", 4)
        v_free = sems("v_free", 4)
        max_ready = sem("max_ready")
        exps_ready = sem("exps_ready")
        probS_ready = sem("probS_ready")
        hist_in = sems("hist_in", 2)
        wtab_in = sem("wtab_in")
        wp_in = sem("wp_in")
        pooled_ready = sem("pooled_ready")
        un_sent = sem("un_sent")
        mix_high = sem("mix_high")
        mix_low = sem("mix_low")
        y_in = sem("y_in")
        ln_in = sem("ln_in")
        var_ready = sem("var_ready")
        std_ready = sem("std_ready")
        norm_ready = sem("norm_ready")
        y_scaled = sem("y_scaled")
        y_ready = sems("y_ready", TT + 1)
        pool_steps = sem("pool_steps")
        kidx_sent = sem("kidx_sent")
        spool_sent = sem("spool_sent")
        y_sent = sem("y_sent")

        banks = Banks(four)
        xb = banks.stage([f"x{t}{q}" for t in range(TT + 1) for q in range(4)], four)
        ab = banks.stage(["wi"], four)

        def rt(place):
            return [f"{place}{e}{t}" for e in range(2) for t in (1, 2, 3)]

        rb = banks.stage([*rt("r0"), *rt("r1")], four, 4)
        zb = banks.stage(["T0", "T1", "ki", "kis", *rt("z"), *(u for n in range(NB) for u in (f"R{n}", f"T{n + 2}")
                                                               if u not in ("T8", "T9"))], four)
        nb = banks.stage(["Rn", "S0", "S1", "Sn"], four)

        def c_uses(X):
            return [f"{u}{X}" for u in ("P0", "P1", "O0", "P2", "O1", "P3", "O2", "O3")]

        cb = banks.stage(["v0", "vs0", "v1", "vs1", "k0", "ks0", "S00", "S10", "S20", "S30", "k1", "ks1",
                          *c_uses(0), "S01", "S11", "S21", "S31", *c_uses(1)], four, 4)

        def key_uses(X, lo, hi):
            return [f"K{n}{X}" for n in range(lo, hi)]

        bb = banks.stage([*key_uses("a", 0, 9), "h0", *key_uses("a", 9, 13), "h1", *key_uses("a", 13, 16), "Sna", "u0",
                          "Pta", "OTa", *key_uses("b", 0, 9), "u1", *key_uses("b", 9, 16), "Snb", "Ptb", "OTb",
                          "m0p", "m0s", "m1p", "m1s"], (4, 5), GROUPS)
        b67 = banks.stage([f"{w}{half}{X}" for X in "ab" for w in "SO" for half in range(2)], (6, 7), GROUPS)
        yb = banks.stage(["yp0", "ys0", "yp1", "ys1"], four, 8)

        def bank_wait(eng, b):
            eng.wait_ge(bank_full[b.slot], b.full)
            return bank[b.slot]

        def stand_alone(eng):
            eng.sem_inc(apart, 1)

        block = ctx.enter_context(nc.Block())

        w_view = w_in[0].rearrange("(k p) c -> p k c", p=P)
        wo_view = w_out[0].rearrange("(k p) c -> p k c", p=P)

        @block.sync
        def _(sp):
            def load_unit(view, half, col, t, width=P):
                sp.wait_ge(stage_ready[t.slot], t.free)
                stand_alone(sp)
                sp.dma_start(rawW[:, t.slot, :, 0:width],
                             view[:, half * HU:(half + 1) * HU, ds(col, width)]).then_inc(w_landed[t.slot], 16)

            def load_tile(view, col, tile, i=None, per=0):
                for half in range(2):
                    load_unit(view, half, col, turn(2 * tile + half, 4, i, 2 * per))

            for t in range(2):
                sp.dma_start(xnat[:, t, :], x_prompt[0, t * P:(t + 1) * P, :]).then_inc(x_in[t], 16)
            for half in range(2):
                load_unit(w_view, half, KI0, turn(half, 4), KW)
            sp.dma_start(pageT[:], page_table.rearrange("(a b) c -> a (b c)", a=1)).then_inc(pages_in, 16)
            sp.dma_start(s_pool[0, :, 0:HIST - NT, :], state_pool[0, :, NT:HIST, :]).then_inc(spool_sent, 16)
            sp.wait_ge(pages_in, 16)

            def page_number(cache, index):
                stand_alone(sp)
                return sp.value_load(pageT[0:1, ds(index, 1)], min_val=0, max_val=cache.shape[0] - 1)

            def load_page(cache, dst, page, done):
                sp.dma_start(dst, cache[ds(page, 1)].rearrange("a p n -> p (a n)")).then_inc(done, 16)

            BESIDE = 6

            def index_page(at):
                load_page(cache_kidx[0], kiPage[:, ds(at, 1), :].rearrange("p a d -> p (a d)"),
                          page_number(cache_kidx[0], at), kip_in)

            with sp.Fori(0, 4) as i:
                for j in range(2):
                    load_tile(w_view, QI0 + (2 * i + j) * P, TILE_A + j, i, 2)
                    for q in range(4):
                        b = xb(f"x{TT}{q}")
                        sp.wait_ge(bank_free[b.slot], b.read)
                    for p in range(BESIDE):
                        index_page(2 * BESIDE * i + (BESIDE * j + p))
            for j in range(2):
                load_tile(w_view, V0 + j * P, TILE_C + j)
            with sp.Fori(8 * BESIDE, NB * PAGES) as at:
                index_page(at)
            order = ((GA0, 0), (K0, 0), (Q0, 0), (K0, 1), (Q0, 1), (GA0, 1), (V0, 2), (V0, 3))
            with sp.Fori(0, 3) as i:
                for j, (col, X) in enumerate(order):
                    load_tile(w_view, col + (2 * i + X) * P, TILE_C + 2 + j, i, 8)
            for j, (col, X) in enumerate(order[:6]):
                load_tile(w_view, col + (6 + X) * P, TILE_C + 26 + j)
            for j in range(2):
                load_tile(w_view, U0 + j * P, TILE_B + j)
            ck = cache_k[0].rearrange("n p h d -> n p (h d)")
            cv = cache_v[0].rearrange("n p h d -> n p (h d)")

            def key_pages(g, X, pair):
                t = turn(4 * X + pair, 2, g, 8)
                pages = [page_number(ck, (2 * g + X) * PAGES + (2 * pair + e)) for e in range(2)]
                if pair >= 2:
                    b = bb(f"K{4 * pair - 5}{'ab'[X]}", g)
                else:
                    b = bb(f"K{4 * pair + 11}a", g) if X else bb(f"K{4 * pair + 11}b", g, ago=1)
                sp.wait_ge(bank_full[b.slot], b.full)
                for e in range(2):
                    load_page(ck, kPage[:, 1 - t.slot, e, :, :].rearrange("p h d -> p (h d)"), pages[e], k_in[t.slot])

            b = nb("Sn")
            sp.wait_ge(bank_free[b.slot], b.read)
            sp.wait_ge(kidx_sent, 32)
            key_pages(0, 0, 0)
            sp.wait_ge(c_done, 1)
            key_pages(0, 0, 1)
            sp.dma_start(wtab[:], windows).then_inc(wtab_in, 16)

            def group(g, last):
                def pool_loads():
                    b = bb("m1s", g, ago=1)
                    sp.wait_ge(bank_full[b.slot], b.full)
                    stand_alone(sp)
                    sp.wait_ge(un_sent, 64 * g + 32)
                    for j in range(2):
                        sp.dma_start(hist[:, j, :], state_pool[0].rearrange("b r c -> (b r) c")[:, ds((2 * g + j) * P, P)]
                                     ).then_inc(hist_in[j], 16)
                    sp.dma_start(wp[:], w_pool[0, ds(g, 1)].rearrange("g (c p) d -> p (g c) d", p=P)).then_inc(wp_in, 16)

                def mask(X):
                    b = bb("OTa", g) if X else bb("OTb", g, ago=1)
                    sp.wait_ge(bank_full[b.slot], b.full)
                    sp.wait_ge(drop_out, 16)
                    stand_alone(sp)
                    sp.dma_start(probS[:], dropD[ds((2 * g + X) * NT, NT), :].unsqueeze(0).to_broadcast([H, NT, L])
                                 ).then_inc(mask_in[X], 16)

                def value_page(X, p):
                    t = turn(8 * X + p, 4, g, 16)
                    page = page_number(cv, (2 * g + X) * PAGES + p)
                    sp.wait_ge(v_free[t.slot], t.free)
                    load_page(cv, vPage[:, t.slot, :, :].rearrange("p h d -> p (h d)"), page, v_in[t.slot])

                def unit(j):
                    tile, half = 2 + j // 2, j % 2
                    t = turn(2 * (TILE_B + tile) + half, 4, g, 8)
                    if tile < 4:
                        load_unit(w_view, half, GB0 + (2 * g + tile - 2) * P, t)
                    elif last:
                        load_unit(wo_view, half, (tile - 4) * P, t)
                    else:
                        load_unit(w_view, half, U0 + (2 * g + 2 + tile - 4) * P, t)

                for X in range(2):
                    if X == 0:
                        pool_loads()
                    else:
                        key_pages(g, 1, 0)
                        key_pages(g, 1, 1)
                    unit(4 * X)
                    if X:
                        unit(5)
                    key_pages(g, X, 2)
                    value_page(X, 0)
                    value_page(X, 1)
                    if not X:
                        unit(1)
                    unit(4 * X + 2)
                    key_pages(g, X, 3)
                    mask(X)
                    value_page(X, 2)
                    value_page(X, 3)
                    unit(4 * X + 3)
                    for p in range(4, PAGES):
                        value_page(X, p)
                if not last:
                    for pair in range(2):
                        key_pages(g + 1, 0, pair)

            with sp.Fori(0, GROUPS - 1) as g:
                group(g, False)
            group(GROUPS - 1, True)
            for name in ("m1p", "m1s"):
                b = bb(name, GROUPS - 1)
                sp.wait_ge(bank_free[b.slot], b.read)
            sp.wait_ge(un_sent, 32 * (2 * GROUPS + 1))
            for t in range(TT):
                sp.dma_start(y[:, t, :], x_prompt[0, t * P:(t + 1) * P, :]).then_inc(y_in, 16)
            sp.dma_start(y[0:NS, TT, :], x_sample.rearrange("b t d -> (b t) d")).then_inc(y_in, 16)
            for d in (2, 3):
                load_tile(wo_view, d * P, TILE_D + d)
            sp.wait_ge(mix_low, KC)
            sp.dma_start(gbc, ln_g[0].partition_broadcast(P)).then_inc(ln_in, 16)
            sp.dma_start(bbc, ln_b[0].partition_broadcast(P)).then_inc(ln_in, 16)
            with sp.Fori(0, 6) as i:
                for j in range(2):
                    load_tile(wo_view, (2 * i + 4 + j) * P, TILE_D + 4 + j, i, 2)
            for t in (0, 2, 1, 4, 3):
                n = P if t < TT else NS
                dst = y_prompt[0, t * P:(t + 1) * P, :] if t < TT else y_sample.rearrange("b t d -> (b t) d")
                sp.wait_ge(y_ready[t], 1)
                sp.dma_start(dst, y[0:n, t, :]).then_inc(y_sent, 16)
            sp.wait_ge(y_sent, 16 * (TT + 1))
            sp.wait_ge(spool_sent, 16)
            sp.wait_ge(kidx_sent, 32)
            sp.wait_ge(kn_sent, 32 * (H + 1))
            sp.wait_ge(vn_sent[0], 32 * (H // 2 + 1))
            sp.wait_ge(vn_sent[1], 32 * (H // 2 + 1))
            sp.wait_ge(un_sent, 32 * (2 * GROUPS + 1))

        @block.gpsimd
        def _(pool):
            def low(slot, full, width=P):
                pool.wait_ge(high_ready[slot], full)
                pool.tensor_tensor(wL[:, slot, :, 0:width], rawW[:, slot, :, 0:width],
                                   wH[:, slot, :, 0:width].bitcast(F32), ALU.subtract).then_inc(stage_ready[slot], 1)

            low(0, 1, KW)
            low(1, 1, KW)
            with pool.Fori(0, (2 * (TILE_D + KC) - 2) // 4) as i:
                for j in range(4):
                    t = turn(2 + j, 4, i, 4)
                    low(t.slot, t.full)

            pool.wait_ge(ln_in, 32)
            pool.wait_ge(norm_ready, 2)
            pool.tensor_tensor(y[:, 1, :], y[:, 1, :], gbc, ALU.mult).then_inc(pool_steps, 1)
            pool.wait_ge(pool_steps, 1)
            pool.tensor_tensor(y[:, 1, :], y[:, 1, :], bbc, ALU.add).then_inc(y_ready[1], 1)
            pool.wait_ge(y_scaled, 1)
            pool.tensor_tensor(y[:, 3, :], y[:, 3, :], bbc, ALU.add).then_inc(y_ready[3], 1)

        @block.scalar
        def _(act):
            def high(tile, half, i=None, per=0, width=P):
                t = turn(2 * tile + half, 4, i, 2 * per)
                act.wait_ge(w_landed[t.slot], 16 * t.full)
                if half == 0:
                    act.wait_ge(stage_free[t.slot // 2], t.free)
                elif not (isinstance(t.free, int) and t.free == 1):
                    act.wait_ge(tile_ready[t.slot // 2], t.free - 1)
                act.activation(wH[:, t.slot, :, 0:width], rawW[:, t.slot, :, 0:width],
                               ACT.Copy).then_inc(high_ready[t.slot], 1)

            def projected(tile, i=None, per=0):
                t = turn(tile, 2, i, per)
                act.wait_ge(tile_ready[t.slot], t.full)
                return acc[t.slot][:, :, 0:HT], acc_copied[t.slot]

            def halves(ap):
                return ap.rearrange("p (a t) -> p a t", a=2)

            def out_of(b, dst, src):
                act.activation(dst, src, ACT.Copy).then_inc(bank_free[b.slot], 1)

            act.dma_start(sq[:], square).then_inc(square_in, 16)
            for t in range(2, TT):
                act.dma_start(xnat[:, t, :], x_prompt[0, t * P:(t + 1) * P, :]).then_inc(x_in[t], 16)
            act.dma_start(xnatS[:], x_sample.rearrange("b t d -> (b t) d")).then_inc(xs_in, 16)
            act.dma_start(headrot[:], head_rot).then_inc(consts_in, 16)
            act.dma_start(halfscale[:], pool_scale[0].rearrange("(j p) -> p j", p=P), allow_slow_non_contiguous=True).then_inc(consts_in, 16)

            for t in range(TT + 1):
                if t == TT:
                    for half in range(2):
                        high(0, half, width=KW)
                n = P if t < TT else NS
                for q in range(4):
                    b = xb(f"x{t}{q}")
                    src = bank_wait(act, b)[:, 0:4 * n]
                    act.activation(actH[:, 4 * q:4 * q + 4, t * P:t * P + n],
                                   src.rearrange("p (k t) -> p k t", k=4), ACT.Copy).then_inc(x_high, 1)
            for q in range(4):
                b = xb(f"x{TT}{q}")
                act.wait_ge(bank_free[b.slot], b.read)
            act.dma_start(irot[:], idx_rot).then_inc(irot_in, 16)

            high(1, 0)
            high(1, 1)
            src, copied = projected(0)
            act.activation(halves(wiT[ID:KW, :]), src[ID:KW], ACT.Copy, scale=ISCALE)
            act.activation(halves(kiT[0:ID, :]), src[0:ID], ACT.Copy).then_inc(copied, 1)
            high(2, 0)
            act.wait_ge(ki_ready, 1)
            act.dma_start(kiT[ID:P, :], kiT[0:ID, :]).then_inc(ki_twice, 16)
            high(2, 1)
            act.dma_start(wiD, wiT[ID:KW, NP_:T]).then_inc(wi_out, 16)

            def rectify(b, before, n, rows, t):
                src = bank_wait(act, b)
                act.wait_ge(bank_free[before.slot], before.read)
                act.activation(relu[0:rows, t.slot, 0:n], src[0:rows, 0:n], ACT.Relu).then_inc(relu_full[t.slot], 1)

            with act.Fori(0, 4) as i:
                names = rt("r0") + rt("r1")
                for j in range(2):
                    high(TILE_A + j + 2, 0, i, 2)
                    for n in range(6 * j, 6 * j + 6):
                        before = rb(names[n - 2], i) if n >= 2 else rb(names[n + 10], i, ago=1)
                        rectify(rb(names[n], i), before, (int(names[n][-1]) + 1) * P, P, turn(n, 2, i, 12))
                    src, copied = projected(TILE_A + j, i, 2)
                    act.activation(halves(raw[:, j]), src, ACT.Copy).then_inc(copied, 1)
                    high(TILE_A + j + 2, 1, i, 2)

            act.wait_ge(wi_out, 16)
            act.dma_start(wiB[:].rearrange("p h t -> p (h t)"),
                          wiD.rearrange("h t -> (h t)").partition_broadcast(P)).then_inc(wi_back, 16)

            def pages_turned(n):
                b = zb(f"T{n}")
                out_of(b, kiPT[:, n % 2, :, :].rearrange("p a k -> p (a k)"), bank_wait(act, b)[:])

            for n in range(2):
                pages_turned(n)
            bk = zb("ki")
            out_of(bk, kiN[:, 0:TT, :].rearrange("p a b -> p (a b)"), bank_wait(act, bk)[:, 0:TT * ID])
            bks = zb("kis")
            out_of(bks, kiN[0:NS, TT, :], bank_wait(act, bks)[0:NS, 0:ID])
            act.wait_ge(qis_near, 1)
            act.dma_start(qiS[ID:P, 1, 0:IH:2, :], qiN[0:ID]).then_inc(qis_far, 16)
            act.dma_start(qiS[0:ID, 0, 1:IH:2, :], qiN[ID:P]).then_inc(qis_far, 16)
            behind = [rb("r112", 3), rb("r113", 3)]
            for n, name in enumerate(rt("z")):
                behind.append(zb(name))
                rectify(zb(name), behind[n], (int(name[-1]) + 1) * P, P, turn(RT + n, 2))
            act.wait_ge(bank_free[bk.slot], bk.read)
            act.dma_start(p_kidx[0, 0].rearrange("(t p) d -> p t d", p=P), kiN[:, 0:TT, :]).then_inc(kidx_sent, 16)
            act.wait_ge(bank_free[bks.slot], bks.read)
            act.dma_start(s_kidx[0].rearrange("b t d -> (b t) d"), kiN[0:NS, TT, :]).then_inc(kidx_sent, 16)

            for n in range(NB):
                behind.append(zb(f"R{n}"))
                rectify(zb(f"R{n}"), behind[-3], 512, P, turn(RS + n, 2))
                if n + 2 < NB:
                    pages_turned(n + 2)
            rectify(nb("Rn"), behind[-2], 512, NS, turn(RS + NB, 2))

            b = nb("Sn")
            act.wait_ge(bank_free[b.slot], b.read)
            act.wait_ge(kidx_sent, 32)
            with act.Fori(0, 4) as i:
                def values(X):
                    b = cb(f"v{X}", i)
                    src = bank_wait(act, b)
                    act.wait_ge(vn_sent[X], 32 * i + 32)
                    out_of(b, vN[:, X, :, :].rearrange("p t d -> p (t d)"), src[:])
                    b2 = cb(f"vs{X}", i)
                    out_of(b2, vS[:, ds(2 * i + X, 1), :].rearrange("p a d -> p (a d)"), bank_wait(act, b2)[0:NS, 0:P])
                    act.wait_ge(bank_free[b.slot], b.read)
                    act.dma_start(p_v[0, 0, :, ds(2 * i + X, 1), :].rearrange("(t p) a d -> p t (a d)", p=P),
                                  vN[:, X, :, :]).then_inc(vn_sent[X], 16)
                    act.wait_ge(bank_free[b2.slot], b2.read)
                    act.dma_start(s_v[0, :, :, ds(2 * i + X, 1), :].rearrange("b t a d -> (b t) (a d)"),
                                  vS[:, ds(2 * i + X, 1), :].rearrange("p a d -> p (a d)")).then_inc(vn_sent[X], 16)

                def keys(X):
                    b, b2 = cb(f"k{X}", i), cb(f"ks{X}", i)
                    src = bank_wait(act, b)
                    act.wait_ge(kn_sent, 64 * i + 32 * X + 32)
                    out_of(b, kN[:, 0:TT, :].rearrange("p t d -> p (t d)"), src[:])
                    out_of(b2, kN[0:NS, TT, :], bank_wait(act, b2)[0:NS, 0:P])

                def keys_out(X):
                    b, b2 = cb(f"k{X}", i), cb(f"ks{X}", i)
                    act.wait_ge(bank_free[b.slot], b.read)
                    act.dma_start(p_k[0, 0, :, ds(2 * i + X, 1), :].rearrange("(t p) a d -> p t (a d)", p=P),
                                  kN[:, 0:TT, :]).then_inc(kn_sent, 16)
                    act.wait_ge(bank_free[b2.slot], b2.read)
                    act.dma_start(s_k[0, :, :, ds(2 * i + X, 1), :].rearrange("b t a d -> (b t) (a d)"),
                                  kN[0:NS, TT, :]).then_inc(kn_sent, 16)

                def sample_part(dst, X, src):
                    act.activation(dst[:, ds(2 * i + X, 1), :].rearrange("p a t -> p (a t)"), src[:, X, NP_:T], ACT.Copy)

                def exps(X):
                    for t in range(TT):
                        b = cb(f"S{t}{X}", i)
                        act.wait_ge(bank_free[b.slot], b.read)
                        pr = prob[:, TRI[t]:TRI[t + 1]]
                        act.activation(pr, pr, ACT.Exp, bias=stat[:, t:t + 1], scale=-1.0,
                                       accum_out=stat[:, 8 + t:9 + t]).then_inc(exp_ready, 1)

                def probs_turned(X, tiles):
                    for t in tiles:
                        b = cb(f"P{t}{X}", i)
                        src = bank_wait(act, b)
                        if t >= 2:
                            bank_wait(act, cb(f"O{t - 2}{X}", i))
                        out_of(b, probT[:, t % 2, 0:t + 1, :].rearrange("p s t -> p (s t)"), src[:, 0:(t + 1) * P])

                for j in range(8):
                    high(TILE_C + j + 2, 0, i, 8)
                    if j in (1, 2):
                        values(j - 1)
                    if j == 3:
                        act.wait_ge(gate_ready, 2 * i + 1)
                        sample_part(gateS, 0, gate)
                    if j == 4:
                        keys(0)
                        sample_part(kS, 0, kT)
                        keys_out(0)
                    if j == 5:
                        act.wait_ge(head_ready, 4 * i + 3)
                        sample_part(qS, 0, qT)
                        exps(0)
                    if j == 6:
                        keys(1)
                        probs_turned(0, (0, 1))
                        sample_part(kS, 1, kT)
                        keys_out(1)
                    if j == 7:
                        act.wait_ge(head_ready, 4 * i + 5)
                        sample_part(qS, 1, qT)
                        exps(1)
                    src, copied = projected(TILE_C + j, i, 8)
                    if j in (2, 7):
                        act.activation(halves(tanhC[:]), src, ACT.Tanh, scale=0.5)
                    dst = {0: raw[:, 0], 1: raw[:, 1], 2: raw[:, 0], 3: kT[:, 0], 4: qT[:, 0], 5: kT[:, 1],
                           6: qT[:, 1], 7: raw[:, 1]}[j]
                    act.activation(halves(dst), src, ACT.Copy).then_inc(copied, 1)
                    if j == 6:
                        probs_turned(0, (2, 3))
                    if j == 7:
                        probs_turned(1, (0, 1))
                    high(TILE_C + j + 2, 1, i, 8)
                probs_turned(1, (2, 3))
                act.wait_ge(gate_ready, 2 * i + 2)
                sample_part(gateS, 1, gate)
            for t in range(TT):
                b = cb(f"O{t}1", 3)
                act.wait_ge(bank_free[b.slot], b.read)
            act.wait_ge(kn_sent, 32 * (H + 1))
            for X in range(2):
                act.wait_ge(vn_sent[X], 32 * (H // 2 + 1))
            act.activation(stat[:, 30:31], halfscale[:, 0:1], ACT.Copy).then_inc(c_done, 1)
            act.wait_ge(drop_ready, 1)
            act.dma_start(dropD, scoreS[:]).then_inc(drop_out, 16)

            with act.Fori(0, GROUPS) as g:
                def keys_copied(X, lo, hi):
                    for n in range(lo, hi, 2):
                        b = bb(f"K{n}{'ab'[X]}", g)
                        out_of(b, kPT[:, 1, :, :].rearrange("p h k -> p (h k)"), bank_wait(act, b)[:])

                def sample_view(ap, lo, hi):
                    return ap[:, HIST + NP_:UW].rearrange("p (b r) -> p b r", b=NB)[:, :, lo:hi]

                def history(t):
                    b = bb(f"h{t}", g)
                    src = bank_wait(act, b)[:, 0:NB * HIST].rearrange("p (b r) -> p b r", b=NB)
                    act.wait_ge(pooled_ready, 2 * g + t + 1)
                    out_of(b, sample_view(U[:, t], 0, HIST), src)

                def copy_tile(t):
                    src, copied = projected(TILE_B + t, g, 4)
                    if t < 2:
                        if t == 0:
                            bank_wait(act, bb("m1s", g, ago=1))
                        act.activation(U[:, t, HIST:HIST + HT], src[:, 0, :], ACT.Copy)
                        act.activation(U[:, t, HIST + HT:HIST + NP_], src[:, 1, 0:NP_ - HT], ACT.Copy)
                        act.activation(newU[:, t, :], src[:, 1, NP_ - HT:HT], ACT.Copy)
                        act.activation(sample_view(U[:, t], HIST, UE),
                                       src[:, 1, NP_ - HT:HT].rearrange("p (b r) -> p b r", b=NB),
                                       ACT.Copy).then_inc(copied, 1)
                    else:
                        if t == 3:
                            act.wait_ge(gate_ready, H + 2 * g + 1)
                        act.activation(halves(rot[:]), src, ACT.Tanh, scale=0.5)
                        act.activation(halves(raw[:, t - 2]), src, ACT.Copy).then_inc(copied, 1)

                def last_rows(t):
                    b = bb(f"u{t}", g)
                    src = bank_wait(act, b)
                    act.wait_ge(un_sent, 64 * g + 32 * t + 32)
                    act.activation(uN[0:HIST, 0, :], src[0:HIST, 0:P], ACT.Copy)
                    out_of(b, uN[:, 1, :], src[0:NS, P:2 * P])
                    act.wait_ge(bank_free[b.slot], b.read)
                    col = ds((2 * g + t) * P, P)
                    act.dma_start(p_pool[0, 0, :, col], uN[0:HIST, 0, :]).then_inc(un_sent, 16)
                    act.dma_start(s_pool[0, :, HIST - NT:HIST, col], uN[:, 1, :]).then_inc(un_sent, 16)

                for X in range(2):
                    keys_copied(X, 1, 9)
                    if X == 0:
                        history(0)
                    else:
                        last_rows(1)
                    high(TILE_B + 2 * X + 2, 0, g, 4)
                    keys_copied(X, 9, 13)
                    if X == 0:
                        history(1)
                    keys_copied(X, 13, 16)
                    act.wait_ge(max_ready, 2 * g + X + 1)
                    act.activation(probS[:], probS[:], ACT.Exp, bias=stat[0:NS, 20:21], scale=-1.0,
                                   accum_out=stat[0:NS, 21:22]).then_inc(exps_ready, 1)
                    copy_tile(2 * X)
                    high(TILE_B + 2 * X + 2, 1, g, 4)
                    if X == 0:
                        last_rows(0)
                    b = bb(f"Pt{'ab'[X]}", g)
                    src = bank_wait(act, b)
                    act.activation(probST[:].rearrange("p a t -> p (a t)"), src[:, 0:PAGES * NS], ACT.Copy)
                    out_of(b, probSTn[:], src[0:NS, PAGES * NS:(PAGES + 1) * NS])
                    high(TILE_B + 2 * X + 3, 0, g, 4)
                    for half in range(2):
                        b = b67(f"O{half}{'ab'[X]}", g)
                        out_of(b, outS[:, 4 * half:4 * half + 4, :].rearrange("p h d -> p (h d)"),
                               bank_wait(act, b)[0:NT, :])
                    copy_tile(2 * X + 1)
                    high(TILE_B + 2 * X + 3, 1, g, 4)

            for name in ("m1p", "m1s"):
                b = bb(name, GROUPS - 1)
                act.wait_ge(bank_free[b.slot], b.read)
            b = bb("OTb", GROUPS - 1)
            act.wait_ge(bank_free[b.slot], b.read)
            for k in range(KC):
                act.activation(actH[:, k, :], mixed[:, k, :], ACT.Copy).then_inc(mix_high, 1)
            with act.Fori(0, 7) as i:
                for j in range(2):
                    high(TILE_D + j + 2, 0, i, 2)
                    src, copied = projected(TILE_D + j, i, 2)
                    act.activation(halves(raw[:, j]), src, ACT.Copy).then_inc(copied, 1)
                    high(TILE_D + j + 2, 1, i, 2)
            for j in range(2):
                src, copied = projected(TILE_D + 14 + j)
                act.activation(halves(raw[:, j]), src, ACT.Copy).then_inc(copied, 1)
            act.wait_ge(var_ready, 1)
            act.activation(std[:], mv[:, :, 1], ACT.Sqrt).then_inc(std_ready, 1)
            act.wait_ge(var_ready, 2)
            for t in range(TT + 1):
                n = P if t < TT else NS
                act.activation(y[0:n, t, :], y[0:n, t, :], ACT.Identity, bias=stat[0:n, 8 + t:9 + t],
                               scale=stat[0:n, t:t + 1]).then_inc(norm_ready, 1)

        @block.tensor
        def _(pe):
            for s in (*stage_ready, *stage_free, *acc_copied, *bank_free.values(), *v_free):
                pe.sem_inc(s, 1)
            pe.sem_inc(head_ready, 1)
            for s in (pooled_ready,):
                pe.sem_inc(s, 2)
            for s in (*vn_sent, kn_sent, un_sent):
                pe.sem_inc(s, 32)

            def unit(tile, half, i=None, per=0, width=P, quarters=(0, 1), chunk_ready=None):
                t, u = turn(tile, 2, i, per), turn(2 * tile + half, 4, i, 2 * per)
                if 0 in quarters:
                    pe.wait_ge(stage_ready[u.slot], u.read)
                    if half == 0:
                        pe.wait_ge(acc_copied[t.slot], t.free)
                for q in quarters:
                    for k in range(q * HU // 2, (q + 1) * HU // 2):
                        kk = half * HU + k
                        if chunk_ready is not None:
                            pe.wait_ge(chunk_ready, kk + 1)
                        for w, parts in ((wH, (actH, actL)), (wL, (actH,))):
                            for a in parts:
                                for e in range(2):
                                    last = pe.matmul(acc[t.slot][0:width, e, 0:HT], w[:, u.slot, k, 0:width],
                                                     a[:, kk, e * HT:(e + 1) * HT], start=(kk == 0 and w is wH and a is actH),
                                                     stop=(kk == KC - 1 and w is wL))
                if 1 in quarters:
                    last.then_inc(tile_ready[t.slot] if half else stage_free[t.slot], 1)

            def take(b):
                pe.wait_ge(bank_free[b.slot], b.free)
                return bank[b.slot]

            def full(b, last):
                last.then_inc(bank_full[b.slot], 1)

            def copied(tile, i=None, per=0):
                t = turn(tile, 2, i, per)
                pe.wait_ge(acc_copied[t.slot], t.read)

            pe.wait_ge(square_in, 16)
            for t in range(TT + 1):
                n = P if t < TT else NS
                if t < TT:
                    pe.wait_ge(x_in[t], 16)
                else:
                    pe.wait_ge(xs_in, 16)
                src = xnat[:, t, :] if t < TT else xnatS[:, :]
                for q in range(4):
                    b = xb(f"x{t}{q}")
                    dst = take(b)
                    for j in range(4):
                        last = pe.transpose(dst[:, j * n:(j + 1) * n], src[:, (4 * q + j) * P:(4 * q + j + 1) * P],
                                            ident[0:n, 0:n])
                    full(b, last)
            for q in range(4):
                b = xb(f"x{TT}{q}")
                pe.wait_ge(bank_free[b.slot], b.read)

            for half in range(2):
                unit(0, half, width=KW)
            b = ab("wi")
            dst = take(b)
            copied(0)
            for t in range(1, TT):
                last = pe.transpose(dst[:, (t - 1) * IH:t * IH], wiT[ID:KW, t * P:(t + 1) * P], ident[ID:KW, ID:KW])
            full(b, last)

            def index_products(bank_of, names, slot):
                for name in names:
                    e, t = int(name[-2]), int(name[-1])
                    b = bank_of(name)
                    part = slice(ID * e, ID * e + ID)
                    full(b, pe.matmul(take(b)[:, 0:(t + 1) * P], raw[part, slot, t * P:(t + 1) * P],
                                      kiT[part, 0:(t + 1) * P], start=True, stop=True))

            with pe.Fori(0, 4) as i:
                for j in range(2):
                    unit(TILE_A + j, 0, i, 2)
                    if j == 0:
                        pe.wait_ge(ki_twice, 16)
                    pe.wait_ge(qi_ready, 2 * i + j + 1)
                    index_products(lambda name: rb(name, i), rt(f"r{j}"), 1 - j)
                    unit(TILE_A + j, 1, i, 2)

            def pages_turned(n):
                b = zb(f"T{n}")
                dst = take(b)
                for a in range(PAGES // 2):
                    at = n * PAGES + 2 * a
                    last = pe.transpose(dst[:, a * P:(a + 1) * P], kiPage[:, at:at + 2, :].rearrange("p a d -> p (a d)"), ident)
                full(b, last)

            pe.wait_ge(kip_in, 16 * NB * PAGES)
            for n in range(2):
                pages_turned(n)
            b = zb("ki")
            dst = take(b)
            for t in range(TT):
                last = pe.transpose(dst[:, t * ID:(t + 1) * ID], kiT[0:ID, t * P:(t + 1) * P], ident[0:ID, 0:ID])
            full(b, last)
            b = zb("kis")
            full(b, pe.transpose(take(b)[0:NS, 0:ID], kiT[0:ID, NP_:T], ident[0:ID, 0:ID]))
            pe.wait_ge(qi_ready, H + 1)
            index_products(zb, rt("z"), 1)
            pe.wait_ge(qis_near, 1)
            pe.wait_ge(qis_far, 32)
            for n in range(NB):
                b, b2 = zb(f"T{n}"), zb(f"R{n}")
                dst = take(b2)
                pe.wait_ge(bank_free[b.slot], b.read)
                for a in range(PAGES // 2):
                    last = pe.matmul(dst[:, a * P:(a + 1) * P], kiPT[:, n % 2, a, :],
                                     qiS[:, :, :, n * NT:(n + 1) * NT].rearrange("p e h t -> p (e h) t"),
                                     start=True, stop=True)
                full(b2, last)
                if n + 2 < NB:
                    pages_turned(n + 2)
            b = nb("Rn")
            full(b, pe.matmul(take(b)[0:NS, :], kiT[0:ID, NP_:T],
                              qiS[0:ID, 0, :, :].rearrange("p h t -> p (h t)"), start=True, stop=True))
            pe.wait_ge(bank_free[b.slot], b.read)
            for half in range(2):
                b = nb(f"S{half}")
                dst = take(b)
                for p in range(4):
                    last = pe.transpose(dst[0:NS, p * P:(p + 1) * P], scoreST[:, 4 * half + p, :], ident)
                full(b, last)
            b = nb("Sn")
            full(b, pe.transpose(take(b)[0:NS, 0:NS], scoreSTn[:], ident[0:NS, 0:NS]))

            with pe.Fori(0, 4) as i:
                def by_token(name, X, src):
                    b = cb(f"{name}{X}", i)
                    dst = take(b)
                    for t in range(TT):
                        last = pe.transpose(dst[:, t * P:(t + 1) * P], src[:, t * P:(t + 1) * P], ident)
                    full(b, last)
                    b = cb(f"{name}s{X}", i)
                    full(b, pe.transpose(take(b)[0:NS, 0:P], src[:, NP_:T], ident))

                def scores(X):
                    for t in range(TT):
                        b = cb(f"S{t}{X}", i)
                        full(b, pe.matmul(take(b)[:, 0:(t + 1) * P], qT[:, X, t * P:(t + 1) * P],
                                          kT[:, X, 0:(t + 1) * P], start=True, stop=True))

                def turned(X, t):
                    b = cb(f"P{t}{X}", i)
                    dst = take(b)
                    pe.wait_ge(prob_ready, 8 * i + 4 * X + t + 1)
                    for s in range(t + 1):
                        last = pe.transpose(dst[:, s * P:(s + 1) * P], prob[:, TRI[t] + s * P:TRI[t] + (s + 1) * P], ident)
                    full(b, last)

                def values_of(X, t):
                    bv, bp, b = cb(f"v{X}", i), cb(f"P{t}{X}", i), cb(f"O{t}{X}", i)
                    dst = take(b)
                    pe.wait_ge(bank_free[bv.slot], bv.read)
                    pe.wait_ge(bank_free[bp.slot], bp.read)
                    for s in range(t + 1):
                        last = pe.matmul(dst[:, 0:P], vN[:, X, s, :], probT[:, t % 2, s, :],
                                         start=(s == 0), stop=(s == t))
                    full(b, last)

                for j in range(8):
                    unit(TILE_C + j, 0, i, 8)
                    if j in (1, 2):
                        copied(TILE_C + j - 1, i, 8)
                        by_token("v", j - 1, raw[:, j - 1])
                    if j == 4:
                        pe.wait_ge(head_ready, 4 * i + 2)
                        by_token("k", 0, kT[:, 0])
                    if j == 5:
                        pe.wait_ge(head_ready, 4 * i + 3)
                        scores(0)
                    if j == 6:
                        pe.wait_ge(head_ready, 4 * i + 4)
                        by_token("k", 1, kT[:, 1])
                        turned(0, 0)
                        turned(0, 1)
                    if j == 7:
                        values_of(0, 2)
                        values_of(0, 3)
                        pe.wait_ge(head_ready, 4 * i + 5)
                        scores(1)
                    unit(TILE_C + j, 1, i, 8)
                    if j == 6:
                        values_of(0, 0)
                        turned(0, 2)
                        values_of(0, 1)
                        turned(0, 3)
                turned(1, 0)
                turned(1, 1)
                values_of(1, 0)
                turned(1, 2)
                values_of(1, 1)
                turned(1, 3)
                values_of(1, 2)
                values_of(1, 3)
            with pe.Fori(0, GROUPS) as g:
                def quarter(X, n):
                    unit(TILE_B + 2 * X + n // 4, n // 2 % 2, g, 4, quarters=(n % 2,))

                def key_pages(X, beside):
                    def turned(n):
                        pair, hp = n // 4, n % 4
                        k = turn(4 * X + pair, 2, g, 8)
                        if hp == 0:
                            pe.wait_ge(k_in[k.slot], 32 * k.full)
                        b = bb(f"K{n}{'ab'[X]}", g)
                        dst = take(b)
                        for e in range(2):
                            for a in range(2):
                                last = pe.transpose(dst[:, (2 * e + a) * P:(2 * e + a + 1) * P],
                                                    kPage[:, 1 - k.slot, a, 2 * hp + e, :], ident)
                        full(b, last)

                    def products(n):
                        pair, hp = n // 4, n % 4
                        b, st = bb(f"K{n}{'ab'[X]}", g), b67(f"S{pair // 2}{'ab'[X]}", g)
                        pe.wait_ge(bank_free[b.slot], b.read)
                        if n == 0:
                            pe.wait_ge(pad_ready, 2 * g + X + 1)
                        if n % 8 == 0:
                            take(st)
                        for e in range(2):
                            h = 2 * hp + e
                            last = pe.matmul(bank[st.slot][0:NS, pair % 2 * 256:pair % 2 * 256 + 256],
                                             qPad[:, X, h * NS:(h + 1) * NS], kPT[:, n % 2, e, :],
                                             start=(h == 0), stop=(h == H - 1))
                        if n % 8 == 7:
                            full(st, last)

                    turned(0)
                    for n in range(16):
                        if n + 1 < 16:
                            turned(n + 1)
                        beside(n)
                        products(n)

                def new_keys(X):
                    b = bb(f"Sn{'ab'[X]}", g)
                    dst = take(b)
                    for h in range(H):
                        last = pe.matmul(dst[0:NS, 0:NS], qPad[:, X, h * NS:(h + 1) * NS], kS[:, h, :],
                                         start=(h == 0), stop=(h == H - 1))
                    full(b, last)

                def probs_turned(X):
                    b = bb(f"Pt{'ab'[X]}", g)
                    dst = take(b)
                    pe.wait_ge(probS_ready, 2 * g + X + 1)
                    stand_alone(pe)
                    for p in range(PAGES):
                        pe.transpose(dst[:, p * NS:(p + 1) * NS], probS[:, p * P:(p + 1) * P], ident[0:NS, 0:NS])
                    full(b, pe.transpose(dst[0:NS, PAGES * NS:(PAGES + 1) * NS], probS[:, PAST:L], ident[0:NS, 0:NS]))

                def value_pages(X, lo, hi):
                    outs = [b67(f"O{half}{'ab'[X]}", g) for half in range(2)]

                    def products(h, probs, values, start, stop):
                        return pe.matmul(bank[outs[h // 4].slot][0:NT, h % 4 * P:(h % 4 + 1) * P], probs, values,
                                         start=start and h % 4 == 0, stop=stop and h % 4 == 3, skip_group_check=True)

                    if lo == 0:
                        for b in outs:
                            take(b)
                        bp = bb(f"Pt{'ab'[X]}", g)
                        pe.wait_ge(bank_free[bp.slot], bp.read)
                    for p in range(lo, hi):
                        v = turn(8 * X + p, 4, g, 16)
                        pe.wait_ge(v_in[v.slot], 16 * v.full)
                        for h in range(H):
                            last = products(h, probST[:, p, h * NT:(h + 1) * NT], vPage[:, v.slot, h, :], p == 0, False)
                        last.then_inc(v_free[v.slot], 1)
                    if hi == PAGES:
                        for h in range(H):
                            last = products(h, probSTn[:, h * NT:(h + 1) * NT], vS[:, h, :], False, True)
                            if h % 4 == 3:
                                full(outs[h // 4], last)

                def output_turned(X):
                    b = bb(f"OT{'ab'[X]}", g)
                    dst = take(b)
                    for half in range(2):
                        o = b67(f"O{half}{'ab'[X]}", g)
                        pe.wait_ge(bank_free[o.slot], o.read)
                    stand_alone(pe)
                    for h in range(H):
                        last = pe.transpose(dst[:, h * NT:(h + 1) * NT], outS[:, h, :], ident[0:NT, 0:NT])
                    full(b, last)

                def history(t):
                    b = bb(f"h{t}", g)
                    dst = take(b)
                    pe.wait_ge(hist_in[t], 16 * g + 16)
                    full(b, pe.transpose(dst[:, 0:NB * HIST], hist[:, t, :], ident[0:NB * HIST, 0:NB * HIST]))

                def last_rows(t):
                    b = bb(f"u{t}", g)
                    dst = take(b)
                    copied(TILE_B + t, g, 4)
                    pe.transpose(dst[0:HIST, 0:P], U[:, t, NP_:NP_ + HIST], ident)
                    full(b, pe.transpose(dst[0:NS, P:2 * P], newU[:, t, :], ident))

                for X in range(2):
                    def beside(n):
                        if n in (3, 7, 11):
                            quarter(X, n // 4)
                        if n == 7 and X == 0:
                            history(0)
                        if n == 7 and X == 1:
                            last_rows(1)
                        if n == 11 and X == 0:
                            history(1)

                    key_pages(X, beside)
                    new_keys(X)
                    quarter(X, 3)
                    quarter(X, 4)
                    if X == 0:
                        last_rows(0)
                    probs_turned(X)
                    quarter(X, 5)
                    value_pages(X, 0, 4)
                    quarter(X, 6)
                    value_pages(X, 4, 8)
                    quarter(X, 7)
                    output_turned(X)
                pe.wait_ge(pooled_ready, 2 * g + 4)
                pe.wait_ge(wp_in, 16 * g + 16)
                for e in range(2):
                    for part, values in (("p", U[:, :, HIST:HIST + NP_]), ("s", pooledS[:])):
                        b = bb(f"m{e}{part}", g)
                        dst = take(b)
                        n = values.shape[-1]
                        for c in range(2):
                            last = pe.matmul(dst[:, 0:n], wp[:, c, e * P:(e + 1) * P], values[:, c, :],
                                             start=(c == 0), stop=(c == 1))
                        full(b, last)

            def rows(j, i):
                copied(TILE_D + j, i, 2)
                b = yb(f"yp{j}", i)
                dst = take(b)
                for t in range(TT):
                    last = pe.transpose(dst[:, t * P:(t + 1) * P], raw[:, j, t * P:(t + 1) * P], ident)
                full(b, last)
                b = yb(f"ys{j}", i)
                full(b, pe.transpose(take(b)[0:NS, 0:P], raw[:, j, NP_:T], ident))

            for half in range(2):
                unit(TILE_D, half, chunk_ready=mix_low)
            with pe.Fori(0, 7) as i:
                for j in range(2):
                    unit(TILE_D + j + 1, 0, i, 2)
                    rows(j, i)
                    unit(TILE_D + j + 1, 1, i, 2)
            unit(TILE_D + KC - 1, 0)
            rows(0, 7)
            unit(TILE_D + KC - 1, 1)
            rows(1, 7)

        @block.vector
        def _(dve):
            own = Steps(dve, dve_steps)

            n = 0
            for t in range(TT + 1):
                m = P if t < TT else NS
                for q in range(4):
                    n += 1
                    b = xb(f"x{t}{q}")
                    dve.wait_ge(x_high, n)
                    at = (slice(None), slice(4 * q, 4 * q + 4), slice(t * P, t * P + m))
                    dve.tensor_tensor(actL[at], bank[b.slot][:, 0:4 * m].rearrange("p (k t) -> p k t", k=4),
                                      actH[at].bitcast(F32), ALU.subtract).then_inc(bank_free[b.slot], 1)

            def rotate(dst, src, rows, table, swap):
                half = rot[0:rows, :]
                stand_alone(dve)
                own.step(dve.stream_shuffle(half, src, swap))
                own.wait()
                own.step(dve.tensor_tensor(half, half, table[0:rows, 1, :], ALU.mult))
                own.step(dve.tensor_tensor(src, src, table[0:rows, 0, :], ALU.mult))
                own.wait()
                return dve.tensor_tensor(dst, src, half, ALU.add)

            def copied(tile, i=None, per=0):
                t = turn(tile, 2, i, per)
                dve.wait_ge(acc_copied[t.slot], t.read)

            copied(0)
            dve.wait_ge(irot_in, 16)
            rotate(kiT[0:ID, :], kiT[0:ID, :], ID, irot, SWAP_I).then_inc(ki_ready, 1)
            own.step(dve.memset(qiS[:], 0.0))
            own.step(dve.memset(scoreP[:], 0.0))
            own.step(dve.memset(wiN[:, :, 0:2], 0.0))
            dve.memset(raw[:, 1, :], 0.0).then_inc(qi_ready, 1)
            dve.wait_ge(ki_ready, 1)
            b = ab("wi")
            dve.tensor_copy(wiN[:, :, 2:2 + IH], bank_wait(dve, b)[:, 0:3 * IH].rearrange("p (t h) -> p t h", t=3)
                            ).then_inc(bank_free[b.slot], 1)
            dve.wait_ge(bank_free[b.slot], b.read)
            own.wait()

            def add_head(b, before, t, r, h):
                sc = scoreP[:, TRI[t] - P:TRI[t + 1] - P]
                dve.wait_ge(relu_full[r.slot], r.full)
                dve.wait_ge(bank_free[before.slot], before.read)
                dve.scalar_tensor_tensor(sc, relu[:, r.slot, 0:(t + 1) * P], wiN[:, t - 1, ds(h, 1)], sc, ALU.mult, ALU.add
                                         ).then_inc(bank_free[b.slot], 1)

            with dve.Fori(0, 4) as i:
                own.enter(i, 8)
                names = rt("r0") + rt("r1")
                for j in range(2):
                    for n in range(6 * j, 6 * j + 6):
                        before = rb(names[n - 3], i) if n >= 3 else rb(names[n + 9], i, ago=1)
                        add_head(rb(names[n], i), before, int(names[n][-1]), turn(n, 2, i, 12),
                                 4 * i + (2 * j + int(names[n][-2])))
                    copied(TILE_A + j, i, 2)
                    own.step(rotate(raw[:, j], raw[:, j], P, irot, SWAP_I))
                    own.wait()
                    dve.tensor_copy(qiN[:, ds(2 * i + j, 1), :].rearrange("p a t -> p (a t)"), raw[:, j, NP_:T]
                                    ).then_inc(qi_ready, 1)
                own.leave(4)
            dve.wait_ge(qi_ready, H + 1)
            own.step(dve.tensor_copy(qiS[0:ID, 0, 0:IH:2, :], qiN[0:ID]))
            dve.tensor_copy(qiS[ID:P, 1, 1:IH:2, :], qiN[ID:P]).then_inc(qis_near, 1)
            behind = [rb(name, 3) for name in rt("r1")[-3:]]
            for n, name in enumerate(rt("z")):
                behind.append(zb(name))
                add_head(zb(name), behind[n], int(name[-1]), turn(RT + n, 2), IH + int(name[-2]))
            for b in behind[-3:]:
                dve.wait_ge(bank_free[b.slot], b.read)
            for t in (1, 2, 3):
                at = TRI[t + 1] - 2 * P
                own.step(dve.tensor_tensor(scoreP[:, at:at + P], scoreP[:, at:at + P], causal, ALU.add))

            EARLY = (0, 2, 4)

            def pick_prompt():
                tiles = [scoreP[:, TRI[t] - P:TRI[t + 1] - P] for t in (1, 2, 3)]
                own.wait()
                stand_alone(dve)
                for n, sc in enumerate(tiles):
                    own.step(dve.max(top8[:, n, :], sc))
                own.wait()
                stand_alone(dve)
                for n, sc in enumerate(tiles):
                    own.step(dve.match_replace(sc, top8[:, n, :], sc, PICKED))

            dve.wait_ge(wi_back, 16)
            for n in range(NB):
                r, b = turn(RS + n, 2), zb(f"R{n}")
                dve.wait_ge(relu_full[r.slot], r.full)
                cols = slice(n * NT, (n + 1) * NT)
                v = relu[:, r.slot, :].rearrange("p (g h t) -> p g h t", g=PAGES, h=IH)
                own.step(dve.tensor_tensor(v, v, wiB[:, :, cols].unsqueeze(1).to_broadcast([P, PAGES, IH, NT]), ALU.mult))
                own.wait()
                dve.tensor_reduce(scoreST[:, :, cols], v.rearrange("p g h t -> p g t h"), AX.X, ALU.add
                                  ).then_inc(bank_free[b.slot], 1)
                if n in EARLY:
                    pick_prompt()
            r = turn(RS + NB, 2)
            dve.wait_ge(relu_full[r.slot], r.full)
            v = relu[0:NS, r.slot, :].rearrange("p (h t) -> p h t", h=IH)
            own.step(dve.tensor_tensor(v, v, wiB[0:NS], ALU.mult))
            own.wait()
            b = nb("Rn")
            dve.tensor_reduce(scoreSTn[:], v.rearrange("p h t -> p t h"), AX.X, ALU.add).then_inc(bank_free[b.slot], 1)
            for half in range(2):
                b = nb(f"S{half}")
                dve.tensor_copy(scoreS[:, 512 * half:512 * (half + 1)], bank_wait(dve, b)[0:NS, :]
                                ).then_inc(bank_free[b.slot], 1)
            b = nb("Sn")
            dve.tensor_tensor(scoreS[:, PAST:L], bank_wait(dve, b)[0:NS, 0:NS], newmask, ALU.add
                              ).then_inc(bank_free[b.slot], 1)
            dve.wait_ge(bank_free[b.slot], b.read)

            def pick(scores, top):
                own.wait()
                stand_alone(dve)
                own.step(dve.max(top, scores))
                own.wait()
                stand_alone(dve)
                own.step(dve.match_replace(scores, top, scores, PICKED))

            with dve.Fori(0, TOPK_P // ROUND - len(EARLY)) as i:
                own.enter(i, 6)
                pick_prompt()
                own.leave(TOPK_P // ROUND - len(EARLY))
            own.wait()
            own.step(dve.tensor_scalar(keepP[:, P:TRI[4]], scoreP[:], PICKED / 1.5, MASKED, ALU.is_gt, ALU.mult))
            own.step(dve.tensor_copy(keepP[:, 0:P], causal))
            dve.wait_ge(consts_in, 32)
            own.step(dve.tensor_scalar(halfscale[:], halfscale[:], 0.5, None, ALU.mult))

            rounds = TOPK_S // ROUND // 4
            with dve.Fori(0, 4) as i:
                own.enter(i, 2 * rounds + 4 * 3 + 8)

                def make_gate(X):
                    dve.scalar_tensor_tensor(gate[:, X, :], tanhC[:], 1.0, raw[:, X, :], ALU.add, ALU.mult
                                             ).then_inc(gate_ready, 1)

                def softmax(X):
                    for t in range(TT):
                        b = cb(f"S{t}{X}", i)
                        src = bank_wait(dve, b)
                        stand_alone(dve)
                        dve.tensor_tensor_reduce(prob[:, TRI[t]:TRI[t + 1]], src[:, 0:(t + 1) * P],
                                                 keepP[:, TRI[t]:TRI[t + 1]], -SCALE, 3e38, ALU.add, ALU.min,
                                                 stat[:, t:t + 1]).then_inc(bank_free[b.slot], 1)
                    for t in range(TT):
                        dve.wait_ge(exp_ready, 8 * i + 4 * X + t + 1)
                        own.step(dve.reciprocal(stat[:, 16 + t:17 + t], stat[:, 8 + t:9 + t]))
                        own.wait()
                        pr = prob[:, TRI[t]:TRI[t + 1]]
                        dve.tensor_scalar(pr, pr, stat[:, 16 + t:17 + t], None, ALU.mult).then_inc(prob_ready, 1)

                def gated(X, tiles):
                    for t in tiles:
                        b = cb(f"O{t}{X}", i)
                        cols = slice(t * P, (t + 1) * P)
                        dve.scalar_tensor_tensor(mixed[:, ds(2 * i + X, 1), cols].rearrange("p a t -> p (a t)"),
                                                 bank_wait(dve, b)[:, 0:P], 0.5, gate[:, X, cols],
                                                 ALU.mult, ALU.mult).then_inc(bank_free[b.slot], 1)

                def rotated(j, dst, X):
                    copied(TILE_C + j, i, 8)
                    dve.wait_ge(head_ready, 4 * i + j - 2)
                    rotate(dst[0:32, X, :], dst[0:32, X, :], 32, headrot, SWAP_H).then_inc(head_ready, 1)

                def pick_keys(n):
                    for _ in range(n):
                        pick(scoreS[:], top8[0:NS, 0, :])

                copied(TILE_C + 2, i, 8)
                make_gate(0)
                pick_keys(3)
                rotated(3, kT, 0)
                pick_keys(3)
                rotated(4, qT, 0)
                pick_keys(rounds - 6)
                softmax(0)
                rotated(5, kT, 1)
                dve.wait_ge(gate_ready, 2 * i + 1)
                gated(0, (0, 1))
                rotated(6, qT, 1)
                gated(0, (2, 3))
                softmax(1)
                copied(TILE_C + 7, i, 8)
                make_gate(1)
                dve.wait_ge(gate_ready, 2 * i + 2)
                gated(1, range(TT))
                own.leave(4)
            own.wait()
            dve.tensor_scalar(scoreS[:], scoreS[:], PICKED / 1.5, MASKED, ALU.is_gt, ALU.mult).then_inc(drop_ready, 1)
            dve.wait_ge(c_done, 1)
            own.step(dve.memset(U[:, :, 0:HIST], 0.0))
            own.step(dve.memset(qPad[:], 0.0))
            own.wait()
            with dve.Fori(0, GROUPS) as g:
                own.enter(g, 2 * 6)

                def queries(X):
                    dve.tensor_copy(qPad[:, X, :].rearrange("p (h c) -> p h c", h=H)[:, :, 0:NT],
                                    qS[:, :, ds((2 * g + X) * NT, NT)]).then_inc(pad_ready, 1)

                def keys_copied(X):
                    for n in range(0, 16, 2):
                        b = bb(f"K{n}{'ab'[X]}", g)
                        dve.tensor_copy(kPT[:, 0, :, :].rearrange("p h k -> p (h k)"), bank_wait(dve, b)[:]
                                        ).then_inc(bank_free[b.slot], 1)

                def softmax(X):
                    dve.wait_ge(mask_in[X], 16 * g + 16)
                    parts = ((b67(f"S0{'ab'[X]}", g), 0, 512), (b67(f"S1{'ab'[X]}", g), 512, PAST), (bb(f"Sn{'ab'[X]}", g), PAST, L))
                    for n, (b, lo, hi) in enumerate(parts):
                        src = bank_wait(dve, b)
                        stand_alone(dve)
                        dve.tensor_tensor_reduce(probS[:, lo:hi], src[0:NS, 0:hi - lo], probS[:, lo:hi], -SCALE, 3e38,
                                                 ALU.add, ALU.min, stat[0:NS, 16 + n:17 + n]).then_inc(bank_free[b.slot], 1)
                    dve.wait_ge(bank_free[b.slot], b.read)
                    dve.tensor_reduce(stat[0:NS, 20:21], stat[0:NS, 16:19], AX.X, ALU.min).then_inc(max_ready, 1)
                    dve.wait_ge(exps_ready, 2 * g + X + 1)
                    own.step(dve.reciprocal(stat[0:NS, 22:23], stat[0:NS, 21:22]))
                    own.wait()
                    dve.tensor_scalar(probS[:], probS[:], stat[0:NS, 22:23], None, ALU.mult
                                      ).then_inc(probS_ready, 1)

                def pool_inputs(t):
                    copied(TILE_B + t, g, 4)
                    dve.wait_ge(wtab_in, 16)
                    u, src = U[:, t, :], U[:, t, :]
                    for lv in range(4):
                        lo, w = (2 << lv) - 1, 1 << lv
                        dst = win[:, lv % 2, :]
                        own.step(dve.scalar_tensor_tensor(dst[:, lo:UW], src[:, lo - w:UW - w], wtab[:, ds(g * WT + lv, 1)],
                                                          src[:, lo:UW], ALU.mult, ALU.add))
                        own.wait()
                        src = dst
                    inv = wtab[:, ds(g * WT + 4, 1)]
                    samples = lambda ap: ap[:, HIST + NP_:UW].rearrange("p (b r) -> p b r", b=NB)[:, :, HIST:UE]
                    dve.scalar_tensor_tensor(pooledS[:, t, :].rearrange("p (b r) -> p b r", b=NB),
                                             samples(src), inv, samples(u), ALU.mult, ALU.subtract)
                    b = bb(f"u{t}", g)
                    dve.wait_ge(bank_full[b.slot], b.full)
                    dve.scalar_tensor_tensor(u[:, 2 * HIST:HIST + NP_], src[:, 2 * HIST:HIST + NP_], inv,
                                             u[:, 2 * HIST:HIST + NP_], ALU.mult, ALU.subtract)
                    first = win[:, 0, HIST:2 * HIST]
                    own.step(dve.tensor_tensor(first, src[:, HIST:2 * HIST], wtab[:, ds(g * WT + 5, HIST)], ALU.mult))
                    own.wait()
                    dve.tensor_tensor(u[:, HIST:2 * HIST], first, u[:, HIST:2 * HIST], ALU.subtract
                                      ).then_inc(pooled_ready, 1)

                def make_gate(t):
                    copied(TILE_B + 2 + t, g, 4)
                    dve.scalar_tensor_tensor(raw[:, t, :], rot[:], 1.0, raw[:, t, :], ALU.add, ALU.mult
                                             ).then_inc(gate_ready, 1)

                for X in range(2):
                    queries(X)
                    keys_copied(X)
                    softmax(X)
                    pool_inputs(X)
                    if X == 1:
                        make_gate(0)
                    b = bb(f"OT{'ab'[X]}", g)
                    dve.scalar_tensor_tensor(mixed[:, 0:H, ds(NP_ + (2 * g + X) * NT, NT)],
                                             bank_wait(dve, b)[:, 0:NS].rearrange("p (h t) -> p h t", h=H), 0.5,
                                             gateS[:, :, ds((2 * g + X) * NT, NT)], ALU.mult, ALU.mult
                                             ).then_inc(bank_free[b.slot], 1)
                make_gate(1)
                dve.wait_ge(gate_ready, 2 * g + H + 2)
                for e in range(2):
                    for part, cols in (("p", slice(0, NP_)), ("s", slice(NP_, T))):
                        b = bb(f"m{e}{part}", g)
                        dve.scalar_tensor_tensor(mixed[:, ds(H + 2 * g + e, 1), cols].rearrange("p a t -> p (a t)"),
                                                 bank_wait(dve, b)[:, 0:cols.stop - cols.start],
                                                 halfscale[:, ds(2 * g + e, 1)], raw[:, e, cols],
                                                 ALU.mult, ALU.mult).then_inc(bank_free[b.slot], 1)
                own.leave(GROUPS)

            for k in range(KC):
                dve.wait_ge(mix_high, k + 1)
                dve.tensor_tensor(actL[:, k, :], mixed[:, k, :], actH[:, k, :].bitcast(F32), ALU.subtract
                                  ).then_inc(mix_low, 1)
            dve.wait_ge(y_in, 16 * (TT + 1))

            def residual(d, j, i):
                b = yb(f"yp{j}", i)
                at = y[:, 0:TT, ds(d * P, P)]
                dve.scalar_tensor_tensor(at, at, ALPHA, bank_wait(dve, b)[:].rearrange("p (t c) -> p t c", t=TT),
                                         ALU.mult, ALU.add).then_inc(bank_free[b.slot], 1)
                b = yb(f"ys{j}", i)
                at = y[0:NS, TT, ds(d * P, P)]
                dve.scalar_tensor_tensor(at, at, ALPHA, bank_wait(dve, b)[0:NS, 0:P], ALU.mult, ALU.add
                                         ).then_inc(bank_free[b.slot], 1)
                dve.wait_ge(bank_free[b.slot], b.read)

            with dve.Fori(0, KC // 2) as i:
                own.enter(i, 2 * (TT + 1))
                for j in range(2):
                    residual(2 * i + j, j, i)
                    for t in range(TT + 1):
                        m = P if t < TT else NS
                        own.step(dve.bn_stats(bn[0:m, t, ds(2 * i + j, 1), :].rearrange("p a s -> p (a s)"),
                                              y[0:m, t, ds((2 * i + j) * P, P)]))
                own.leave(KC // 2)
            own.wait()
            own.step(dve.memset(mv[:], 1.0))
            own.wait()
            for t in range(TT + 1):
                m = P if t < TT else NS
                own.step(dve.bn_aggr(mv[0:m, t, :], bn[0:m, t, :, :].rearrange("p a s -> p (a s)")))
            own.wait()
            dve.tensor_scalar(mv[:, :, 1], mv[:, :, 1], EPS, None, ALU.add).then_inc(var_ready, 1)
            dve.wait_ge(std_ready, 1)
            own.step(dve.reciprocal(stat[:, 0:5], std[:]))
            own.wait()
            dve.scalar_tensor_tensor(stat[:, 8:13], mv[:, :, 0], -1.0, stat[:, 0:5], ALU.mult, ALU.mult
                                     ).then_inc(var_ready, 1)
            dve.wait_ge(ln_in, 32)
            for t in (0, 2, 3, 4):
                m = P if t < TT else NS
                dve.wait_ge(norm_ready, t + 1)
                scaled = dve.tensor_tensor(y[0:m, t, :], y[0:m, t, :], gbc[0:m], ALU.mult)
                if t == 3:
                    scaled.then_inc(y_scaled, 1)
                    continue
                own.step(scaled)
                own.wait()
                dve.tensor_tensor(y[0:m, t, :], y[0:m, t, :], bbc[0:m], ALU.add).then_inc(y_ready[t], 1)


def rotation(dim, rotated, rows):
    import numpy as np
    half = rotated // 2
    pos = np.concatenate([np.arange(NP_), PAST + np.tile(np.arange(NT), NB)]).astype(np.float32)
    freqs = np.float32(500000.0) ** (-np.arange(half, dtype=np.float32) * np.float32(2.0 / rotated))
    ang = pos[None, :] * freqs.astype(np.float32)[:, None]
    table = np.zeros((rows, 2, T), np.float32)
    table[:, 0, :] = 1.0
    for start in range(0, rows, dim):
        for a in range(2):
            table[start + a * half:start + (a + 1) * half, 0, :] = np.cos(ang)
            table[start + a * half:start + (a + 1) * half, 1, :] = np.sin(ang) * (2 * a - 1)
    return table


def squares():
    import numpy as np
    out = np.zeros((P, 288), np.float32)
    out[:, 0:P] = np.eye(P)
    r = np.arange(P)
    out[:, P:2 * P] = np.where(r[None, :] <= r[:, None], 0.0, MASKED)
    n = np.arange(NS)
    seen = (n[None, :] // NT == n[:, None] // NT) & (n[None, :] % NT <= n[:, None] % NT)
    out[0:NS, 256:288] = np.where(seen, 0.0, MASKED)
    return out


def window_table():
    import numpy as np
    out = np.zeros((P, GROUPS * WT), np.float32)
    for g, w in enumerate(WINDOWS):
        row = [float(w > (1 << lv)) for lv in range(4)] + [1.0 / w] + [1.0 / min(t + 1, w) for t in range(HIST)]
        out[:, g * WT:(g + 1) * WT] = np.array(row, np.float32)
    return out


_INS = ["x_prompt", "x_sample", "cache_k", "cache_v", "cache_kidx", "state_pool", "page_table", "w_in", "w_pool",
        "pool_scale", "w_out", "ln_g", "ln_b"]
_OUTS = [("y_prompt", (1, NP_, D)), ("y_sample", (NB, NT, D)), ("p_k", (1, 1, NP_, H, P)), ("p_v", (1, 1, NP_, H, P)),
         ("p_kidx", (1, 1, NP_, ID)), ("p_pool", (1, 1, HIST, H * P)), ("s_k", (1, NB, NT, H, P)),
         ("s_v", (1, NB, NT, H, P)), ("s_kidx", (1, NB, NT, ID)), ("s_pool", (1, NB, HIST, H * P))]


def kernel(**inputs):
    import numpy as _np
    import concourse.bacc as _bacc
    from concourse.bass_utils import run_bass_kernel_spmd as _run

    nc = _bacc.Bacc("TRN2", target_bir_lowering=False, num_devices=1, dynamic_dma_scratch_size=1024)
    arrays = {f"in_{name}": _np.ascontiguousarray(inputs[name]) for name in _INS}
    arrays["const_square"] = squares()
    arrays["const_idx_rot"] = rotation(ID, 16, P)
    arrays["const_head_rot"] = rotation(P, 32, 32)
    arrays["const_windows"] = window_table()
    args = [nc.dram_tensor(name, a.shape, mybir.dt.from_np(a.dtype), kind="ExternalInput").ap()
            for name, a in arrays.items()]
    args += [nc.dram_tensor(f"out_{name}", shape, F32, kind="ExternalOutput").ap() for name, shape in _OUTS]
    layer_program(nc, *args)
    r = _run(nc, [arrays], core_ids=[0])
    return tuple(r.results[0][f"out_{name}"] for name, _ in _OUTS)
```
